# Optimizing a Trainium2 kernel written in Bass

```python
import math
import jax, jax.numpy as jnp
from jax import lax
import numpy as np

D_MODEL = 1024
BATCH = 1
SEQ = 512
DEPTH = 2

CHUNK = 64
N_A_LAYERS = DEPTH // 2
N_B_LAYERS = DEPTH - N_A_LAYERS

RET_HEADS = 8
RET_QK_DIM = D_MODEL // RET_HEADS
RET_V_DIM = 2 * RET_QK_DIM
RET_QK_WIDTH = RET_HEADS * RET_QK_DIM
RET_WIDTH = RET_HEADS * RET_V_DIM
RET_IN_WIDTH = 2 * RET_QK_WIDTH + 2 * RET_WIDTH

DIFF_HEADS = 8
DIFF_HEAD_DIM = D_MODEL // (2 * DIFF_HEADS)
DIFF_V_DIM = 2 * DIFF_HEAD_DIM
DIFF_QK_WIDTH = DIFF_HEADS * 2 * DIFF_HEAD_DIM
DIFF_WIDTH = DIFF_HEADS * DIFF_V_DIM
DIFF_IN_WIDTH = DIFF_QK_WIDTH + DIFF_WIDTH
KV_WIDTH = DIFF_QK_WIDTH + DIFF_WIDTH

ROPE_THETA = 10000.0
Q_BLOCK = 128
EPS = 1e-6


def rmsnorm(x, g):
    xf = x.astype(jnp.float32)
    y = xf * lax.rsqrt(jnp.mean(xf * xf, axis=-1, keepdims=True) + EPS)
    return (y * g.astype(jnp.float32)).astype(x.dtype)

def rope(x):
    s, dim = x.shape[1], x.shape[-1]
    half = dim // 2
    inv = ROPE_THETA ** (-jnp.arange(half, dtype=jnp.float32) / half)
    ang = jnp.arange(s, dtype=jnp.float32)[:, None] * inv[None, :]
    shape = (1, s) + (1,) * (x.ndim - 3) + (half,)
    cos = jnp.cos(ang).reshape(shape)
    sin = jnp.sin(ang).reshape(shape)
    xf = x.astype(jnp.float32)
    x1, x2 = xf[..., :half], xf[..., half:]
    return jnp.concatenate([x1 * cos - x2 * sin, x1 * sin + x2 * cos], axis=-1).astype(x.dtype)

def retention(q, k, v):
    b, s, h, dk = q.shape
    dv = v.shape[-1]
    n = s // CHUNK
    log_gamma = jnp.log1p(-jnp.exp2(-5.0 - jnp.arange(h, dtype=jnp.float32)))
    pos = jnp.arange(CHUNK, dtype=jnp.float32)
    diff = pos[:, None] - pos[None, :]
    decay_mask = jnp.where(diff[None] >= 0,
                           jnp.exp(jnp.maximum(diff, 0.0)[None] * log_gamma[:, None, None]),
                           0.0)
    q_decay = jnp.exp((pos[None, :] + 1.0) * log_gamma[:, None])[:, :, None]
    k_decay = jnp.exp((CHUNK - 1.0 - pos[None, :]) * log_gamma[:, None])[:, :, None]
    chunk_decay = jnp.exp(CHUNK * log_gamma)[None, :, None, None]

    def to_chunks(t):
        return t.astype(jnp.float32).reshape(b, n, CHUNK, h, t.shape[-1]).transpose(1, 0, 3, 2, 4)

    qc = to_chunks(q)
    kc = to_chunks(k) * (dk ** -0.5)
    vc = to_chunks(v)
    scores = jnp.einsum('nbhid,nbhjd->nbhij', qc, kc) * decay_mask[None, None]
    intra = jnp.einsum('nbhij,nbhje->nbhie', scores, vc)

    def step(state, inp):
        q_i, k_i, v_i = inp
        inter = jnp.einsum('bhcd,bhde->bhce', q_i * q_decay, state)
        state = state * chunk_decay + jnp.einsum('bhcd,bhce->bhde', k_i * k_decay, v_i)
        return state, inter

    state0 = jnp.zeros((b, h, dk, dv), jnp.float32)
    _, inter = lax.scan(step, state0, (qc, kc, vc))
    o = (intra + inter).transpose(1, 0, 3, 2, 4).reshape(b, s, h, dv)
    mu = jnp.mean(o, axis=-1, keepdims=True)
    var = jnp.mean(jnp.square(o - mu), axis=-1, keepdims=True)
    return (o - mu) * lax.rsqrt(var + EPS)

def diff_attention(q, k, v, lam):
    b, s, h, _, dh = q.shape
    dv = v.shape[-1]
    nblk = s // Q_BLOCK
    scale = dh ** -0.5
    qb = q.reshape(b, nblk, Q_BLOCK, h, 2, dh).transpose(1, 0, 2, 3, 4, 5)
    kf = k.astype(jnp.float32)
    vf = v.astype(jnp.float32)
    key_chunk = jnp.arange(s) // CHUNK
    neg = jnp.finfo(jnp.float32).min

    def block(args):
        q_i, i = args
        q_chunk = (i * Q_BLOCK + jnp.arange(Q_BLOCK)) // CHUNK
        mask = key_chunk[None, :] <= q_chunk[:, None]
        sc = jnp.einsum('bqhtd,bkhtd->bhtqk', q_i.astype(jnp.float32), kf) * scale
        p = jax.nn.softmax(jnp.where(mask, sc, neg), axis=-1)
        w = p[:, :, 0] - lam * p[:, :, 1]
        return jnp.einsum('bhqk,bkhe->bqhe', w, vf)

    out = lax.map(block, (qb, jnp.arange(nblk)))
    return out.transpose(1, 0, 2, 3, 4).reshape(b, s, h, dv)

def first_inputs(seed: int = 0) -> dict:
    key = jax.random.key(seed)
    ks = jax.random.split(key, 16)
    f32 = jnp.float32

    def nrm(k, shape, scale):
        return jax.random.normal(k, shape, f32) * scale

    return {
        "x": nrm(ks[0], (BATCH, SEQ, D_MODEL), 1.0),
        "pre_norm": 1.0 + nrm(ks[1], (DEPTH, D_MODEL), 0.02),
        "post_norm": 1.0 + nrm(ks[2], (DEPTH, D_MODEL), 0.02),
        "w_in_a": nrm(ks[3], (N_A_LAYERS, D_MODEL, RET_IN_WIDTH), D_MODEL ** -0.5),
        "w_out_a": nrm(ks[4], (N_A_LAYERS, RET_WIDTH, D_MODEL), RET_WIDTH ** -0.5),
        "kv_norm": 1.0 + nrm(ks[5], (D_MODEL,), 0.02),
        "w_kv": nrm(ks[6], (D_MODEL, KV_WIDTH), D_MODEL ** -0.5),
        "w_in_b": nrm(ks[7], (N_B_LAYERS, D_MODEL, DIFF_IN_WIDTH), D_MODEL ** -0.5),
        "lam_q1": nrm(ks[8], (N_B_LAYERS, DIFF_HEAD_DIM), 0.1),
        "lam_k1": nrm(ks[9], (N_B_LAYERS, DIFF_HEAD_DIM), 0.1),
        "lam_q2": nrm(ks[10], (N_B_LAYERS, DIFF_HEAD_DIM), 0.1),
        "lam_k2": nrm(ks[11], (N_B_LAYERS, DIFF_HEAD_DIM), 0.1),
        "sub_norm_b": 1.0 + nrm(ks[12], (N_B_LAYERS, DIFF_V_DIM), 0.02),
        "w_out_b": nrm(ks[13], (N_B_LAYERS, DIFF_WIDTH, D_MODEL), DIFF_WIDTH ** -0.5),
    }

def first_block(x, pre_norm, post_norm, w_in_a, w_out_a, kv_norm, w_kv, w_in_b,
              lam_q1, lam_k1, lam_q2, lam_k2, sub_norm_b, w_out_b):
    b, s, _ = x.shape
    k_shared = None
    v_shared = None
    for layer in range(DEPTH):
        h = rmsnorm(x, pre_norm[layer])
        if layer < N_A_LAYERS:
            proj = h @ w_in_a[layer]
            q = proj[..., :RET_QK_WIDTH].reshape(b, s, RET_HEADS, RET_QK_DIM)
            k = proj[..., RET_QK_WIDTH:2 * RET_QK_WIDTH].reshape(b, s, RET_HEADS, RET_QK_DIM)
            v = proj[..., 2 * RET_QK_WIDTH:2 * RET_QK_WIDTH + RET_WIDTH].reshape(b, s, RET_HEADS, RET_V_DIM)
            gate = proj[..., 2 * RET_QK_WIDTH + RET_WIDTH:]
            o = retention(rope(q), rope(k), v).reshape(b, s, RET_WIDTH)
            y = (o.astype(x.dtype) * jax.nn.silu(gate)) @ w_out_a[layer]
        else:
            j = layer - N_A_LAYERS
            if k_shared is None:
                kv = rmsnorm(x, kv_norm) @ w_kv
                k_shared = rope(kv[..., :DIFF_QK_WIDTH].reshape(b, s, DIFF_HEADS, 2, DIFF_HEAD_DIM))
                v_shared = kv[..., DIFF_QK_WIDTH:].reshape(b, s, DIFF_HEADS, DIFF_V_DIM)
            lambda_init = 0.8 - 0.6 * math.exp(-0.3 * layer)
            lam = (jnp.exp(jnp.sum(lam_q1[j].astype(jnp.float32) * lam_k1[j].astype(jnp.float32)))
                   - jnp.exp(jnp.sum(lam_q2[j].astype(jnp.float32) * lam_k2[j].astype(jnp.float32)))
                   + lambda_init)
            proj = h @ w_in_b[layer - N_A_LAYERS]
            q = rope(proj[..., :DIFF_QK_WIDTH].reshape(b, s, DIFF_HEADS, 2, DIFF_HEAD_DIM))
            gate = proj[..., DIFF_QK_WIDTH:]
            o = diff_attention(q, k_shared, v_shared, lam)
            o = rmsnorm(o, sub_norm_b[j]) * (1.0 - lambda_init)
            o = o.reshape(b, s, DIFF_WIDTH).astype(x.dtype)
            y = (o * jax.nn.silu(gate)) @ w_out_b[j]
        x = x + rmsnorm(y, post_norm[layer])
    return x


DEPTH_2 = 1

N_META = 16
D_FF = 2816
MLA_HEADS = 8
MLA_Q_RANK = 256
MLA_KV_RANK = 128
MLA_NOPE = 64
MLA_ROPE = 32
MLA_V = 64
GDN_HEADS = 8
GDN_DK = 64
GDN_DV = 64
CONV_K = 4
SPLITS = (MLA_Q_RANK, MLA_KV_RANK, MLA_ROPE,
          GDN_HEADS * GDN_DK, GDN_HEADS * GDN_DK, GDN_HEADS * GDN_DV,
          GDN_HEADS, GDN_HEADS, GDN_HEADS * GDN_DV,
          D_MODEL, D_MODEL)
D_IN = sum(SPLITS)
GDN_CONV_CH = 2 * GDN_HEADS * GDN_DK + GDN_HEADS * GDN_DV


def rmsnorm_2(x, w):
    x32 = x.astype(jnp.float32)
    y = x32 * lax.rsqrt(jnp.mean(x32 * x32, axis=-1, keepdims=True) + EPS)
    return (y * w.astype(jnp.float32)).astype(x.dtype)

def swiglu(x, w_gate, w_up, w_down):
    return (jax.nn.silu(x @ w_gate) * (x @ w_up)) @ w_down

def rope_tables(length):
    pos = jnp.arange(length, dtype=jnp.float32)
    inv = ROPE_THETA ** (-jnp.arange(0, MLA_ROPE, 2, dtype=jnp.float32) / MLA_ROPE)
    ang = pos[:, None] * inv[None, :]
    return jnp.cos(ang), jnp.sin(ang)

def apply_rope(x, cos, sin):
    half = x.shape[-1] // 2
    x1 = x[..., :half].astype(jnp.float32)
    x2 = x[..., half:].astype(jnp.float32)
    out = jnp.concatenate([x1 * cos - x2 * sin, x2 * cos + x1 * sin], axis=-1)
    return out.astype(x.dtype)

def mla(c_q_raw, c_kv_raw, k_rope_raw, q_norm, w_uq, kv_norm, w_ukv):
    b, length, _ = c_q_raw.shape
    q = (rmsnorm_2(c_q_raw, q_norm) @ w_uq).reshape(b, length, MLA_HEADS, MLA_NOPE + MLA_ROPE)
    kv = (rmsnorm_2(c_kv_raw, kv_norm) @ w_ukv).reshape(b, length, MLA_HEADS, MLA_NOPE + MLA_V)
    q_nope, q_rope = q[..., :MLA_NOPE], q[..., MLA_NOPE:]
    k_nope, v = kv[..., :MLA_NOPE], kv[..., MLA_NOPE:]
    cos, sin = rope_tables(length)
    q_rope = apply_rope(q_rope, cos[:, None, :], sin[:, None, :])
    k_rope = apply_rope(k_rope_raw, cos, sin)
    scale = (MLA_NOPE + MLA_ROPE) ** -0.5
    n_blk = -(-length // Q_BLOCK)
    l_pad = n_blk * Q_BLOCK

    def to_blocks(t):
        t = jnp.pad(t, ((0, 0), (0, l_pad - length), (0, 0), (0, 0)))
        return t.reshape(b, n_blk, Q_BLOCK, MLA_HEADS, t.shape[-1]).transpose(1, 0, 2, 3, 4)

    qn_blocks = to_blocks(q_nope)
    qr_blocks = to_blocks(q_rope)
    starts = jnp.arange(n_blk, dtype=jnp.int32) * Q_BLOCK
    k_pos = jnp.arange(length, dtype=jnp.int32)

    def attend_block(args):
        qn_b, qr_b, start = args
        s = (jnp.einsum('bqhd,bkhd->bhqk', qn_b, k_nope)
             + jnp.einsum('bqhd,bkd->bhqk', qr_b, k_rope)).astype(jnp.float32) * scale
        q_pos = start + jnp.arange(Q_BLOCK, dtype=jnp.int32)
        causal = k_pos[None, :] <= q_pos[:, None]
        s = jnp.where(causal, s, -jnp.inf)
        p = jax.nn.softmax(s, axis=-1).astype(v.dtype)
        return jnp.einsum('bhqk,bkhd->bqhd', p, v)

    o = lax.map(attend_block, (qn_blocks, qr_blocks, starts))
    o = o.transpose(1, 0, 2, 3, 4).reshape(b, l_pad, MLA_HEADS * MLA_V)
    return o[:, :length]

def short_conv(x, w):
    ch = x.shape[-1]
    return lax.conv_general_dilated(
        x, w[:, None, :].astype(x.dtype), window_strides=(1,),
        padding=[(CONV_K - 1, 0)], dimension_numbers=('NWC', 'WIO', 'NWC'),
        feature_group_count=ch)

def l2norm(x):
    return x * lax.rsqrt(jnp.sum(x * x, axis=-1, keepdims=True) + EPS)

def gated_deltanet(q_raw, k_raw, v_raw, b_raw, a_raw, z_raw, conv_w, a_log, dt_bias, gdn_norm):
    b, length, _ = q_raw.shape
    dtype = q_raw.dtype
    qkv = jax.nn.silu(short_conv(jnp.concatenate([q_raw, k_raw, v_raw], axis=-1), conv_w))
    nq = GDN_HEADS * GDN_DK
    q = qkv[..., :nq].reshape(b, length, GDN_HEADS, GDN_DK).astype(jnp.float32)
    k = qkv[..., nq:2 * nq].reshape(b, length, GDN_HEADS, GDN_DK).astype(jnp.float32)
    v = qkv[..., 2 * nq:].reshape(b, length, GDN_HEADS, GDN_DV).astype(jnp.float32)
    q = l2norm(q) * (GDN_DK ** -0.5)
    k = l2norm(k)
    beta = jax.nn.sigmoid(b_raw.astype(jnp.float32))
    g = -jnp.exp(a_log.astype(jnp.float32)) * jax.nn.softplus(
        a_raw.astype(jnp.float32) + dt_bias.astype(jnp.float32))

    pad_front = (-N_META) % CHUNK
    lc = pad_front + length
    n_chunk = lc // CHUNK

    def to_chunks(t):
        t = jnp.pad(t, ((0, 0), (pad_front, 0)) + ((0, 0),) * (t.ndim - 2))
        t = t.reshape((b, n_chunk, CHUNK) + t.shape[2:])
        return jnp.moveaxis(t, 3, 1)

    qc, kc, vc = to_chunks(q), to_chunks(k), to_chunks(v)
    bc = to_chunks(beta)
    gc = jnp.cumsum(to_chunks(g), axis=-1)
    tri_incl = jnp.tril(jnp.ones((CHUNK, CHUNK), dtype=bool))
    tri_strict = jnp.tril(jnp.ones((CHUNK, CHUNK), dtype=bool), -1)
    diff = gc[..., :, None] - gc[..., None, :]
    decay = jnp.exp(jnp.where(tri_incl, diff, -jnp.inf))
    kb = kc * bc[..., None]
    lmat = jnp.where(tri_strict, jnp.einsum('bhncd,bhnsd->bhncs', kb, kc) * decay, 0.0)
    eye = jnp.eye(CHUNK, dtype=jnp.float32)
    tmat = lax.linalg.triangular_solve(eye + lmat, jnp.broadcast_to(eye, lmat.shape),
                                       left_side=True, lower=True)
    u_c = tmat @ (vc * bc[..., None])
    w_c = tmat @ (kb * jnp.exp(gc)[..., None])
    intra = jnp.einsum('bhncd,bhnsd->bhncs', qc, kc) * decay

    def step(state, inp):
        q_i, k_i, u_i, w_i, g_i, a_i = inp
        v_new = u_i - w_i @ state
        o_i = (q_i * jnp.exp(g_i)[..., None]) @ state + a_i @ v_new
        g_last = g_i[..., -1]
        k_dec = k_i * jnp.exp(g_last[..., None] - g_i)[..., None]
        state = state * jnp.exp(g_last)[..., None, None] + jnp.einsum('bhcd,bhce->bhde', k_dec, v_new)
        return state, o_i

    xs = tuple(jnp.moveaxis(t, 2, 0) for t in (qc, kc, u_c, w_c, gc, intra))
    s0 = jnp.zeros((b, GDN_HEADS, GDN_DK, GDN_DV), jnp.float32)
    _, o = lax.scan(step, s0, xs)
    o = o.transpose(1, 0, 3, 2, 4).reshape(b, lc, GDN_HEADS, GDN_DV)[:, pad_front:]
    z = z_raw.reshape(b, length, GDN_HEADS, GDN_DV).astype(jnp.float32)
    o = rmsnorm_2(o, gdn_norm) * jax.nn.silu(z)
    return o.reshape(b, length, GDN_HEADS * GDN_DV).astype(dtype)

def _w(k, shape, fan_in):
    return jax.random.normal(k, shape, jnp.float32) * (fan_in ** -0.5)

def _gain(k, shape):
    return 1.0 + 0.02 * jax.random.normal(k, shape, jnp.float32)

def second_inputs(seed: int = 0) -> dict:
    key = jax.random.key(seed)
    ks = jax.random.split(key, 32)
    d = D_MODEL
    dt = jnp.exp(jax.random.uniform(ks[15], (DEPTH_2, GDN_HEADS), jnp.float32,
                                    minval=math.log(1e-3), maxval=math.log(1e-1)))
    return {
        'x': jax.random.normal(ks[0], (BATCH, SEQ, d), jnp.float32),
        'meta_tokens': jax.random.normal(ks[1], (N_META, d), jnp.float32),
        'ffn1_norm': _gain(ks[2], (DEPTH_2, d)),
        'ffn1_w_gate': _w(ks[3], (DEPTH_2, d, D_FF), d),
        'ffn1_w_up': _w(ks[4], (DEPTH_2, d, D_FF), d),
        'ffn1_w_down': _w(ks[5], (DEPTH_2, D_FF, d), D_FF),
        'mix_norm': _gain(ks[6], (DEPTH_2, d)),
        'w_in': _w(ks[7], (DEPTH_2, d, D_IN), d),
        'q_norm': _gain(ks[8], (DEPTH_2, MLA_Q_RANK)),
        'w_uq': _w(ks[9], (DEPTH_2, MLA_Q_RANK, MLA_HEADS * (MLA_NOPE + MLA_ROPE)), MLA_Q_RANK),
        'kv_norm': _gain(ks[10], (DEPTH_2, MLA_KV_RANK)),
        'w_ukv': _w(ks[11], (DEPTH_2, MLA_KV_RANK, MLA_HEADS * (MLA_NOPE + MLA_V)), MLA_KV_RANK),
        'w_mla_o': _w(ks[12], (DEPTH_2, MLA_HEADS * MLA_V, d), MLA_HEADS * MLA_V),
        'conv_w': _w(ks[13], (DEPTH_2, CONV_K, GDN_CONV_CH), CONV_K),
        'a_log': jnp.log(jax.random.uniform(ks[14], (DEPTH_2, GDN_HEADS), jnp.float32, minval=1.0, maxval=16.0)),
        'dt_bias': dt + jnp.log(-jnp.expm1(-dt)),
        'gdn_norm': _gain(ks[16], (DEPTH_2, GDN_DV)),
        'w_gdn_o': _w(ks[17], (DEPTH_2, GDN_HEADS * GDN_DV, d), GDN_HEADS * GDN_DV),
        'w_out': _w(ks[18], (DEPTH_2, d, d), d),
        'ffn2_norm': _gain(ks[19], (DEPTH_2, d)),
        'ffn2_w_gate': _w(ks[20], (DEPTH_2, d, D_FF), d),
        'ffn2_w_up': _w(ks[21], (DEPTH_2, d, D_FF), d),
        'ffn2_w_down': _w(ks[22], (DEPTH_2, D_FF, d), D_FF),
        'final_norm': _gain(ks[23], (d,)),
    }

def second_block(x, meta_tokens, ffn1_norm, ffn1_w_gate, ffn1_w_up, ffn1_w_down, mix_norm, w_in,
              q_norm, w_uq, kv_norm, w_ukv, w_mla_o, conv_w, a_log, dt_bias, gdn_norm, w_gdn_o,
              w_out, ffn2_norm, ffn2_w_gate, ffn2_w_up, ffn2_w_down, final_norm):
    b = x.shape[0]
    meta = jnp.broadcast_to(meta_tokens[None].astype(x.dtype), (b, N_META, D_MODEL))
    h = jnp.concatenate([meta, x], axis=1)
    split_points = [int(p) for p in np.cumsum(SPLITS)[:-1]]
    for l in range(DEPTH_2):
        h = h + 0.5 * swiglu(rmsnorm_2(h, ffn1_norm[l]), ffn1_w_gate[l], ffn1_w_up[l], ffn1_w_down[l])
        u = rmsnorm_2(h, mix_norm[l])
        (c_q, c_kv, k_rope, g_q, g_k, g_v, g_b, g_a, g_z,
         gate_mla, gate_gdn) = jnp.split(u @ w_in[l], split_points, axis=-1)
        y_mla = mla(c_q, c_kv, k_rope, q_norm[l], w_uq[l], kv_norm[l], w_ukv[l]) @ w_mla_o[l]
        y_gdn = gated_deltanet(g_q, g_k, g_v, g_b, g_a, g_z, conv_w[l], a_log[l], dt_bias[l],
                               gdn_norm[l]) @ w_gdn_o[l]
        merged = jax.nn.sigmoid(gate_mla) * y_mla + jax.nn.sigmoid(gate_gdn) * y_gdn
        h = h + merged @ w_out[l]
        h = h + 0.5 * swiglu(rmsnorm_2(h, ffn2_norm[l]), ffn2_w_gate[l], ffn2_w_up[l], ffn2_w_down[l])
    return rmsnorm_2(h, final_norm)[:, N_META:]


def setup_inputs(seed=0):
    out = dict(first_inputs(seed))
    for name, value in second_inputs(seed + 1).items():
        if name != "x":
            out[name + "_2"] = value
    return out


def reference(
    x, pre_norm, post_norm, w_in_a, w_out_a, kv_norm, w_kv, w_in_b, lam_q1, lam_k1, lam_q2,
    lam_k2, sub_norm_b, w_out_b, meta_tokens_2, ffn1_norm_2, ffn1_w_gate_2, ffn1_w_up_2,
    ffn1_w_down_2, mix_norm_2, w_in_2, q_norm_2, w_uq_2, kv_norm_2, w_ukv_2, w_mla_o_2,
    conv_w_2, a_log_2, dt_bias_2, gdn_norm_2, w_gdn_o_2, w_out_2, ffn2_norm_2, ffn2_w_gate_2,
    ffn2_w_up_2, ffn2_w_down_2, final_norm_2,
):
    x = first_block(
        x, pre_norm, post_norm, w_in_a, w_out_a, kv_norm, w_kv, w_in_b, lam_q1, lam_k1, lam_q2,
        lam_k2, sub_norm_b, w_out_b,
    )
    return second_block(
        x, meta_tokens_2, ffn1_norm_2, ffn1_w_gate_2, ffn1_w_up_2, ffn1_w_down_2, mix_norm_2,
        w_in_2, q_norm_2, w_uq_2, kv_norm_2, w_ukv_2, w_mla_o_2, conv_w_2, a_log_2, dt_bias_2,
        gdn_norm_2, w_gdn_o_2, w_out_2, ffn2_norm_2, ffn2_w_gate_2, ffn2_w_up_2, ffn2_w_down_2,
        final_norm_2,
    )


_drawn_inputs = setup_inputs


def setup_inputs(seed=0):
    import zlib

    import numpy as np

    out = dict(_drawn_inputs(seed))
    spreads = {}
    factors = {'kv_norm': 2.83,
     'lam_k1': 8.0,
     'lam_q2': 8.0,
     'sub_norm_b': 4.951,
     'ffn1_norm_2': 8.0,
     'mix_norm_2': 7.84,
     'q_norm_2': 8.0,
     'kv_norm_2': 23.967,
     'gdn_norm_2': 25.793,
     'ffn2_norm_2': 27.308,
     'final_norm_2': 8.171}
    for name, (base, spread) in spreads.items():
        noise = np.random.default_rng([zlib.crc32(name.encode()), seed]).standard_normal(out[name].shape)
        drawn = base * np.exp(spread * noise) if base else spread * noise
        out[name] = __import__('jax').numpy.asarray(drawn.astype(out[name].dtype))
    for name, factor in factors.items():
        out[name] = (out[name] * factor).astype(out[name].dtype)
    return out
```

```python
from contextlib import ExitStack

import numpy as np

import concourse.bass as bass
from concourse import mybir

F32 = mybir.dt.float32
F32R = mybir.dt.float32r
ALU = mybir.AluOpType
ACT = mybir.ActivationFunctionType
AX = mybir.AxisListType

P = 128
D = 1024
KC = D // P
SEQ = 512
META = 16
TOK = META + SEQ
HALF = TOK // 2
NT = SEQ // P
EPS = 1e-6
NEG = -float(2.0 ** 100)
HEADS = 8
RET_DK, RET_DV = 128, 256
DIFF_DH = 64
LAMBDA_INIT = 0.8 - 0.6 * float(np.exp(-0.3))
FFN = 2816
MLA_Q_RANK, MLA_KV_RANK = 256, 128
MLA_NOPE, MLA_ROPE, MLA_V = 64, 32, 64
GDN_D = 64
GDN_WIDTH = HEADS * GDN_D
CONV = 4
FFN_PARTS = (12, 10)

UCOL = 256
UNIT = KC * UCOL
RAWS = 4
SPLITS = 2
SLOTS = 4


def rope_tables(half, reps, positions):
    inv = (np.float32(10000.0) ** (-np.arange(half, dtype=np.float32) / np.float32(half))).astype(np.float32)
    ang = (np.arange(positions, dtype=np.float32)[:, None] * inv[None, :]).astype(np.float32)
    cos = np.cos(ang.astype(np.float64)).T
    sin = np.sin(ang.astype(np.float64)).T
    c = np.concatenate([cos, cos] * reps, axis=0)
    s = np.concatenate([-sin, sin] * reps, axis=0)
    return np.ascontiguousarray(np.stack([c, s], axis=1)).astype(np.float32)


def retention_decay():
    j = np.arange(P)[:, None]
    c = np.arange(SEQ)[None, :]
    out = np.zeros((HEADS, P, SEQ), np.float64)
    for h in range(HEADS):
        out[h] = np.where(c >= j, np.exp(np.log1p(-2.0 ** (-5.0 - h)) * (c - j)), 0.0) * RET_DK ** -0.5
    return out.astype(np.float32)


def chunk_masks():
    r, c = np.arange(P)[:, None], np.arange(P)[None, :]
    same = r // 64 == c // 64
    masks = [same & (r <= c), same & (r > c)]
    for s in (1, 2, 4, 8, 16, 32):
        masks.append((r // (2 * s) == c // (2 * s)) & (r // s % 2 == 1) & (c // s % 2 == 0))
    return np.ascontiguousarray(np.stack(masks, axis=1)).astype(np.float32)


class Job:

    def __init__(self, units, at, fold=1, loop=True, chunks=None):
        self.units, self.fold = units, fold
        self.unit0, self.chunk0, self.tick0 = at
        self.turns = units // 4 if loop and units >= 8 else 0
        self.end = (self.unit0 + units, self.chunk0 + (chunks or 2 * units // fold), self.tick0 + (chunks or 2 * units))


def build(nc, A, out):
    ctx = ExitStack()
    with ctx:
        def sem(name):
            return ctx.enter_context(nc.semaphore(name))

        FIRST, LAST = 16512, 229344
        ends, starts = {None: FIRST}, {}

        def place(name, shape, after, dt=F32, over=None):
            size = (int(np.prod(shape[1:])) * 4 + 31) // 32 * 32
            at = ends[after] if over is None else starts[over]
            assert at + size <= LAST, (name, at + size - LAST)
            starts[name], ends[name] = at, at + size
            return nc.alloc_sbuf_tensor_at(name, list(shape), dt, offset=at)

        RES = place("residual", [P, KC, TOK], None)
        UH = place("u_hi", [P, KC, TOK], "residual", F32R)
        UL = place("u_lo", [P, KC, TOK], "u_hi", F32R)
        RAW = place("w_raw", [P, RAWS, UNIT], "u_lo")
        WH = place("w_hi", [P, SPLITS, UNIT], "w_raw", F32R)
        WL = place("w_lo", [P, SPLITS, UNIT], "w_hi", F32R)
        IDENT = place("ident", [P, P], "w_lo")
        ONES = place("ones", [P, P], "ident")
        SUMSQ = place("sumsq", [P, TOK], "ones")
        SQ = place("sq", [P, 2, TOK], "sumsq")
        TMP = place("tmp", [P, 2, TOK], "sq")
        SG = place("sg", [P, 2, TOK], "tmp")
        DIAG = place("diag", [P, TOK], None, over="sg")
        GAINS = place("gains", [P, P], "sg")
        GROW = place("gain_rows", [P, P], None, over="tmp")
        STAT = place("stat", [P, 3, 8], "gains")
        BN6 = place("bn6", [P, NT, 6], "stat")
        BNA = place("bn_mv", [P, NT, 2], "bn6")
        VEPS = place("var_eps", [P, 8], "bn_mv")
        RSTD = place("rstd", [P, 8], "var_eps")
        MHALF = place("minus_half", [P, 8], "rstd")
        LAMS = place("lam_cols", [P, 8], "minus_half")
        LAMV = place("lam_vectors", [1, 4, 64], "lam_cols")
        NEGM2 = place("neg_max2", [P, 8], "lam_vectors")
        ESUM2 = place("exp_sum2", [P, 4, NT], "neg_max2")
        RSUM2 = place("inv_sum2", [P, 4, NT], "exp_sum2")
        ROWS = place("mask_rows", [1, 256], "inv_sum2")
        arena = "mask_rows"

        QK = place("ret_qk", [P, 2 * HEADS, SEQ], arena)
        V = place("ret_v", [P, NT, HEADS * RET_DV], "ret_qk")
        SC = place("ret_scores", [P, 2, 1280], "ret_v")
        TAB = place("ret_rope", [P, 2, SEQ], None, over="ret_scores")
        DECAY = place("ret_decay", [P, 2, SEQ], None, over="tmp")
        ON = place("ret_norm", [P, NT, RET_DV], None, over="sq")
        X0 = place("x_rows", [P, NT, D], None, over="ret_v")
        M0 = place("meta_rows", [META, D], "x_rows")
        YL = place("ret_y_lo", [P, 2 * HEADS, SEQ], None, F32R, over="ret_qk")
        YH = place("ret_y_hi", [P, 2 * HEADS, SEQ], None, F32R, over="ret_v")
        Y2 = place("proj_out", [P, KC, SEQ], None, over="u_hi")

        DQK = place("diff_qk", [P, 2 * HEADS, SEQ], arena)
        DYL = place("diff_y_lo", [P, HEADS, SEQ], None, F32R, over="diff_qk")
        DYH = place("diff_y_hi", [P, HEADS, SEQ], "diff_y_lo", F32R)
        DV = place("diff_v", [P, NT, D], "diff_qk")
        RB = place("inv_rms", [P, SEQ], "diff_v")
        DTAB = place("diff_rope", [P, 2, SEQ], "inv_rms")
        DE = place("diff_exp", [P, 2, 2, SEQ], "diff_rope")
        DW = place("diff_w", [P, 2, SEQ], "diff_exp")
        DWT = place("diff_wt", [P, 2, SEQ], "diff_w")
        DON = place("diff_norm", [P, 2, NT, P], "diff_wt")
        NEGM = place("neg_max", [P, 2, 2], "diff_norm")
        ESUM = place("exp_sum", [P, 2, 2], "neg_max")
        RSUM = place("inv_sum", [P, 2, NT, 2], "exp_sum")
        COEF = place("coef", [P, 2], "inv_sum")
        SSQ = place("ssq", [P, NT], "coef")
        DSQ = place("diff_sq", [P, NT, P], None, over="sq")

        HH = place("hidden_hi", [P, FFN_PARTS[0], TOK], arena, F32R)
        HL = place("hidden_lo", [P, FFN_PARTS[0], TOK], "hidden_hi", F32R)

        MISC = place("mix_misc", [P, TOK], arena)
        OMF = place("mla_out", [P, 4, SEQ], "mix_misc")
        MPT = place("mla_pt", [P, 2, 640], "mla_out")
        ME = place("mla_exp", [P, 2, TOK], "mla_pt")
        MON = place("mla_norm", [P, 2, NT, P], "mla_exp")
        CQF = place("cq", [P, 2, SEQ], "mix_misc")
        CQH = place("cq_hi", [P, 2, SEQ], "cq", F32R)
        CQL = place("cq_lo", [P, 2, SEQ], "cq_hi", F32R)
        CKF = place("ckv", [P, 1, TOK], "cq_lo")
        CKH = place("ckv_hi", [P, 1, TOK], "ckv", F32R)
        CKL = place("ckv_lo", [P, 1, TOK], "ckv_hi", F32R)
        MTAB = place("mla_rope", [P, 2, TOK], "ckv_lo")
        assert ends["mla_norm"] <= ends["mla_rope"]
        QC = place("mla_q", [P, HEADS, SEQ], "mla_rope")
        KCAT = place("mla_k", [P, HEADS, TOK], "mla_q")
        MV = place("mla_v", [P, NT + 1, SEQ], "mla_k")
        CMASK = place("causal", [P, P], "mla_v")

        CVS = place("gdn_conv", [P, 12, TOK], "mla_out")
        ZS = place("gdn_gate", [P, 4, SEQ], "gdn_conv")
        ROWQ = place("gdn_rows", [P, 3, GDN_WIDTH], "gdn_gate")
        NQ = place("gdn_nq", [P, GDN_WIDTH], "gdn_rows")
        NK = place("gdn_nk", [P, GDN_WIDTH], "gdn_nq")
        KT = place("gdn_kt", [P, 4, P], "gdn_nk")
        QT = place("gdn_qt", [P, 4, P], "gdn_kt")
        KBT = place("gdn_kbt", [P, 4, P], "gdn_qt")
        KB = place("gdn_kb", [P, GDN_WIDTH], "gdn_kbt")
        QGT = place("gdn_qgt", [P, 4, P], "gdn_kb")
        KBG = place("gdn_kbg", [P, GDN_WIDTH], "gdn_qgt")
        KD = place("gdn_kd", [P, GDN_WIDTH], "gdn_kbg")
        QG = place("gdn_qg", [P, GDN_WIDTH], "gdn_kd")
        DEC = place("gdn_dec", [P, HEADS, P], "gdn_qg")
        SMALL = place("gdn_small", [P, 640], "gdn_dec")
        PRE = place("gdn_pre", [P, 2, TOK + 8], None, over="gdn_kt")
        GSQ = place("gdn_sq", [P, 2, GDN_WIDTH], None, over="gdn_dec")
        GON = place("gdn_on", [P, GDN_WIDTH], None, over="gdn_dec")
        TI = place("gdn_inv", [P, HEADS, P], None, over="gdn_kt")
        TIT = place("gdn_inv_t", [P, HEADS, P], None, over="gdn_kbt")
        XX = place("gdn_x", [P, HEADS, P], None, over="gdn_rows")
        UU = place("gdn_u", [P, GDN_WIDTH], None, over="gdn_nq")
        VN = place("gdn_vn", [P, GDN_WIDTH], None, over="gdn_nk")
        WTT = place("gdn_wt", [P, 4, P], None, over="gdn_qg")
        LT = place("gdn_lt", [P, HEADS, P], None, over="tmp")
        AT = place("gdn_at", [P, HEADS, P], "gdn_lt")
        assert ends["gdn_at"] <= ends["sg"]
        UG = place("gdn_ug", [P, HEADS, P], None, over="gdn_lt")
        TRI = place("gdn_tri", [P, HEADS, P], None, over="sumsq")
        SS = place("gdn_ss", [P, 4, GDN_D], "gdn_tri")
        assert ends["gdn_ss"] <= ends["sq"]
        ST = place("gdn_state", [P, 2, 4, GDN_D], None, over="mix_misc")

        OML = place("mla_out_lo", [P, 4, SEQ], None, F32R, over="mla_out")
        MH = place("merged_hi", [P, KC, SEQ], None, F32R, over="gdn_conv")
        OMH = place("mla_out_hi", [P, 4, SEQ], "merged_hi", F32R)
        assert ends["mla_out_hi"] <= ends["gdn_conv"]
        GOL = place("gdn_out_lo", [P, 4, SEQ], None, F32R, over="gdn_gate")
        ML = place("merged_lo", [P, KC, SEQ], "gdn_gate", F32R)
        GOH = place("gdn_out_hi", [P, 4, SEQ], "merged_lo", F32R)
        GATE = place("branch_gates", [P, 2, 2, SEQ], "gdn_out_hi")

        FN = place("final_normed", [P, KC, SEQ], arena)
        OUTR = place("out_rows", [P, NT, D], "final_normed")

        PS = ctx.enter_context(nc.psum_tensor("ps", [P, 8, 512], F32))

        s_ident, s_ones, s_x, s_meta, s_gain, s_tab = [
            sem(n) for n in ("ident_in", "ones_set", "x_in", "meta_in", "gain_in", "rope_in")]
        raw_in = [sem(f"raw_in{i}") for i in range(RAWS)]
        hi_done, lo_done = sem("w_hi_done"), sem("w_lo_done")
        done = sem("pe_done")
        ps_free = [sem(f"ps_free{i}") for i in range(SLOTS)]
        sq_done, sq_added = sem("sq_done"), sem("sq_added")
        ms_done, inv_done, root_done, diag_done = [
            sem(n) for n in ("mean_square", "inverse_ms", "root_done", "diag_done")]
        sum_zeroed = sem("sum_zeroed")
        t_done, uh_done, ul_done = sem("scaled_done"), sem("u_hi_done"), sem("u_lo_done")
        post_t, res_done = sem("post_scaled"), sem("residual_done")
        shift_done, sin_done, rope_done = sem("shift_done"), sem("sin_done"), sem("rope_done")
        dec_in = [sem(f"decay_in{i}") for i in range(2)]
        ra_s, ra_m, ra_pv, ra_bn, ra_ve, ra_rs, ra_on, ra_t, ra_e = [sem(n) for n in (
            "ret_scored", "ret_masked", "ret_pv", "ret_stats", "ret_vareps", "ret_rstd", "ret_normed",
            "ret_turned", "ret_out")]
        y_done, yh_done, yl_done = sem("y_done"), sem("y_hi_done"), sem("y_lo_done")
        s_half, s_rows, s_lamv, lam_step, lam_exp = [
            sem(n) for n in ("half_set", "rows_set", "lam_in", "lam_step", "lam_exp")]
        s_dtab, rb_done = sem("diff_rope_in"), sem("inv_rms_kept")
        da_s, da_max, da_e, da_c, da_w, da_t, da_wt, da_pv, da_sq, da_ve, da_rs, da_on = [sem(n) for n in (
            "diff_scored", "diff_max", "diff_exp_done", "diff_coef", "diff_w_done", "diff_w_turned", "diff_wt_out",
            "diff_pv", "diff_sq_done", "diff_vareps", "diff_rstd", "diff_normed")]
        s_mtab, kr_done, s_cmask = sem("mla_rope_in"), sem("key_rope"), sem("causal_in")
        qr_done = sem("query_rope")
        ma_s, ma_max, ma_e, ma_t, ma_pt, ma_pv, ma_rs, ma_on = [sem(n) for n in (
            "mla_scored", "mla_max", "mla_exp_done", "mla_turned", "mla_turned_out", "mla_pv", "mla_inv_sum",
            "mla_normed")]
        s_tri, s_al, z_done = sem("tri_in"), sem("gdn_vectors_in"), sem("gdn_gate_done")
        pre_zero, pre_in, tap_done, conv_done = [sem(n) for n in ("pre_zeroed", "pre_in", "tap_done", "conv_done")]
        sp_done = sem("softplus_done")
        gexp_done = sem("gdn_exp_done")
        ba_zero = sem("ba_zeroed")
        g_pe, g_act, g_dve, g_pool = [sem(f"gdn_{n}") for n in ("pe", "act", "dve", "pool")]
        oh_done, ol_done, gh_done, gl_done = [sem(n) for n in (
            "mla_hi_done", "mla_lo_done", "gdn_hi_done", "gdn_lo_done")]
        merged_done, mh_done, ml_done, f_done, kept_done = [sem(n) for n in (
            "merged", "merged_hi_done", "merged_lo_done", "final_scaled", "rows_kept")]
        hh_done, hl_done = sem("hidden_hi_done"), sem("hidden_lo_done")
        s_out = sem("out_stored")

        c_ident = nc.inline_tensor(np.eye(P, dtype=np.float32), "c_ident").ap()
        c_rope_ret = nc.inline_tensor(rope_tables(RET_DK // 2, 1, SEQ), "c_rope_ret").ap()
        c_rope_diff = nc.inline_tensor(rope_tables(DIFF_DH // 2, 2, SEQ), "c_rope_diff").ap()
        c_rope_mla = nc.inline_tensor(rope_tables(MLA_ROPE // 2, 4, TOK), "c_rope_mla").ap()
        c_causal = nc.inline_tensor(np.where(np.arange(P)[None, :] > np.arange(P)[:, None], np.float32(NEG),
                                             np.float32(0.0)).astype(np.float32), "c_causal").ap()
        c_tri = nc.inline_tensor(chunk_masks(), "c_tri").ap()
        c_decay = nc.inline_tensor(retention_decay(), "c_decay").ap()

        at = [0, 0, 0]

        def job(units, **kw):
            j = Job(units, tuple(at), **kw)
            at[:] = j.end
            return j

        def chunks(n):
            c = tuple(at)
            at[1] += n
            at[2] += n
            return c

        at_x = chunks(9)
        at_norm0 = chunks(2)
        at_lam = chunks(1)
        j_ret_qk, j_ret_v, j_ret_gate = job(8), job(8), job(8)
        j_ret_out = job(8, fold=2)
        at_post0 = chunks(2)
        at_norm1 = chunks(2)
        j_kv_k, j_kv_v, j_diff_q, j_diff_gate, j_diff_out = job(4), job(4), job(4), job(4), job(4)
        at_post1 = chunks(2)
        ffns = {}

        def ffn_jobs(name, last):
            ffns[name] = []
            for n, part in enumerate(FFN_PARTS):
                ffns[name].append((job(part), job(8, fold=2, loop=not (last and n))))

        at_ffn1 = chunks(2)
        ffn_jobs("ffn1", False)
        at_mix = chunks(2)
        j_cq, j_kvm = job(1), job(1)
        at_cq, at_ckv = chunks(2), chunks(2)
        j_uq, j_ukv = job(1, chunks=8), job(1, chunks=9)
        j_gqkv, j_z = job(6, loop=False), job(2)
        j_merge = job(12, loop=False, chunks=32)
        j_wout = job(4)
        at_ffn2 = chunks(2)
        ffn_jobs("ffn2", True)
        at_final = chunks(2)
        at_rows = chunks(NT)
        n_units = at[0]

        w_in_a = A["w_in_a"][0].rearrange("(c p) n -> p c n", p=P)
        w_out_a = A["w_out_a"][0].rearrange("(c p) n -> p c n", p=P)
        w_kv = A["w_kv"].rearrange("(c p) n -> p c n", p=P)
        w_in_b = A["w_in_b"][0].rearrange("(c p) n -> p c n", p=P)
        w_out_b = A["w_out_b"][0].rearrange("(c p) n -> p c n", p=P)
        w_in = A["w_in_2"][0].rearrange("(c p) n -> p c n", p=P)
        w_uq = A["w_uq_2"][0].rearrange("(c p) (h n) -> p c h n", p=P, h=HEADS)
        w_ukv = A["w_ukv_2"][0].rearrange("p (h n) -> p h n", h=HEADS)
        w_mla_o = A["w_mla_o_2"][0].rearrange("(c p) n -> p c n", p=P)
        w_gdn_o = A["w_gdn_o_2"][0].rearrange("(c p) n -> p c n", p=P)
        w_out2 = A["w_out_2"][0].rearrange("(c p) n -> p c n", p=P)
        w_ffn = {f"ffn{n}": [A[f"ffn{n}_w_{k}_2"][0].rearrange("(c p) n -> p c n", p=P) for k in ("gate", "up", "down")]
                 for n in (1, 2)}

        def each(eng, jb, body, peel=0):
            for u in range(4 * peel if jb.turns else 0):
                body(u // 4, u % 4)
            if jb.turns > peel:
                with eng.Fori(peel, jb.turns) as i:
                    for j in range(4):
                        body(i, j)
            for u in range(4 * jb.turns, jb.units):
                body(u // 4, u % 4)

        def wait(eng, semaphore, value):
            if not isinstance(value, int) or value > 0:
                eng.wait_ge(semaphore, value)

        def chunk_of(jb, i, j, m):
            c = jb.chunk0 + 2 * (j // jb.fold) + m
            return c % SLOTS, c // SLOTS + 2 // jb.fold * i

        def tick_of(jb, i, j, m):
            return jb.tick0 + 8 * i + 2 * j + m + 1

        def slot_free(eng, slot, uses):
            if not isinstance(uses, int) or uses:
                eng.wait_ge(ps_free[slot], uses)

        def acc(slot, width):
            return PS[:, 2 * slot, 0:width] if width <= 512 else PS[:, 2 * slot:2 * slot + 2, 0:width // 2]

        def halves(ap):
            return ap.rearrange("p (a n) -> p a n", a=2) if ap.shape[-1] > 512 else ap

        def token_tiles(width):
            return (4, 128) if width == SEQ else (6, 88)

        SEQ_COLS, ALL_COLS, PLAIN = slice(META, TOK), slice(0, TOK), slice(0, SEQ)

        norms = {}

        def norm(name, at_norm, cols, squares=KC, features=D):
            before = sum(x[4] for x in norms.values())
            norms[name] = (len(norms), at_norm, cols, before, squares, features)

        norm("norm0", at_norm0, SEQ_COLS)
        norm("post0", at_post0, SEQ_COLS)
        applied = {"norm0": 0, "norm1": 8, "norm1q": 16, "ffn1": 24, "mix": 32, "cq": 40, "ckv": 42, "ffn2": 43,
                   "final": 51}
        norm("norm1", at_norm1, SEQ_COLS)
        norm("post1", at_post1, SEQ_COLS)
        norm("ffn1", at_ffn1, ALL_COLS)
        norm("mix", at_mix, ALL_COLS)
        norm("cq", at_cq, PLAIN, 2, MLA_Q_RANK)
        norm("ckv", at_ckv, ALL_COLS, 2, MLA_KV_RANK)
        norm("ffn2", at_ffn2, SEQ_COLS)
        norm("final", at_final, SEQ_COLS)

        norms["norm1q"] = norms.get("norm1")

        several = {j_kvm.unit0: 3, j_uq.unit0: 7, j_ukv.unit0: 1}
        several.update({j_merge.unit0 + 3 * n + 2: 1 for n in range(4)})

        def extra_loads(u):
            return sum(n for v, n in several.items() if v <= u and v % RAWS == u % RAWS)

        def uses_before(chunk):
            return [len([c for c in range(chunk) if c % SLOTS == s]) for s in range(SLOTS)]

        MLA_LAG = 2 * NT + 4
        mla_turns = []
        for s in range(HEADS * NT + MLA_LAG):
            if 1 <= s <= HEADS * NT:
                mla_turns.append(("item", s - 1))
            if s >= MLA_LAG and (s - MLA_LAG) % (2 * NT) == 0 and (s - MLA_LAG) // (2 * NT) < HEADS // 2:
                mla_turns.append(("pair", (s - MLA_LAG) // (2 * NT)))
        mla_turn_no = {what: n for n, what in enumerate(mla_turns)}

        def mla_step_turns(s):
            found = [("item", s - 1)] if ("item", s - 1) in mla_turn_no else []
            if s >= MLA_LAG and (s - MLA_LAG) % (2 * NT) == 0 and ("pair", (s - MLA_LAG) // (2 * NT)) in mla_turn_no:
                found.append(("pair", (s - MLA_LAG) // (2 * NT)))
            return found

        def levels(t):
            return [1, 2, 4, 8] if t == 0 else [1, 2, 4, 8, 16, 32]

        pe_steps, act_steps, dve_steps, pool_steps = [], [], [], []
        for t in range(NT + 1):
            full = t > 0
            lev = [(kind, n, g) for n in levels(t) for kind in ("x", "y") for g in range(2)]
            pe_steps += [(t, n) for n in ["turn_in", "decay", "turn_scaled", "kk"] + ["kq"] * full + lev + ["uw"]]
            pe_steps += [(t, (n, c)) for c in range(1 + full) for n in ["ws"] * full + ["state"] + ["out"] * full]
            pe_steps += [(t, "turn_out")] * full
            act_steps += [(t, n) for n in ["square", "rows", "decay", "turned", "uw"] + ["out_square"] * full]
            pool_steps += [(t, n) for n in ["ug", "rnorm", "kbg", "kd", "vb", "eye"] + ["at"] * full + ["out_rnorm"] * full]
            dve_steps += [(t, n) for n in ["ssum", "seps", "f_kb", "f_kd", "f_kbg"] + ["f_q", "f_qg"] * full + ["kb", "nk"]
                          + ["nq", "qg"] * full + ["lt"] + ["at"] * full]
            dve_steps += [(t, n) for s in levels(t) for n in [("x", s, 0), ("x", s, 1)]
                          + [(kind, s, g) for g in range(2) for kind in ["d"] * (s != levels(t)[-1]) + ["e"]]]
            dve_steps += [(t, (n, c)) for c in range(1 + full) for n in ["vn", "sd"] * full + ["s"]]
            dve_steps += [(t, n) for n in [("out_inter", 0), ("out_inter", 1), "out_join", "out_sum", "out_eps", "out_norm", "out_gate"] * full]
        N_PRE_PE, N_PRE_ACT, N_PRE_DVE = 2, 5, 7
        PE_AT = {key: n + 1 + N_PRE_PE for n, key in enumerate(pe_steps)}
        ACT_AT = {key: n + 1 + N_PRE_ACT for n, key in enumerate(act_steps)}
        DVE_AT = {key: n + 1 + N_PRE_DVE for n, key in enumerate(dve_steps)}
        POOL_AT = {key: n + 1 for n, key in enumerate(pool_steps)}
        progress = {"pe": list(pe_steps), "act": list(act_steps), "dve": list(dve_steps), "pool": list(pool_steps)}

        def one(eng, t, name):
            assert progress[eng].pop(0) == (t, name), (eng, t, name)
            return 1

        def tile(t):
            return (META, slice(0, META)) if t == 0 else (P, slice(META + P * (t - 1), META + P * t))

        BA = SMALL[:, 0:80].rearrange("p (t n) -> p t n", t=NT + 1)
        BETA = SMALL[:, 80:120].rearrange("p (t n) -> p t n", t=NT + 1)
        GG = SMALL[:, 120:160].rearrange("p (t n) -> p t n", t=NT + 1)
        GEXP = SMALL[:, 160:272]
        XA = SMALL[:, 272:312].rearrange("p (t n) -> p t n", t=NT + 1)
        RELU = SMALL[:, 312:352].rearrange("p (t n) -> p t n", t=NT + 1)
        EN = SMALL[:, 352:392].rearrange("p (t n) -> p t n", t=NT + 1)
        EAL = SMALL[:, 392:400]
        ALROW = SMALL[0:1, 400:416]
        SSV, RN = SMALL[:, 416:432], SMALL[:, 432:448]
        FAC = SMALL[:, 448:496].rearrange("p (f n) -> p f n", f=6)
        LNE = SMALL[:, 496:536].rearrange("p (t n) -> p t n", t=NT + 1)
        OSS, ORN = SMALL[:, 536:544], SMALL[:, 544:552]

        def exp_gc(t):
            return GEXP[0:META, 96:104] if t == 0 else GEXP[:, 8 * (t - 1):8 * t]

        def exp_rest(t):
            return GEXP[0:META, 104:112] if t == 0 else GEXP[:, 32 + 8 * (t - 1):32 + 8 * t]

        def over_heads(ap, w, n):
            return ap.unsqueeze(2).to_broadcast([w, HEADS, n])

        def by_head(ap):
            return ap.rearrange("p (h n) -> p h n", h=HEADS)

        def every_other(ap, which):
            return ap.rearrange("p (h a) c -> p h a c", a=2)[:, :, which, :]

        def joined(ap, size, which):
            if len(ap.shape) == 2:
                return ap.rearrange("p (b a s) -> p b a s", a=2, s=size)[:, :, which, :]
            return ap.rearrange("p h (b a s) -> p h b a s", a=2, s=size)[:, :, :, which, :]

        ITEMS, HEAD_LAG = HEADS * NT, 9
        turns = []
        for s in range(ITEMS + HEAD_LAG):
            if 1 <= s <= ITEMS:
                turns.append(("item", s - 1))
            if s >= HEAD_LAG and (s - HEAD_LAG) % NT == 0 and (s - HEAD_LAG) // NT < HEADS:
                turns.append(("head", (s - HEAD_LAG) // NT))
        turn_no = {what: n for n, what in enumerate(turns)}

        def width_of(cols):
            return cols.stop - cols.start

        block = ctx.enter_context(nc.Block())

        @block.sync
        def _(sp):
            sp.dma_start(IDENT[:, :], c_ident).then_inc(s_ident, 16)
            sp.dma_start(X0[:, :, :], A["x"][0].rearrange("(t p) n -> p t n", p=P)).then_inc(s_x, 16)
            sp.dma_start(M0[:, :], A["meta_tokens_2"]).then_inc(s_meta, 16)
            for g, (name, row) in enumerate(GAIN_ROWS):
                src = A[name] if row is None else A[name][row]
                sp.dma_start(GROW[g * KC:(g + 1) * KC, :], src.rearrange("(c p) -> c p", p=P)).then_inc(s_gain, 16)
            for row, src in other_rows(A):
                sp.dma_start(GROW[row:row + src.shape[0], 0:src.shape[1]], src).then_inc(s_gain, 16)
            gdn_gain = A["gdn_norm_2"]
            sp.dma_start(GROW[GDN_ROW:GDN_ROW + 1, 64:128], gdn_gain).then_inc(s_gain, 16)
            sp.dma_start(TAB[:, :, :], c_rope_ret).then_inc(s_tab, 16)
            for n, name in enumerate(("lam_q1", "lam_q2", "lam_k1", "lam_k2")):
                sp.dma_start(LAMV[:, n, :], A[name]).then_inc(s_lamv, 16)

            def load(jb, src):
                def body(i, j):
                    u = jb.unit0 + j
                    need = u - RAWS + 1 + 4 * i
                    if not isinstance(need, int) or need > 0:
                        sp.wait_ge(lo_done, need)
                    src(i, j, RAW[:, u % RAWS, :], raw_in[u % RAWS])
                if jb.unit0:
                    each(sp, jb, body)
                else:
                    for u in range(jb.units):
                        body(u // 4, u % 4)

            def cols(w, first):
                def f(i, j, dst, s):
                    sp.dma_start(dst.rearrange("p (c n) -> p c n", c=KC),
                                 w[:, :, bass.ds(4 * UCOL * i + (first + j * UCOL), UCOL)]).then_inc(s, 16)
                return f

            def folded(w, first, kc):
                def f(i, j, dst, s):
                    a = first + (j % 2) * kc
                    sp.dma_start(dst[:, 0:kc * UCOL].rearrange("p (c n) -> p c n", c=kc),
                                 w[:, a:a + kc, bass.ds(2 * UCOL * i + (j // 2) * UCOL, UCOL)]).then_inc(s, 16)
                return f

            load(j_ret_qk, cols(w_in_a, 0))
            load(j_ret_v, cols(w_in_a, 2 * HEADS * RET_DK))
            load(j_ret_gate, cols(w_in_a, 2 * HEADS * RET_DK + HEADS * RET_DV))
            load(j_ret_out, folded(w_out_a, 0, KC))
            sp.wait_ge(done, j_ret_gate.end[2])
            sp.wait_ge(yl_done, 2 * HEADS)
            sp.wait_ge(done, j_ret_out.end[2])
            sp.dma_start(DTAB[:, :, :], c_rope_diff).then_inc(s_dtab, 16)
            load(j_kv_k, cols(w_kv, 0))
            load(j_kv_v, cols(w_kv, D))
            load(j_diff_q, cols(w_in_b, 0))
            load(j_diff_gate, cols(w_in_b, D))
            load(j_diff_out, cols(w_out_b, 0))

            def pairs(w_gate, w_up, first):
                def f(i, j, dst, s):
                    w = (w_gate, w_up)[j % 2]
                    sp.dma_start(dst.rearrange("p (c n) -> p c n", c=KC),
                                 w[:, :, bass.ds(2 * UCOL * i + (first + (j // 2) * UCOL), UCOL)]).then_inc(s, 16)
                return f

            def load_ffn(name):
                f0 = 0
                wg, wu, wd = w_ffn[name]
                for part, (jg, jd) in zip(FFN_PARTS, ffns[name]):
                    load(jg, pairs(wg, wu, f0 * P))
                    load(jd, folded(wd, f0, part // 2))
                    f0 += part

            load_ffn("ffn1")

            def unit_dst(jb, n=0):
                u = jb.unit0 + n
                sp.wait_ge(lo_done, u - RAWS + 1)
                return RAW[:, u % RAWS, :], raw_in[u % RAWS]

            sp.wait_ge(done, at_mix[2])
            sp.dma_start(MTAB[:, :, :], c_rope_mla).then_inc(s_mtab, 16)
            sp.dma_start(CMASK[:, :], c_causal).then_inc(s_cmask, 16)
            load(j_cq, cols(w_in, 0))
            dst, s = unit_dst(j_kvm)
            d3 = dst.rearrange("p (c n) -> p c n", c=KC)
            kr = MLA_Q_RANK + MLA_KV_RANK
            for a, b, n in ((0, MLA_Q_RANK, MLA_KV_RANK + MLA_ROPE), (160, kr + 16, 16), (176, kr, 16),
                            (192, kr + MLA_ROPE + 3 * GDN_WIDTH, 64)):
                sp.dma_start(d3[:, :, a:a + n], w_in[:, :, b:b + n]).then_inc(s, 16)
            dst, s = unit_dst(j_uq)
            for k in range(2):
                d3 = dst[:, 1024 * k:1024 * (k + 1)]
                for off, a, b, n in ((0, 0, 0, MLA_NOPE), (512, 0, MLA_NOPE, 32), (768, 0, MLA_NOPE + 16, 16),
                                     (768, 16, MLA_NOPE, 16)):
                    wide = MLA_NOPE if off == 0 else 32
                    sp.dma_start(d3[:, off:off + HEADS * wide].rearrange("p (h n) -> p h n", h=HEADS)[:, :, a:a + n],
                                 w_uq[:, k, :, b:b + n]).then_inc(s, 16)
            dst, s = unit_dst(j_ukv)
            for k in range(2):
                sp.dma_start(dst[:, 512 * k:512 * (k + 1)].rearrange("p (h n) -> p h n", h=HEADS),
                             w_ukv[:, :, MLA_NOPE * k:MLA_NOPE * (k + 1)]).then_inc(s, 16)
            first = MLA_Q_RANK + MLA_KV_RANK + MLA_ROPE
            load(j_gqkv, cols(w_in, first))
            sp.wait_ge(kr_done, 4)
            sp.dma_start(TRI[:, :, :], c_tri).then_inc(s_tri, 16)
            sp.wait_ge(ma_pt, len(mla_turns))
            sp.dma_start(ALROW[:, 0:8], A["a_log_2"]).then_inc(s_al, 16)
            sp.dma_start(ALROW[:, 8:16], A["dt_bias_2"]).then_inc(s_al, 16)
            load(j_z, cols(w_in, first + 3 * GDN_WIDTH + 16))
            first += 3 * GDN_WIDTH + 16 + GDN_WIDTH
            for u in range(j_merge.units):
                n, q = u // 3, u % 3
                dst, s = unit_dst(j_merge, u)
                if q < 2:
                    a = first + q * D + n * UCOL
                    sp.dma_start(dst.rearrange("p (c n) -> p c n", c=KC), w_in[:, :, a:a + UCOL]).then_inc(s, 16)
                else:
                    d3 = dst.rearrange("p (b c n) -> p b c n", b=2, c=4)
                    for b, w in enumerate((w_mla_o, w_gdn_o)):
                        sp.dma_start(d3[:, b, :, :], w[:, :, n * UCOL:(n + 1) * UCOL]).then_inc(s, 16)
            load(j_wout, cols(w_out2, 0))
            load_ffn("ffn2")
            for t in range(NT):
                sp.wait_ge(ps_free[(at_rows[1] + t) % SLOTS], (at_rows[1] + t) // SLOTS + 1)
                sp.dma_start(out[0, P * t:P * (t + 1), :], OUTR[:, t, :]).then_inc(s_out, 16)
            sp.wait_ge(s_out, 16 * NT)

        @block.gpsimd
        def _(pool):
            pool.memset(ONES[:, :], 1.0).then_inc(s_ones, 1)
            pool.memset(MHALF[:, :], -0.5).then_inc(s_half, 1)
            pool.memset(ROWS[:, 0:64], 1.0).then_inc(s_rows, 1)
            pool.memset(ROWS[:, 64:128], 0.0).then_inc(s_rows, 1)
            pool.memset(ROWS[:, 128:192], NEG).then_inc(s_rows, 1)
            pool.wait_ge(s_half, 1)

            def lo(u, i):
                pool.wait_ge(hi_done, u + 1 + 4 * i)
                pool.tensor_tensor(WL[:, u % SPLITS, :], RAW[:, u % RAWS, :], WH[:, u % SPLITS, :].bitcast(F32),
                                   ALU.subtract).then_inc(lo_done, 1)

            def split(jb):
                def body(i, j):
                    if not isinstance(i, int) or jb.unit0 + 4 * i + j + 1 < n_units:
                        lo(jb.unit0 + j + 1, i)
                each(pool, jb, body)

            lo(0, 0)
            split(j_ret_qk)
            split(j_ret_v)
            for h in range(HEADS):
                pool.wait_ge(ra_ve, h + 1)
                pool.tensor_tensor(RSTD[:, 0:NT], VEPS[:, 0:NT], MHALF[:, 0:NT], ALU.pow).then_inc(ra_rs, 1)
            split(j_ret_gate)
            split(j_ret_out)
            split(j_kv_k)
            split(j_kv_v)
            split(j_diff_q)
            for h in range(HEADS):
                pool.wait_ge(da_ve, 2 * h + 2)
                pool.tensor_tensor(RSTD[:, 0:NT], VEPS[:, 0:NT], MHALF[:, 0:NT], ALU.pow).then_inc(da_rs, 1)
            split(j_diff_gate)
            split(j_diff_out)
            for jg, jd in ffns["ffn1"]:
                split(jg)
                split(jd)
            split(j_cq)
            split(j_kvm)
            split(j_uq)
            split(j_ukv)
            pool.wait_ge(ma_pt, len(mla_turns))
            pool.memset(BA[:, :, :], 0.0).then_inc(ba_zero, 1)
            pool.memset(PRE[:, :, 0:CONV - 1], 0.0).then_inc(pre_zero, 1)
            split(j_gqkv)
            split(j_z)
            for t in range(NT + 1):
                w, _ = tile(t)
                pool.wait_ge(g_dve, N_PRE_DVE)
                pool.wait_ge(s_tri, 16)
                pool.wait_ge(conv_done, 12)
                if t:
                    pool.wait_ge(g_pe, PE_AT[t - 1, ("x", levels(t - 1)[-1], 1)])
                pool.tensor_tensor(UG[0:w, :, 0:w], TRI[0:w, 0:1, 0:w].to_broadcast([w, HEADS, w]),
                                   over_heads(GG[0:w, t, :], w, w), ALU.mult).then_inc(g_pool, one("pool", t, "ug"))
                pool.wait_ge(g_dve, DVE_AT[t, "seps"])
                pool.tensor_tensor(RN[0:w, :], SSV[0:w, :], MHALF[0:w, 0:1].to_broadcast([w, 16]),
                                   ALU.pow).then_inc(g_pool, one("pool", t, "rnorm"))
                pool.wait_ge(g_act, ACT_AT[t, "rows"])
                pool.wait_ge(g_dve, DVE_AT[t, "f_kbg"])
                pool.tensor_tensor(by_head(KBG[0:w, :]), by_head(ROWQ[0:w, 1, :]), over_heads(FAC[0:w, 3, :], w, GDN_D),
                                   ALU.mult).then_inc(g_pool, one("pool", t, "kbg"))
                pool.tensor_tensor(by_head(KD[0:w, :]), by_head(ROWQ[0:w, 1, :]), over_heads(FAC[0:w, 4, :], w, GDN_D),
                                   ALU.mult).then_inc(g_pool, one("pool", t, "kd"))
                pool.tensor_tensor(by_head(ROWQ[0:w, 2, :]), by_head(ROWQ[0:w, 2, :]), over_heads(BETA[0:w, t, :], w, GDN_D),
                                   ALU.mult).then_inc(g_pool, one("pool", t, "vb"))
                pool.wait_ge(g_pe, PE_AT[t, "kq" if t else "kk"])
                pool.tensor_copy(TI[0:w, :, 0:w], IDENT[0:w, 0:w].unsqueeze(1).to_broadcast([w, HEADS, w]))
                pool.tensor_copy(TIT[0:w, :, 0:w], IDENT[0:w, 0:w].unsqueeze(1).to_broadcast([w, HEADS, w])).then_inc(
                    g_pool, one("pool", t, "eye"))
                if t:
                    pool.wait_ge(g_dve, DVE_AT[t, "at"])
                    pool.wait_ge(g_act, ACT_AT[t, "decay"])
                    pool.tensor_tensor(AT[:, :, :], AT[:, :, :], DEC[:, :, :], ALU.mult).then_inc(g_pool, one("pool", t, "at"))
                    pool.wait_ge(g_dve, DVE_AT[t, "out_eps"])
                    pool.tensor_tensor(ORN[:, :], OSS[:, :], MHALF[:, :], ALU.pow).then_inc(g_pool, one("pool", t, "out_rnorm"))

            for u in range(j_merge.units):
                lo(j_merge.unit0 + u + 1, 0)
            split(j_wout)
            for jg, jd in ffns["ffn2"]:
                split(jg)
                split(jd)

        @block.scalar
        def _(act):
            def hi(u, i, used):
                act.wait_ge(raw_in[u % RAWS], 16 * i + 16 * (u // RAWS + 1) + 16 * extra_loads(u))
                if used is not None:
                    act.wait_ge(done, used)
                nc.scalar.activation(WH[:, u % SPLITS, :], RAW[:, u % RAWS, :], ACT.Copy).then_inc(hi_done, 1)

            def next_hi(jb, i, j):
                if not isinstance(i, int) or jb.unit0 + 4 * i + j + 1 < n_units:
                    hi(jb.unit0 + j + 1, i, jb.tick0 + 8 * i + 2 * j)

            def square(src, q, width):
                if not isinstance(q, int) or q >= 2:
                    act.wait_ge(sq_added, q - 1)
                par = q % 2 if isinstance(q, int) else square.par
                nc.scalar.activation(halves(SQ[:, par, 0:width]), src, ACT.Square).then_inc(sq_done, 1)

            def root(name):
                n, _, cols = norms[name][:3]
                k, w = token_tiles(width_of(cols))
                act.wait_ge(inv_done, n + 1)
                nc.scalar.activation(STAT[0:w, 2, 0:k], STAT[0:w, 1, 0:k], ACT.Sqrt).then_inc(root_done, 1)

            def u_hi(name, jb_before, dst=UH, count=KC):
                cols = norms[name][2]
                if jb_before is not None:
                    act.wait_ge(done, jb_before.end[2])
                for k in range(count):
                    act.wait_ge(t_done, applied[name] + k + 1)
                    nc.scalar.activation(dst[:, k, cols], TMP[:, k % 2, 0:width_of(cols)], ACT.Copy).then_inc(uh_done, 1)

            hi(0, 0, None)
            for k in range(KC):
                slot = (at_x[1] + k) % SLOTS
                act.wait_ge(done, at_x[2] + k + 1)
                square(acc(slot, SEQ), k, SEQ)
                nc.scalar.activation(RES[:, k, SEQ_COLS], acc(slot, SEQ), ACT.Copy).then_inc(ps_free[slot], 1)
            slot = (at_x[1] + KC) % SLOTS
            act.wait_ge(done, at_x[2] + KC + 1)
            nc.scalar.activation(GAINS[:, 0:N_ROWS], PS[:, 2 * slot, P:P + N_ROWS], ACT.Copy)
            nc.scalar.activation(RES[:, :, 0:META], PS[:, 2 * slot, 0:KC * META].rearrange("p (k n) -> p k n", k=KC),
                                 ACT.Copy).then_inc(ps_free[slot], 1)
            root("norm0")
            u_hi("norm0", None)
            act.wait_ge(lam_step, 2)
            nc.scalar.activation(LAMS[0:1, 2:4], LAMS[0:1, 0:2], ACT.Exp).then_inc(lam_exp, 1)

            jb = j_ret_qk

            def body(i, j):
                next_hi(jb, i, j)
                for m in range(2):
                    slot, uses = chunk_of(jb, i, j, m)
                    act.wait_ge(done, tick_of(jb, i, j, m))
                    wait(act, rope_done, 8 * i + max(2 * j + m - 1, 0))
                    nc.scalar.activation(SG[0:64, m, 0:SEQ], PS[64:128, 2 * slot, :], ACT.Copy).then_inc(shift_done, 1)
                    nc.scalar.activation(SG[64:128, m, 0:SEQ], PS[0:64, 2 * slot, :], ACT.Copy).then_inc(shift_done, 1)
            each(act, jb, body, peel=1)

            jb = j_ret_v

            def body(i, j):
                next_hi(jb, i, j)
                for m in range(2):
                    slot, uses = chunk_of(jb, i, j, m)
                    act.wait_ge(done, tick_of(jb, i, j, m))
                    nc.scalar.activation(V[:, 2 * m:2 * m + 2, bass.ds(4 * UCOL * i + j * UCOL, UCOL)],
                                         PS[:, 2 * slot, :].rearrange("p (t n) -> p t n", t=2),
                                         ACT.Copy).then_inc(ps_free[slot], 1)
            each(act, jb, body)

            act.wait_ge(rope_done, 2 * HEADS)
            for h in range(2):
                act.dma_start(DECAY[:, h % 2, 0:SEQ], c_decay[h]).then_inc(dec_in[h % 2], 16)
            for h in range(HEADS):
                act.wait_ge(ra_t, h + 1)
                nc.scalar.activation(QK[:, 2 * h:2 * h + 2, :], PS[:, 6:8, :], ACT.Copy).then_inc(ra_e, 1)
                if h + 2 < HEADS:
                    act.wait_ge(ra_m, NT * (h + 1))
                    act.dma_start(DECAY[:, h % 2, 0:SEQ], c_decay[h + 2]).then_inc(dec_in[h % 2], 16)

            jb = j_ret_gate

            def body(i, j):
                next_hi(jb, i, j)
                for m in range(2):
                    slot, uses = chunk_of(jb, i, j, m)
                    act.wait_ge(done, tick_of(jb, i, j, m))
                    wait(act, y_done, 8 * i + max(2 * j + m - 1, 0))
                    nc.scalar.activation(SG[:, m, 0:SEQ], acc(slot, SEQ), ACT.Silu).then_inc(ps_free[slot], 1)
                    act.wait_ge(y_done, 8 * i + 2 * j + m + 1)
                    nc.scalar.activation(YH[:, bass.ds(8 * i + (2 * j + m), 1), :],
                                         TMP[:, m:m + 1, 0:SEQ], ACT.Copy).then_inc(yh_done, 1)
            each(act, jb, body, peel=1)

            jb = j_ret_out
            q0 = norms["post0"][3]

            def body(i, j):
                next_hi(jb, i, j)
                if j % 2:
                    for m in range(2):
                        slot, uses = chunk_of(jb, i, j, m)
                        act.wait_ge(done, tick_of(jb, i, j, m))
                        square.par = m
                        square(acc(slot, SEQ), q0 + 4 * i + (j - 1 + m), SEQ)
                        nc.scalar.activation(Y2[:, bass.ds(4 * i + (j - 1 + m), 1), :],
                                             PS[:, 2 * slot:2 * slot + 1, :], ACT.Copy).then_inc(ps_free[slot], 1)
            each(act, jb, body)
            root("post0")

            def residual_squares(name, ready):
                cols, q0 = norms[name][2:4]
                for k in range(KC):
                    act.wait_ge(*ready(k))
                    square(halves(RES[:, k, cols]), q0 + k, width_of(cols))

            def swap_quarters(jb, n0, scale):
                def body(i, j):
                    next_hi(jb, i, j)
                    for m in range(2):
                        slot, uses = chunk_of(jb, i, j, m)
                        act.wait_ge(done, tick_of(jb, i, j, m))
                        act.wait_ge(rope_done, n0 + 8 * i + 2 * j + m - 1)
                        for a, b in ((0, 32), (32, 0), (64, 96), (96, 64)):
                            nc.scalar.activation(SG[a:a + 32, m, 0:SEQ], PS[b:b + 32, 2 * slot, :], ACT.Copy,
                                                 scale=scale).then_inc(shift_done, 1)
                each(act, jb, body)

            def keep_rows(jb, dst):
                def body(i, j):
                    next_hi(jb, i, j)
                    for m in range(2):
                        slot, uses = chunk_of(jb, i, j, m)
                        act.wait_ge(done, tick_of(jb, i, j, m))
                        nc.scalar.activation(dst[:, 2 * m:2 * m + 2, bass.ds(4 * UCOL * i + j * UCOL, UCOL)],
                                             PS[:, 2 * slot, :].rearrange("p (t n) -> p t n", t=2),
                                             ACT.Copy).then_inc(ps_free[slot], 1)
                each(act, jb, body)

            residual_squares("norm1", lambda k: (res_done, k + 1))
            root("norm1")
            u_hi("norm1", j_ret_out)
            swap_quarters(j_kv_k, 16, 1.0)
            keep_rows(j_kv_v, DV)
            u_hi("norm1q", j_kv_v)
            swap_quarters(j_diff_q, 24, DIFF_DH ** -0.5)

            for s in range(ITEMS + HEAD_LAG):
                if s < ITEMS:
                    h, b = s // NT, s % NT
                    n = P * (b + 1)
                    act.wait_ge(da_max, s + 1)
                    if s >= 2:
                        act.wait_ge(da_w, s - 1)
                    for t in range(2):
                        nc.scalar.activation(DE[:, s % 2, t, 0:n], PS[:, 2 * (s % 2) + t, 0:n], ACT.Exp,
                                             bias=NEGM[:, s % 2, t:t + 1],
                                             accum_out=ESUM[:, s % 2, t:t + 1]).then_inc(da_e, 1)
                for kind, g in [x for x in (("item", s - 1), ("head", (s - HEAD_LAG) / NT)) if x in turn_no]:
                    g = int(g)
                    no = turn_no[kind, g]
                    act.wait_ge(da_t, no + 1)
                    if kind == "item":
                        if g >= 2:
                            act.wait_ge(da_pv, g - 1)
                        n = P * (g % NT + 1)
                        nc.scalar.activation(DWT[:, g % 2, 0:n], PS[:, 4 + no % 2, 0:n], ACT.Copy).then_inc(da_wt, 1)
                    else:
                        nc.scalar.activation(DQK[:, g, :], PS[:, 4 + no % 2, :], ACT.Copy).then_inc(da_wt, 1)
                if s >= 6 and (s - 6) % NT == 0 and (s - 6) // NT < HEADS:
                    h = (s - 6) // NT
                    act.wait_ge(da_on, 2 * h + 1)
                    if h:
                        act.wait_ge(da_ve, 2 * h)
                    nc.scalar.activation(DSQ[:, :, :], DON[:, h % 2, :, :], ACT.Square).then_inc(da_sq, 1)

            jb = j_diff_gate

            def body(i, j):
                next_hi(jb, i, j)
                for m in range(2):
                    slot, uses = chunk_of(jb, i, j, m)
                    n = 8 * i + 2 * j + m
                    act.wait_ge(done, tick_of(jb, i, j, m))
                    act.wait_ge(y_done, 16 + n - 1)
                    nc.scalar.activation(SG[:, m, 0:SEQ], acc(slot, SEQ), ACT.Silu).then_inc(ps_free[slot], 1)
                    act.wait_ge(y_done, 16 + n + 1)
                    nc.scalar.activation(DYH[:, n, :], TMP[:, m, 0:SEQ], ACT.Copy).then_inc(yh_done, 1)
            each(act, jb, body)

            jb = j_diff_out

            def body(i, j):
                next_hi(jb, i, j)
                for m in range(2):
                    slot, uses = chunk_of(jb, i, j, m)
                    act.wait_ge(done, tick_of(jb, i, j, m))
                    n = 2 * (4 * i + j) + m
                    square(acc(slot, SEQ), norms["post1"][3] + n, SEQ)
                    nc.scalar.activation(Y2[:, n, :], acc(slot, SEQ), ACT.Copy).then_inc(ps_free[slot], 1)
            each(act, jb, body)
            root("post1")

            def res_chunk(k, cols):
                ap = RES[:, bass.ds(k, 1), cols]
                if width_of(cols) > 512:
                    return ap.rearrange("p o (a n) -> p (o a) n", a=2)
                return ap.rearrange("p o n -> p (o n)")

            def ffn_act(name, number, after):
                cols = norms[name][2]
                width = width_of(cols)
                for part, (jg, jd) in enumerate(ffns[name]):
                    h0 = 22 * number + (FFN_PARTS[0] if part else 0)
                    if part:
                        act.wait_ge(done, ffns[name][0][1].end[2])

                    def body(i, j):
                        next_hi(jg, i, j)
                        for m in range(2):
                            n = 2 * (j // 2) + m
                            slot, uses = chunk_of(jg, i, j, m)
                            if j % 2 == 0:
                                act.wait_ge(done, tick_of(jg, i, j, m))
                                wait(act, hl_done, h0 + 4 * i + max(n - 1, 0))
                                nc.scalar.activation(halves(SG[:, m, 0:width]), acc(slot, width),
                                                     ACT.Silu).then_inc(ps_free[slot], 1)
                            else:
                                act.wait_ge(ps_free[slot], uses + 1)
                                nc.scalar.activation(HH[:, bass.ds(4 * i + n, 1), 0:width], TMP[:, m:m + 1, 0:width],
                                                     ACT.Copy).then_inc(hh_done, 1)
                    each(act, jg, body, peel=int(h0 == 0))

                    def body(i, j):
                        next_hi(jd, i, j)
                        if j % 2 and part:
                            for m in range(2):
                                slot, uses = chunk_of(jd, i, j, m)
                                act.wait_ge(ps_free[slot], uses + 1)
                                square.par = m
                                square(res_chunk(4 * i + (j - 1 + m), cols), norms[after][3] + 4 * i + (j - 1 + m), width)
                    if after is None:
                        def body(i, j):
                            next_hi(jd, i, j)
                    each(act, jd, body)

            residual_squares("ffn1", lambda k: (res_done, KC + k + 1))
            root("ffn1")
            u_hi("ffn1", j_diff_out)
            ffn_act("ffn1", 0, "mix")

            root("mix")
            u_hi("mix", ffns["ffn1"][-1][0])
            next_hi(j_cq, 0, 0)
            q0 = norms["cq"][3]
            for m in range(2):
                slot, _ = chunk_of(j_cq, 0, 0, m)
                act.wait_ge(done, tick_of(j_cq, 0, 0, m))
                square(acc(slot, SEQ), q0 + m, SEQ)
                nc.scalar.activation(CQF[:, m, :], acc(slot, SEQ), ACT.Copy).then_inc(ps_free[slot], 1)
            next_hi(j_kvm, 0, 0)
            slot, _ = chunk_of(j_kvm, 0, 0, 0)
            act.wait_ge(done, tick_of(j_kvm, 0, 0, 0))
            q0 = norms["ckv"][3]
            for a in range(2):
                square(PS[:, 2 * slot + a, 0:HALF], q0 + a, HALF)
            nc.scalar.activation(halves(CKF[:, 0, :]), acc(slot, TOK), ACT.Copy).then_inc(ps_free[slot], 1)
            slot, _ = chunk_of(j_kvm, 0, 0, 1)
            act.wait_ge(done, tick_of(j_kvm, 0, 0, 1))
            nc.scalar.activation(halves(MISC[:, :]), acc(slot, TOK), ACT.Copy).then_inc(ps_free[slot], 1)
            root("cq")
            u_hi("cq", None, CQH, 2)
            root("ckv")
            u_hi("ckv", None, CKH, 1)
            next_hi(j_uq, 0, 0)
            scale = float(MLA_NOPE + MLA_ROPE) ** -0.5
            for n in range(4):
                c = j_uq.chunk0 + 4 + n
                slot = c % SLOTS
                act.wait_ge(done, j_uq.tick0 + 4 + n + 1)
                nc.scalar.activation(QC[0:64, 2 * n, :], PS[0:64, 2 * slot, :], ACT.Copy, scale=scale)
                nc.scalar.activation(QC[0:64, 2 * n + 1, :], PS[64:128, 2 * slot, :], ACT.Copy,
                                     scale=scale).then_inc(ps_free[slot], 1)
            next_hi(j_ukv, 0, 0)
            for n in range(4):
                c = j_ukv.chunk0 + n
                slot = c % SLOTS
                act.wait_ge(done, j_ukv.tick0 + n + 1)
                nc.scalar.activation(halves(KCAT[0:64, 2 * n, :]), PS[0:64, 2 * slot:2 * slot + 2, 0:HALF], ACT.Copy)
                nc.scalar.activation(halves(KCAT[0:64, 2 * n + 1, :]), PS[64:128, 2 * slot:2 * slot + 2, 0:HALF],
                                     ACT.Copy).then_inc(ps_free[slot], 1)
            for t in range(NT + 1):
                c = j_ukv.chunk0 + 4 + t
                slot = c % SLOTS
                w = META if t == 0 else P
                act.wait_ge(done, j_ukv.tick0 + 4 + t + 1)
                nc.scalar.activation(MV[0:w, t, :], PS[0:w, 2 * slot, :], ACT.Copy).then_inc(ps_free[slot], 1)
            for s in range(HEADS * NT + MLA_LAG):
                if s < HEADS * NT:
                    b = s % NT
                    n = META + P * (b + 1)
                    act.wait_ge(ma_max, s + 1)
                    if s >= 2:
                        act.wait_ge(ma_t, mla_turn_no["item", s - 2] + 1)
                    k = 2 * (s % 2)
                    src = PS[:, k, 0:n] if n <= 512 else PS[:, k:k + 2, 0:HALF]
                    nc.scalar.activation(halves(ME[:, s % 2, 0:n]), src, ACT.Exp, bias=NEGM2[:, s % 2:s % 2 + 1],
                                         accum_out=ESUM2[:, (s // NT) % 4, b:b + 1]).then_inc(ma_e, 1)
                for kind, g in mla_step_turns(s):
                    no = mla_turn_no[kind, g]
                    act.wait_ge(ma_t, no + 1)
                    if kind == "item":
                        b = g % NT
                        if g >= 2:
                            act.wait_ge(ma_pv, g - 1)
                        if b < NT - 1:
                            n = P * (b + 2)
                            nc.scalar.activation(MPT[:, g % 2, 0:n], PS[:, 4 + no % 2, 0:n], ACT.Copy).then_inc(ma_pt, 1)
                        else:
                            nc.scalar.activation(MPT[:, g % 2, 0:SEQ], PS[:, 4 + no % 2, :], ACT.Copy)
                            nc.scalar.activation(MPT[0:META, g % 2, SEQ:640], PS[0:META, 7, 0:P],
                                                 ACT.Copy).then_inc(ma_pt, 1)
                    else:
                        nc.scalar.activation(OMF[:, g, :], PS[:, 4 + no % 2, :], ACT.Copy).then_inc(ma_pt, 1)

            jb = j_gqkv
            for n in range(14):
                if n < 12:
                    i, j, m = n // 8, n // 2 % 4, n % 2
                    if m == 0:
                        next_hi(jb, 0, n // 2)
                    slot, uses = chunk_of(jb, 0, n // 2, m)
                    act.wait_ge(done, tick_of(jb, 0, n // 2, m))
                    if n >= 2:
                        act.wait_ge(tap_done, 4 * (n - 1))
                    nc.scalar.activation(halves(PRE[:, m, CONV - 1:CONV - 1 + TOK]), acc(slot, TOK),
                                         ACT.Copy).then_inc(ps_free[slot], 1)
                if n >= 1 and n <= 12:
                    act.wait_ge(tap_done, 4 * n)
                    nc.scalar.activation(CVS[:, n - 1, :], TMP[:, (n - 1) % 2, :], ACT.Silu).then_inc(conv_done, 1)
            jb = j_z
            for j in range(2):
                next_hi(jb, 0, j)
                for m in range(2):
                    slot, uses = chunk_of(jb, 0, j, m)
                    act.wait_ge(done, tick_of(jb, 0, j, m))
                    nc.scalar.activation(ZS[:, 2 * j + m, :], acc(slot, SEQ), ACT.Silu).then_inc(ps_free[slot], 1)
            act.wait_ge(g_pe, 1)
            act.wait_ge(ba_zero, 1)
            nc.scalar.activation(BA[:, 1:NT + 1, :], PS[:, 0, 16:80].rearrange("p (t n) -> p t n", t=NT), ACT.Copy)
            nc.scalar.activation(BA[0:META, 0, :], PS[0:META, 0, 0:16], ACT.Copy).then_inc(g_act, 1)
            nc.scalar.activation(EAL[:, :], PS[:, 1, 0:8], ACT.Exp).then_inc(g_act, 1)
            act.wait_ge(g_act, 1)
            nc.scalar.activation(BETA[:, :, :], BA[:, :, 0:8], ACT.Exp, scale=-1.0).then_inc(g_act, 1)
            act.wait_ge(g_dve, 3)
            nc.scalar.activation(EN[:, :, :], XA[:, :, :], ACT.Exp).then_inc(g_act, 1)
            act.wait_ge(g_dve, 6)
            nc.scalar.activation(LNE[:, :, :], EN[:, :, :], ACT.Ln).then_inc(g_act, 1)
            act.wait_ge(g_pe, N_PRE_PE)
            nc.scalar.activation(GEXP[:, 0:80], PS[:, 2, 0:80], ACT.Exp)
            nc.scalar.activation(GEXP[:, 80:96], PS[:, 3, 80:96], ACT.Exp)
            nc.scalar.activation(GEXP[0:META, 96:112], PS[0:META, 2, 96:112], ACT.Exp).then_inc(gexp_done, 1)
            for t in range(NT + 1):
                w, cols = tile(t)
                q0 = 0 if t else 1
                act.wait_ge(g_pe, PE_AT[t, "turn_in"])
                if t:
                    act.wait_ge(g_pool, POOL_AT[t, "ug"])
                    if t > 1:
                        act.wait_ge(g_pe, PE_AT[t - 1, "turn_out"])
                        act.wait_ge(g_pool, POOL_AT[t - 1, "at"])
                    act.wait_ge(g_dve, DVE_AT[t - 1, ("s", 1 if t > 1 else 0)])
                    act.wait_ge(g_pe, PE_AT[t - 1, "uw"])
                nc.scalar.activation(GSQ[0:w, q0:2, :], PS[0:w, q0:2, :], ACT.Square).then_inc(g_act, one("act", t, "square"))
                nc.scalar.activation(ROWQ[0:w, q0:3, :], PS[0:w, q0:3, :], ACT.Copy).then_inc(g_act, one("act", t, "rows"))
                act.wait_ge(g_pe, PE_AT[t, "decay"])
                act.wait_ge(g_dve, DVE_AT[t, "ssum"])
                for b in range(2):
                    last = nc.scalar.activation(DEC[0:w, 4 * b:4 * b + 4, 0:w],
                                                PS[0:w, b, 0:4 * w].rearrange("p (h c) -> p h c", h=4), ACT.Exp)
                last.then_inc(g_act, one("act", t, "decay"))
                act.wait_ge(g_pe, PE_AT[t, "turn_scaled"])
                for bank, dst in ((3, KT), (4, QT), (5, KBT), (6, QGT)):
                    if t or bank in (3, 5):
                        last = nc.scalar.activation(dst[:, :, 0:w], PS[:, bank, 0:4 * w].rearrange("p (h c) -> p h c", h=4),
                                                    ACT.Copy)
                last.then_inc(g_act, one("act", t, "turned"))
                act.wait_ge(g_pe, PE_AT[t, "uw"])
                if t:
                    nc.scalar.activation(WTT[:, :, :], PS[:, 6, :].rearrange("p (h c) -> p h c", h=4), ACT.Copy)
                nc.scalar.activation(UU[0:w, :], PS[0:w, 5, :], ACT.Copy).then_inc(g_act, one("act", t, "uw"))
                if t:
                    act.wait_ge(g_dve, DVE_AT[t, "out_join"])
                    nc.scalar.activation(GSQ[:, 1, :], GON[:, :], ACT.Square).then_inc(g_act, one("act", t, "out_square"))

            def merge_chunk(n, c):
                chunk = j_merge.chunk0 + 8 * n + c
                return chunk % SLOTS, chunk // SLOTS, j_merge.tick0 + 8 * n + c + 1

            act.wait_ge(g_dve, DVE_AT[NT, "out_gate"])
            next_hi(j_merge, 0, 0)
            for k in range(4):
                nc.scalar.activation(OMH[:, k, :], OMF[:, k, :], ACT.Copy).then_inc(oh_done, 1)
            for k in range(4):
                nc.scalar.activation(GOH[:, k, :], ZS[:, k, :], ACT.Copy).then_inc(gh_done, 1)
            for n in range(4):
                for q in range(3):
                    if n or q:
                        hi(j_merge.unit0 + 3 * n + q + 1, 0, j_merge.tick0 + 8 * n + 2 * q)
                    if q < 2:
                        for m in range(2):
                            slot, uses, tick = merge_chunk(n, 2 * q + m)
                            act.wait_ge(done, tick)
                            if n:
                                act.wait_ge(ml_done, 2 * n)
                            nc.scalar.activation(GATE[:, q, m, :], acc(slot, SEQ), ACT.Sigmoid).then_inc(ps_free[slot], 1)
                for m in range(2):
                    act.wait_ge(merged_done, 2 * n + m + 1)
                    nc.scalar.activation(MH[:, 2 * n + m, :], GATE[:, 0, m, :], ACT.Copy).then_inc(mh_done, 1)
            q0 = norms["ffn2"][3]
            for j in range(j_wout.units):
                next_hi(j_wout, 0, j)
                for m in range(2):
                    slot, uses = chunk_of(j_wout, 0, j, m)
                    act.wait_ge(ps_free[slot], uses + 1)
                    square(RES[:, 2 * j + m, SEQ_COLS], q0 + 2 * j + m, SEQ)
            root("ffn2")
            u_hi("ffn2", j_merge)
            ffn_act("ffn2", 1, "final")
            root("final")
            for t in range(0, NT, 2):
                slot = (at_rows[1] + t) % SLOTS
                act.wait_ge(done, at_rows[2] + t + 1)
                nc.scalar.activation(OUTR[:, t, :], PS[:, 2 * slot:2 * slot + 2, :].rearrange("p a n -> p (a n)"),
                                     ACT.Copy).then_inc(ps_free[slot], 1)

        @block.vector
        def _(dve):
            def add_square(q, first, width, par):
                dve.wait_ge(sq_done, q + 1)
                if first:
                    nc.vector.tensor_copy(SUMSQ[:, 0:width], SQ[:, par, 0:width]).then_inc(sq_added, 1)
                else:
                    dve.wait_ge(sq_added, q)
                    nc.vector.tensor_tensor(SUMSQ[:, 0:width], SUMSQ[:, 0:width], SQ[:, par, 0:width],
                                            ALU.add).then_inc(sq_added, 1)

            def spread(name):
                n, (_, chunk, tick), cols, _, _, features = norms[name]
                k, w = token_tiles(width_of(cols))
                slot = chunk % SLOTS
                dve.wait_ge(done, tick + 1)
                nc.vector.tensor_scalar(STAT[0:w, 0, 0:k], PS[0:w, 2 * slot, 0:k], 1.0 / features, EPS,
                                        ALU.mult, ALU.add).then_inc(ps_free[slot], 1)
                dve.wait_ge(ps_free[slot], chunk // SLOTS + 1)
                nc.vector.reciprocal(STAT[0:w, 1, 0:k], STAT[0:w, 0, 0:k]).then_inc(inv_done, 1)
                dve.wait_ge(root_done, n + 1)
                for t in range(k):
                    last = nc.vector.tensor_scalar(DIAG[0:w, t * w:(t + 1) * w], IDENT[0:w, 0:w],
                                                   STAT[0:w, 2, t:t + 1], None, ALU.mult)
                last.then_inc(diag_done, 1)

            def apply(name, gain, x=RES, lo=UL, hi=UH, count=KC, kept=None, keep=None):
                n, (_, chunk, tick), cols = norms[name][:3]
                width = width_of(cols)
                slot = (chunk + 1) % SLOTS
                a = applied[name]
                src = acc(slot, width) if kept is None else kept
                if kept is None:
                    dve.wait_ge(done, tick + 2)

                def low(k):
                    dve.wait_ge(uh_done, a + k + 1)
                    nc.vector.tensor_tensor(lo[:, k, cols], TMP[:, k % 2, 0:width], hi[:, k, cols].bitcast(F32),
                                            ALU.subtract).then_inc(ul_done, 1)
                for k in range(count):
                    if k >= 2:
                        low(k - 2)
                        dve.wait_ge(ul_done, a + k - 1)
                    nc.vector.scalar_tensor_tensor(
                        out=halves(TMP[:, k % 2, 0:width]), in0=halves(x[:, k, cols]),
                        scalar=GAINS[:, gain + k:gain + k + 1], in1=src, op0=ALU.mult, op1=ALU.mult).then_inc(t_done, 1)
                if keep is not None:
                    nc.vector.tensor_copy(keep, acc(slot, width)).then_inc(ps_free[slot], 1)
                elif kept is None:
                    nc.vector.tensor_copy(STAT[:, 0, 7:8], PS[:, 2 * slot, 0:1]).then_inc(ps_free[slot], 1)
                for k in range(max(count - 2, 0), count):
                    low(k)

            def post(name, gain, squares):
                n, (_, chunk, tick), cols = norms[name][:3]
                slot = (chunk + 1) % SLOTS
                b = KC * squares
                dve.wait_ge(done, tick + 2)
                for k in range(KC):
                    if k >= 2:
                        dve.wait_ge(res_done, b + k - 1)
                    nc.vector.scalar_tensor_tensor(
                        out=TMP[:, k % 2, 0:SEQ], in0=Y2[:, k, :], scalar=GAINS[:, gain * KC + k:gain * KC + k + 1],
                        in1=acc(slot, SEQ), op0=ALU.mult, op1=ALU.mult).then_inc(post_t, 1)
                    if k >= 1:
                        dve.wait_ge(post_t, b + k)
                        nc.vector.tensor_tensor(RES[:, k - 1, cols], RES[:, k - 1, cols], TMP[:, (k - 1) % 2, 0:SEQ],
                                                ALU.add).then_inc(res_done, 1)
                nc.vector.tensor_copy(STAT[:, 0, 7:8], PS[:, 2 * slot, 0:1]).then_inc(ps_free[slot], 1)
                dve.wait_ge(post_t, b + KC)
                nc.vector.tensor_tensor(RES[:, KC - 1, cols], RES[:, KC - 1, cols], TMP[:, (KC - 1) % 2, 0:SEQ],
                                        ALU.add).then_inc(res_done, 1)

            for k in range(KC):
                add_square(k, k == 0, SEQ, k % 2)
            dve.wait_ge(s_ident, 16)
            spread("norm0")
            for k in range(KC + 1):
                dve.wait_ge(ps_free[(at_x[1] + k) % SLOTS], (at_x[1] + k) // SLOTS + 1)
            apply("norm0", 0 * KC)
            dve.wait_ge(s_lamv, 64)
            nc.vector.tensor_tensor(LAMV[:, 0:2, :], LAMV[:, 0:2, :], LAMV[:, 2:4, :], ALU.mult).then_inc(lam_step, 1)
            dve.wait_ge(lam_step, 1)
            nc.vector.tensor_reduce(LAMS[0:1, 0:2], LAMV[:, 0:2, :], AX.X, ALU.add).then_inc(lam_step, 1)
            dve.wait_ge(lam_exp, 1)
            nc.vector.tensor_scalar(LAMS[0:1, 4:5], LAMS[0:1, 3:4], LAMS[0:1, 2:3], -LAMBDA_INIT,
                                    ALU.subtract, ALU.add).then_inc(lam_step, 1)
            slot = at_lam[1] % SLOTS
            dve.wait_ge(done, at_lam[2] + 1)
            nc.vector.tensor_scalar(LAMS[:, 6:7], GAINS[:, SUB_ROW:SUB_ROW + 1], 1.0 - LAMBDA_INIT, None,
                                    ALU.mult).then_inc(lam_step, 1)
            nc.vector.tensor_copy(LAMS[:, 5:6], PS[:, 2 * slot, 0:1]).then_inc(ps_free[slot], 1)
            dve.wait_ge(ps_free[slot], at_lam[1] // SLOTS + 1)
            nc.vector.tensor_copy(LAMS[:, 7:8], LAMS[:, 5:6]).then_inc(lam_step, 1)

            jb = j_ret_qk
            dve.wait_ge(s_tab, 16)

            def body(i, j):
                for m in range(2):
                    slot, uses = chunk_of(jb, i, j, m)
                    n = 2 * j + m
                    dve.wait_ge(done, tick_of(jb, i, j, m))
                    dve.wait_ge(shift_done, 16 * i + 2 * n + 2)
                    wait(dve, rope_done, 8 * i + max(n - 1, 0))
                    nc.vector.tensor_tensor(TMP[:, m, 0:SEQ], acc(slot, SEQ), TAB[:, 0, :], ALU.mult).then_inc(ps_free[slot], 1)
                    nc.vector.tensor_tensor(SG[:, m, 0:SEQ], SG[:, m, 0:SEQ], TAB[:, 1, :], ALU.mult).then_inc(sin_done, 1)
                    dve.wait_ge(ps_free[slot], uses + 1)
                    dve.wait_ge(sin_done, 8 * i + n + 1)
                    nc.vector.tensor_tensor(QK[:, bass.ds(i + 2 * n, 1), :], TMP[:, m:m + 1, 0:SEQ],
                                            SG[:, m:m + 1, 0:SEQ], ALU.add).then_inc(rope_done, 1)
            each(dve, jb, body, peel=1)

            OFF = [0, 512, 896, 1152]
            for h in range(HEADS + 1):
                if h < HEADS:
                    dve.wait_ge(dec_in[h % 2], 16 * (h // 2 + 1))
                    dve.wait_ge(ra_s, h + 1)
                    if h >= 2:
                        dve.wait_ge(ra_pv, h - 1)
                    for b in range(NT):
                        w = SEQ - P * b
                        nc.vector.tensor_tensor(SC[:, h % 2, OFF[b]:OFF[b] + w], PS[:, b, P * b:SEQ],
                                                DECAY[:, h % 2, 0:w], ALU.mult).then_inc(ra_m, 1)
                if h:
                    g = h - 1
                    dve.wait_ge(ra_pv, g + 1)
                    for b in range(NT):
                        nc.vector.bn_stats(BN6[:, b, :], PS[:, 4 + b // 2, RET_DV * (b % 2):RET_DV * (b % 2 + 1)]).then_inc(ra_bn, 1)
                    dve.wait_ge(ra_bn, 2 * NT * g + NT)
                    for b in range(NT):
                        nc.vector.bn_aggr(BNA[:, b, :], BN6[:, b, :]).then_inc(ra_bn, 1)
                    dve.wait_ge(ra_bn, 2 * NT * (g + 1))
                    nc.vector.tensor_scalar(VEPS[:, 0:NT], BNA[:, :, 1], EPS, None, ALU.add).then_inc(ra_ve, 1)
                    dve.wait_ge(ra_rs, g + 1)
                    if g:
                        dve.wait_ge(ra_t, g)
                    for b in range(NT):
                        last = nc.vector.tensor_scalar(
                            ON[:, b, :], PS[:, 4 + b // 2, RET_DV * (b % 2):RET_DV * (b % 2 + 1)],
                            BNA[:, b, 0:1], RSTD[:, b:b + 1], ALU.subtract, ALU.mult)
                    last.then_inc(ra_on, 1)

            jb = j_ret_gate
            dve.wait_ge(ra_e, HEADS)

            def body(i, j):
                for m in range(2):
                    slot, uses = chunk_of(jb, i, j, m)
                    n = 2 * j + m
                    dve.wait_ge(ps_free[slot], uses + 1)
                    nc.vector.tensor_tensor(TMP[:, m:m + 1, 0:SEQ], SG[:, m:m + 1, 0:SEQ],
                                            QK[:, bass.ds(8 * i + n, 1), :], ALU.mult).then_inc(y_done, 1)
                    dve.wait_ge(yh_done, 8 * i + n + 1)
                    nc.vector.tensor_tensor(YL[:, bass.ds(8 * i + n, 1), :], TMP[:, m:m + 1, 0:SEQ],
                                            YH[:, bass.ds(8 * i + n, 1), :].bitcast(F32), ALU.subtract).then_inc(yl_done, 1)
            each(dve, jb, body)

            jb = j_ret_out
            q0 = norms["post0"][3]
            add_square(q0, True, SEQ, 0)
            for k in range(1, KC):
                add_square(q0 + k, False, SEQ, k % 2)
            spread("post0")
            for s in range(SLOTS):
                dve.wait_ge(ps_free[s], len([c for c in range(at_post0[1]) if c % SLOTS == s]))
            post("post0", 1, 0)

            def rotate(jb, r0, tab, dst, scale):
                sh0 = 32 + 4 * (r0 - 16)

                def body(i, j):
                    for m in range(2):
                        slot, uses = chunk_of(jb, i, j, m)
                        n = 8 * i + 2 * j + m
                        dve.wait_ge(shift_done, sh0 + 4 * n + 4)
                        dve.wait_ge(rope_done, r0 + n - 1)
                        nc.vector.scalar_tensor_tensor(out=TMP[:, m, 0:SEQ], in0=acc(slot, SEQ), scalar=scale,
                                                       in1=tab[:, 0, :], op0=ALU.mult, op1=ALU.mult).then_inc(ps_free[slot], 1)
                        nc.vector.tensor_tensor(SG[:, m, 0:SEQ], SG[:, m, 0:SEQ], tab[:, 1, :], ALU.mult).then_inc(sin_done, 1)
                        dve.wait_ge(ps_free[slot], uses + 1)
                        dve.wait_ge(sin_done, r0 + n + 1)
                        nc.vector.tensor_tensor(dst(n), TMP[:, m, 0:SEQ], SG[:, m, 0:SEQ], ALU.add).then_inc(rope_done, 1)
                each(dve, jb, body)

            for k in range(KC):
                add_square(norms["norm1"][3] + k, k == 0, SEQ, k % 2)
            spread("norm1")
            apply("norm1", 2 * KC, keep=RB[:, :])
            dve.wait_ge(s_dtab, 16)
            rotate(j_kv_k, 16, DTAB, lambda n: DQK[:, HEADS + n, :], 1.0)
            dve.wait_ge(done, j_kv_v.end[2])
            dve.wait_ge(rope_done, 24)
            apply("norm1q", 3 * KC, kept=RB[:, :])
            rotate(j_diff_q, 24, DTAB, lambda n: DQK[:, n, :], DIFF_DH ** -0.5)

            dve.wait_ge(lam_step, 5)
            for s in range(ITEMS + HEAD_LAG):
                if s < 4 * HEADS:
                    n = P * (s % NT + 1)
                    dve.wait_ge(da_s, s + 1)
                    if s >= 2:
                        dve.wait_ge(da_e, 2 * (s - 1))
                    nc.vector.tensor_reduce(NEGM[:, s % 2, :], PS[:, 2 * (s % 2):2 * (s % 2) + 2, 0:n], AX.X, ALU.max,
                                            negate=True).then_inc(da_max, 1)
                if 1 <= s <= 4 * HEADS:
                    g = s - 1
                    h, b = g // NT, g % NT
                    n = P * (b + 1)
                    dve.wait_ge(da_e, 2 * g + 2)
                    if b == 0 and h >= 2:
                        dve.wait_ge(da_on, 2 * (h - 1) - 1)
                    nc.vector.reciprocal(RSUM[:, h % 2, b, :], ESUM[:, g % 2, :]).then_inc(da_c, 1)
                    dve.wait_ge(da_c, 2 * g + 1)
                    dve.wait_ge(da_w, g)
                    nc.vector.scalar_tensor_tensor(out=COEF[:, 0:1], in0=ESUM[:, g % 2, 0:1],
                                                   scalar=RSUM[:, h % 2, b, 1:2], in1=LAMS[:, 5:6],
                                                   op0=ALU.mult, op1=ALU.mult).then_inc(da_c, 1)
                    dve.wait_ge(da_c, 2 * g + 2)
                    if g >= 2:
                        dve.wait_ge(da_t, turn_no["item", g - 2] + 1)
                    nc.vector.scalar_tensor_tensor(out=DW[:, g % 2, 0:n], in0=DE[:, g % 2, 1, 0:n], scalar=COEF[:, 0:1],
                                                   in1=DE[:, g % 2, 0, 0:n], op0=ALU.mult, op1=ALU.add).then_inc(da_w, 1)
                if s >= 6 and (s - 6) % NT == 0 and (s - 6) // NT < HEADS:
                    h = (s - 6) // NT
                    dve.wait_ge(da_pv, NT * (h + 1))
                    if h >= 2:
                        dve.wait_ge(da_t, turn_no["head", h - 2] + 1)
                    nc.vector.tensor_tensor(DON[:, h % 2, :, :], PS[:, 6 + h % 2, :].rearrange("p (t n) -> p t n", t=NT),
                                            RSUM[:, h % 2, :, 0:1].to_broadcast([P, NT, P]), ALU.mult).then_inc(da_on, 1)
                if s >= 7 and (s - 7) % NT == 0 and (s - 7) // NT < HEADS:
                    h = (s - 7) // NT
                    dve.wait_ge(da_sq, h + 1)
                    nc.vector.tensor_reduce(SSQ[:, :], DSQ[:, :, :], AX.X, ALU.add).then_inc(da_ve, 1)
                    dve.wait_ge(da_ve, 2 * h + 1)
                    nc.vector.tensor_scalar(VEPS[:, 0:NT], SSQ[:, :], 1.0 / P, EPS, ALU.mult, ALU.add).then_inc(da_ve, 1)
                if s >= 8 and (s - 8) % NT == 0 and (s - 8) // NT < HEADS:
                    h = (s - 8) // NT
                    dve.wait_ge(da_rs, h + 1)
                    nc.vector.tensor_tensor(DON[:, h % 2, :, :], DON[:, h % 2, :, :],
                                            RSTD[:, 0:NT].unsqueeze(2).to_broadcast([P, NT, P]), ALU.mult).then_inc(da_on, 1)

            jb = j_diff_gate
            dve.wait_ge(da_wt, len(turns))

            def body(i, j):
                for m in range(2):
                    slot, uses = chunk_of(jb, i, j, m)
                    n = 8 * i + 2 * j + m
                    dve.wait_ge(ps_free[slot], uses + 1)
                    if n >= 2:
                        dve.wait_ge(yl_done, 16 + n - 1)
                    nc.vector.scalar_tensor_tensor(out=TMP[:, m, 0:SEQ], in0=DQK[:, n, :], scalar=LAMS[:, 6:7],
                                                   in1=SG[:, m, 0:SEQ], op0=ALU.mult, op1=ALU.mult).then_inc(y_done, 1)
                    dve.wait_ge(yh_done, 16 + n + 1)
                    nc.vector.tensor_tensor(DYL[:, n, :], TMP[:, m, 0:SEQ], DYH[:, n, :].bitcast(F32),
                                            ALU.subtract).then_inc(yl_done, 1)
            each(dve, jb, body)
            q0 = norms["post1"][3]
            dve.wait_ge(yl_done, 24)
            for k in range(KC):
                add_square(q0 + k, k == 0, SEQ, k % 2)
            spread("post1")
            for s, n in enumerate(uses_before(at_post1[1])):
                dve.wait_ge(ps_free[s], n)
            post("post1", 4, 1)

            def res_chunk(k, cols):
                ap = RES[:, bass.ds(k, 1), cols]
                if width_of(cols) > 512:
                    return ap.rearrange("p o (a n) -> p (o a) n", a=2)
                return ap.rearrange("p o n -> p (o n)")

            def ffn_dve(name, number, after):
                cols = norms[name][2]
                width = width_of(cols)
                for part, (jg, jd) in enumerate(ffns[name]):
                    h0 = 22 * number + (FFN_PARTS[0] if part else 0)
                    if part:
                        dve.wait_ge(done, ffns[name][0][1].end[2])

                    def body(i, j):
                        if j % 2:
                            for m in range(2):
                                n = 2 * (j // 2) + m
                                slot, uses = chunk_of(jg, i, j, m)
                                gslot, guses = chunk_of(jg, i, j - 1, m)
                                dve.wait_ge(done, tick_of(jg, i, j, m))
                                dve.wait_ge(ps_free[gslot], guses + 1)
                                wait(dve, hl_done, h0 + 4 * i + max(n - 1, 0))
                                nc.vector.tensor_tensor(halves(TMP[:, m, 0:width]), halves(SG[:, m, 0:width]),
                                                        acc(slot, width), ALU.mult).then_inc(ps_free[slot], 1)
                                dve.wait_ge(hh_done, h0 + 4 * i + n + 1)
                                nc.vector.tensor_tensor(HL[:, bass.ds(4 * i + n, 1), 0:width], TMP[:, m:m + 1, 0:width],
                                                        HH[:, bass.ds(4 * i + n, 1), 0:width].bitcast(F32),
                                                        ALU.subtract).then_inc(hl_done, 1)
                    each(dve, jg, body, peel=int(h0 == 0))

                    squares = part and after is not None
                    if squares:
                        nc.vector.memset(SUMSQ[:, 0:width], 0.0).then_inc(sum_zeroed, 1)
                        dve.wait_ge(sum_zeroed, number + 1)

                    def body(i, j):
                        if j % 2:
                            for m in range(2):
                                k = 4 * i + (j - 1 + m)
                                slot, uses = chunk_of(jd, i, j, m)
                                dve.wait_ge(done, tick_of(jd, i, j, m))
                                nc.vector.scalar_tensor_tensor(out=res_chunk(k, cols), in0=acc(slot, width), scalar=0.5,
                                                               in1=res_chunk(k, cols), op0=ALU.mult,
                                                               op1=ALU.add).then_inc(ps_free[slot], 1)
                            if squares:
                                for m in range(2):
                                    add_square(4 * i + (norms[after][3] + j - 1 + m), False, width, m)
                    each(dve, jd, body)

            for k in range(KC):
                add_square(norms["ffn1"][3] + k, k == 0, TOK, k % 2)
            spread("ffn1")
            apply("ffn1", 5 * KC)
            ffn_dve("ffn1", 0, "mix")

            dve.wait_ge(hl_done, 22)
            spread("mix")
            apply("mix", 6 * KC)
            q0 = norms["cq"][3]
            add_square(q0, True, SEQ, 0)
            add_square(q0 + 1, False, SEQ, 1)
            dve.wait_ge(done, at_cq[2] + 1)
            for a in range(2):
                q = norms["ckv"][3] + a
                dve.wait_ge(sq_done, q + 1)
                nc.vector.tensor_copy(SUMSQ[:, a * HALF:(a + 1) * HALF], SQ[:, a, 0:HALF]).then_inc(sq_added, 1)
            dve.wait_ge(ul_done, applied["cq"])
            spread("cq")
            dve.wait_ge(ps_free[chunk_of(j_cq, 0, 0, 1)[0]], chunk_of(j_cq, 0, 0, 1)[1] + 1)
            apply("cq", QN_ROW, CQF, CQL, CQH, 2)
            dve.wait_ge(ul_done, applied["ckv"])
            spread("ckv")
            dve.wait_ge(ps_free[chunk_of(j_kvm, 0, 0, 0)[0]], chunk_of(j_kvm, 0, 0, 0)[1] + 1)
            apply("ckv", KVN_ROW, CKF, CKL, CKH, 1)
            dve.wait_ge(s_mtab, 16)
            dve.wait_ge(ps_free[chunk_of(j_kvm, 0, 0, 1)[0]], chunk_of(j_kvm, 0, 0, 1)[1] + 1)
            dve.wait_ge(ul_done, applied["ffn2"])
            dve.wait_ge(done, at_ckv[2] + 2)
            nc.vector.tensor_tensor(TMP[0:32, 0, :], MISC[0:32, :], MTAB[0:32, 0, :], ALU.mult).then_inc(kr_done, 1)
            nc.vector.tensor_tensor(SG[0:32, 0, :], MISC[32:64, :], MTAB[32:64, 1, :], ALU.mult).then_inc(kr_done, 1)
            dve.wait_ge(kr_done, 2)
            nc.vector.tensor_tensor(KCAT[64:96, 0, :], TMP[0:32, 0, :], SG[0:32, 0, :], ALU.add).then_inc(kr_done, 1)
            dve.wait_ge(kr_done, 3)
            nc.vector.tensor_copy(KCAT[64:96, 1:HEADS, :], KCAT[64:96, 0:1, :].to_broadcast([32, HEADS - 1, TOK])).then_inc(kr_done, 1)
            scale = float(MLA_NOPE + MLA_ROPE) ** -0.5
            for r in range(2):
                c = j_uq.chunk0 + 2 * r
                sa, sb = c % SLOTS, (c + 1) % SLOTS
                dve.wait_ge(done, j_uq.tick0 + 2 * r + 2)
                if r:
                    dve.wait_ge(qr_done, 4)
                nc.vector.scalar_tensor_tensor(out=TMP[:, 0, 0:SEQ], in0=acc(sa, SEQ), scalar=scale,
                                               in1=MTAB[:, 0, META:TOK], op0=ALU.mult, op1=ALU.mult).then_inc(ps_free[sa], 1)
                nc.vector.scalar_tensor_tensor(out=SG[:, 0, 0:SEQ], in0=acc(sb, SEQ), scalar=scale,
                                               in1=MTAB[:, 1, META:TOK], op0=ALU.mult, op1=ALU.mult).then_inc(ps_free[sb], 1)
                dve.wait_ge(ps_free[sa], c // SLOTS + 1)
                dve.wait_ge(ps_free[sb], (c + 1) // SLOTS + 1)
                for g in range(4):
                    q = slice(32 * g, 32 * g + 32)
                    nc.vector.tensor_tensor(QC[64:96, 4 * r + g, :], TMP[q, 0, 0:SEQ], SG[q, 0, 0:SEQ],
                                            ALU.add).then_inc(qr_done, 1)
            for s in range(HEADS * NT + MLA_LAG):
                if s < HEADS * NT:
                    b = s % NT
                    n = META + P * (b + 1)
                    dve.wait_ge(ma_s, s + 1)
                    if s >= 2:
                        dve.wait_ge(ma_e, s - 1)
                    k = 2 * (s % 2)
                    if n <= 512:
                        nc.vector.tensor_reduce(NEGM2[:, s % 2:s % 2 + 1], PS[:, k, 0:n], AX.X, ALU.max,
                                                negate=True).then_inc(ma_max, 1)
                    else:
                        nc.vector.tensor_reduce(NEGM2[:, s % 2:s % 2 + 1], PS[:, k:k + 2, 0:HALF], AX.XY, ALU.max,
                                                negate=True).then_inc(ma_max, 1)
                if s >= 6 and (s - 6) % NT == 0 and (s - 6) // NT < HEADS:
                    h = (s - 6) // NT
                    if h >= 4:
                        dve.wait_ge(ma_on, h - 3)
                    dve.wait_ge(ma_e, NT * (h + 1))
                    nc.vector.reciprocal(RSUM2[:, h % 4, :], ESUM2[:, h % 4, :]).then_inc(ma_rs, 1)
                    dve.wait_ge(ma_rs, h + 1)
                    dve.wait_ge(ma_pv, NT * (h + 1))
                    pair = h // 2
                    if pair >= 2:
                        dve.wait_ge(ma_t, mla_turn_no["pair", pair - 2] + 1)
                    nc.vector.tensor_tensor(MON[:, pair % 2, :, 64 * (h % 2):64 * (h % 2) + 64],
                                            PS[:, 6, 0:256].rearrange("p (t n) -> p t n", t=NT),
                                            RSUM2[:, h % 4, :].unsqueeze(2).to_broadcast([P, NT, 64]),
                                            ALU.mult).then_inc(ma_on, 1)

            dve.wait_ge(pre_zero, 1)
            dve.wait_ge(qr_done, 8)
            for n in range(12):
                slot, uses = chunk_of(j_gqkv, 0, n // 2, n % 2)
                dve.wait_ge(ps_free[slot], uses + 1)
                if n >= 2:
                    dve.wait_ge(conv_done, n - 1)
                for tap in range(CONV):
                    x = PRE[:, n % 2, tap:tap + TOK]
                    c = CONV_ROW + 12 * tap + n
                    o = TMP[:, n % 2, :]
                    if tap:
                        dve.wait_ge(tap_done, 4 * n + tap)
                        nc.vector.scalar_tensor_tensor(out=o, in0=x, scalar=GAINS[:, c:c + 1], in1=o, op0=ALU.mult,
                                                       op1=ALU.add).then_inc(tap_done, 1)
                    else:
                        nc.vector.tensor_scalar(o, x, GAINS[:, c:c + 1], None, ALU.mult).then_inc(tap_done, 1)
            wide = [P, NT + 1, HEADS]
            dve.wait_ge(g_act, 2)
            nc.vector.tensor_tensor(XA[:, :, :], BA[:, :, 8:16], PS[:, 1, 8:16].unsqueeze(1).to_broadcast(wide),
                                    ALU.add).then_inc(g_dve, 1)
            dve.wait_ge(g_dve, 1)
            nc.vector.tensor_scalar(RELU[:, :, :], XA[:, :, :], 0.0, None, ALU.max).then_inc(g_dve, 1)
            dve.wait_ge(g_dve, 2)
            nc.vector.scalar_tensor_tensor(out=XA[:, :, :], in0=RELU[:, :, :], scalar=-2.0, in1=XA[:, :, :], op0=ALU.mult,
                                           op1=ALU.add).then_inc(g_dve, 1)
            dve.wait_ge(g_act, 3)
            nc.vector.tensor_scalar(BETA[:, :, :], BETA[:, :, :], 1.0, None, ALU.add).then_inc(g_dve, 1)
            dve.wait_ge(g_dve, 4)
            nc.vector.reciprocal(BETA[:, :, :], BETA[:, :, :]).then_inc(g_dve, 1)
            dve.wait_ge(g_act, 4)
            nc.vector.tensor_scalar(EN[:, :, :], EN[:, :, :], 1.0, None, ALU.add).then_inc(g_dve, 1)
            dve.wait_ge(g_act, 5)
            nc.vector.tensor_tensor(LNE[:, :, :], LNE[:, :, :], RELU[:, :, :], ALU.add).then_inc(sp_done, 1)
            dve.wait_ge(sp_done, 1)
            nc.vector.scalar_tensor_tensor(out=GG[:, :, :], in0=LNE[:, :, :], scalar=-1.0,
                                           in1=EAL[:, :].unsqueeze(1).to_broadcast(wide), op0=ALU.mult,
                                           op1=ALU.mult).then_inc(g_dve, 1)
            dve.wait_ge(gexp_done, 1)
            for s, n in enumerate(uses_before(j_z.end[1])):
                dve.wait_ge(ps_free[s], n)
            for t in range(NT + 1):
                w, cols = tile(t)
                f0 = 0 if t else 8
                q0 = 0 if t else 1
                dve.wait_ge(g_act, ACT_AT[t, "square"])
                if t:
                    dve.wait_ge(g_pool, POOL_AT[t - 1, "vb"])
                nc.vector.tensor_reduce(SSV[0:w, f0:16], GSQ[0:w, q0:2, :].rearrange("p a (h n) -> p (a h) n", h=HEADS),
                                        AX.X, ALU.add).then_inc(g_dve, one("dve", t, "ssum"))
                dve.wait_ge(g_dve, DVE_AT[t, "ssum"])
                if t == 0:
                    nc.vector.memset(SSV[0:w, 0:8], 1.0)
                nc.vector.tensor_scalar(SSV[0:w, f0:16], SSV[0:w, f0:16], EPS, None,
                                        ALU.add).then_inc(g_dve, one("dve", t, "seps"))
                dve.wait_ge(g_pool, POOL_AT[t, "rnorm"])
                rk, rq = RN[0:w, 8:16], RN[0:w, 0:8]
                nc.vector.tensor_tensor(FAC[0:w, 2, :], rk, BETA[0:w, t, :], ALU.mult).then_inc(g_dve, one("dve", t, "f_kb"))
                nc.vector.tensor_tensor(FAC[0:w, 4, :], rk, exp_rest(t), ALU.mult).then_inc(g_dve, one("dve", t, "f_kd"))
                dve.wait_ge(g_dve, DVE_AT[t, "f_kb"])
                nc.vector.tensor_tensor(FAC[0:w, 3, :], FAC[0:w, 2, :], exp_gc(t), ALU.mult).then_inc(
                    g_dve, one("dve", t, "f_kbg"))
                if t:
                    nc.vector.tensor_scalar(FAC[0:w, 0, :], rq, GDN_D ** -0.5, None, ALU.mult).then_inc(
                        g_dve, one("dve", t, "f_q"))
                    dve.wait_ge(g_dve, DVE_AT[t, "f_q"])
                    nc.vector.tensor_tensor(FAC[0:w, 5, :], FAC[0:w, 0, :], exp_gc(t), ALU.mult).then_inc(
                        g_dve, one("dve", t, "f_qg"))
                dve.wait_ge(g_act, ACT_AT[t, "rows"])
                if t:
                    dve.wait_ge(g_pe, PE_AT[t - 1, "uw"])
                    dve.wait_ge(g_pe, PE_AT[t - 1, ("state", 0 if t == 1 else 1)])
                    if t > 1:
                        dve.wait_ge(g_pe, PE_AT[t - 1, ("out", 1)])
                    dve.wait_ge(g_act, ACT_AT[t - 1, "uw"])
                todo = [("kb", KB, 1, FAC[0:w, 2, :]), ("nk", NK, 1, rk)]
                if t:
                    todo += [("nq", NQ, 0, FAC[0:w, 0, :]), ("qg", QG, 0, FAC[0:w, 5, :])]
                for name, dst, part, f in todo:
                    if name == "qg":
                        dve.wait_ge(g_dve, DVE_AT[t, "f_qg"])
                    nc.vector.tensor_tensor(by_head(dst[0:w, :]), by_head(ROWQ[0:w, part, :]), over_heads(f, w, GDN_D),
                                            ALU.mult).then_inc(g_dve, one("dve", t, name))
                dve.wait_ge(g_act, ACT_AT[t, "decay"])
                dve.wait_ge(g_pe, PE_AT[t, "kk"])

                def scores(dst, bank, b, factor):
                    return nc.vector.tensor_tensor(every_other(dst[0:w, :, 0:w], b),
                                                   PS[0:w, bank, 0:4 * w].rearrange("p (h c) -> p h c", h=4),
                                                   factor, ALU.mult)
                for b in range(2):
                    last = scores(LT, (2, 7)[b], b, every_other(DEC[0:w, :, 0:w], b))
                last.then_inc(g_dve, one("dve", t, "lt"))
                if t:
                    dve.wait_ge(g_pe, PE_AT[t, "kq"])
                    for b in range(2):
                        last = scores(AT, 3 + b, b, TRI[0:w, 0:1, 0:w].to_broadcast([w, 4, w]))
                    last.then_inc(g_dve, one("dve", t, "at"))
                for n, s in enumerate(levels(t)):
                    for g in range(2):
                        hs = slice(4 * g, 4 * g + 4)
                        dve.wait_ge(g_pe, PE_AT[t, ("x", s, g)])
                        if n == 0:
                            dve.wait_ge(g_pool, POOL_AT[t, "vb"])
                            dve.wait_ge(g_dve, DVE_AT[t, "qg" if t else "nk"])
                        nc.vector.tensor_tensor(XX[0:w, hs, 0:w], PS[0:w, g, 0:4 * w].rearrange("p (h c) -> p h c", h=4),
                                                TRI[0:w, 2 + n:3 + n, 0:w].to_broadcast([w, 4, w]),
                                                ALU.mult).then_inc(g_dve, one("dve", t, ("x", s, g)))
                    for g in range(2):
                        hs = slice(4 * g, 4 * g + 4)
                        dve.wait_ge(g_pe, PE_AT[t, ("y", s, g)])
                        for name, dst, bank, which in (("d", TI, (2, 7)[g], 0), ("e", TIT, 3 + g, 1)):
                            if name == "d" and s == levels(t)[-1]:
                                continue
                            if n:
                                dve.wait_ge(g_dve, DVE_AT[t, (name, levels(t)[n - 1], g)])
                            o = joined(dst[0:w, hs, 0:w], s, which)
                            y = PS[0:w, bank, 0:2 * w].rearrange("p (h b s) -> p h b s", h=4, s=s)
                            nc.vector.tensor_tensor(o, o, y, ALU.subtract).then_inc(g_dve, one("dve", t, (name, s, g)))
                for c in range(2 if t else 1):
                    r = slice(64 * c, 64 * c + 64)
                    no = 2 * (t - 1) + c + 1 if t else 0
                    if t:
                        dve.wait_ge(g_act, ACT_AT[t, "uw"])
                        dve.wait_ge(g_pe, PE_AT[t, ("ws", c)])
                        for par in range(2):
                            last = nc.vector.tensor_tensor(
                                every_other(by_head(VN[r, :]), par), every_other(by_head(UU[r, :]), par),
                                PS[r, 3 * par, 0:4 * GDN_D].rearrange("p (h n) -> p h n", h=4), ALU.subtract)
                        last.then_inc(g_dve, one("dve", t, ("vn", c)))
                        col = 64 + 16 * c + 4 * (t - 1)
                        dve.wait_ge(g_dve, DVE_AT[t if c else t - 1, ("s", 0 if c or t == 1 else 1)])
                        nc.vector.tensor_tensor(SS[:, :, :], ST[:, (no - 1) % 2, :, :],
                                                GEXP[:, col:col + 4].unsqueeze(2).to_broadcast([P, 4, GDN_D]),
                                                ALU.mult).then_inc(g_dve, one("dve", t, ("sd", c)))
                        dve.wait_ge(g_dve, DVE_AT[t, ("sd", c)])
                    dve.wait_ge(g_pe, PE_AT[t, ("state", c)])
                    new = PS[:, 1, 0:4 * GDN_D].rearrange("p (h n) -> p h n", h=4)
                    if t:
                        nc.vector.tensor_tensor(ST[:, no % 2, :, :], SS[:, :, :], new, ALU.add).then_inc(
                            g_dve, one("dve", t, ("s", c)))
                    else:
                        nc.vector.tensor_copy(ST[:, no % 2, :, :], new).then_inc(g_dve, one("dve", t, ("s", c)))
                if t:
                    dve.wait_ge(g_pe, PE_AT[t, ("out", 1)])
                    for par in range(2):
                        nc.vector.tensor_copy(every_other(by_head(GON[:, :]), par),
                                              PS[:, 4 + par, 0:4 * GDN_D].rearrange("p (h n) -> p h n", h=4)).then_inc(
                                                  g_dve, one("dve", t, ("out_inter", par)))
                    dve.wait_ge(g_dve, DVE_AT[t, ("out_inter", 1)])
                    nc.vector.tensor_tensor(GON[:, :], GON[:, :], PS[:, 2, :], ALU.add).then_inc(
                        g_dve, one("dve", t, "out_join"))
                    dve.wait_ge(g_act, ACT_AT[t, "out_square"])
                    if t > 1:
                        dve.wait_ge(g_pool, POOL_AT[t - 1, "out_rnorm"])
                    nc.vector.tensor_reduce(OSS[:, :], by_head(GSQ[:, 1, :]), AX.X, ALU.add).then_inc(
                        g_dve, one("dve", t, "out_sum"))
                    dve.wait_ge(g_dve, DVE_AT[t, "out_sum"])
                    nc.vector.tensor_scalar(OSS[:, :], OSS[:, :], 1.0 / GDN_D, EPS, ALU.mult, ALU.add).then_inc(
                        g_dve, one("dve", t, "out_eps"))
                    dve.wait_ge(g_pool, POOL_AT[t, "out_rnorm"])
                    nc.vector.tensor_tensor(by_head(GON[:, :]), by_head(GON[:, :]), over_heads(ORN[:, :], P, GDN_D),
                                            ALU.mult).then_inc(g_dve, one("dve", t, "out_norm"))
                    dve.wait_ge(g_pe, PE_AT[t, "turn_out"])
                    o = ZS[:, :, P * (t - 1):P * t]
                    nc.vector.scalar_tensor_tensor(out=o, in0=PS[:, 7, :].rearrange("p (h c) -> p h c", h=4),
                                                   scalar=GAINS[:, GDN_ROW:GDN_ROW + 1], in1=o, op0=ALU.mult,
                                                   op1=ALU.mult).then_inc(g_dve, one("dve", t, "out_gate"))

            for src, hi_part, lo_part, hi_sem, lo_sem in ((OMF, OMH, OML, oh_done, ol_done),
                                                          (ZS, GOH, GOL, gh_done, gl_done)):
                for k in range(4):
                    dve.wait_ge(hi_sem, k + 1)
                    nc.vector.tensor_tensor(lo_part[:, k, :], src[:, k, :], hi_part[:, k, :].bitcast(F32),
                                            ALU.subtract).then_inc(lo_sem, 1)
            for n in range(4):
                for m in range(2):
                    for b in range(2):
                        c = j_merge.chunk0 + 8 * n + 4 + 2 * m + b
                        gate = j_merge.chunk0 + 8 * n + 2 * b + m
                        dve.wait_ge(ps_free[gate % SLOTS], gate // SLOTS + 1)
                        dve.wait_ge(done, j_merge.tick0 + 8 * n + 4 + 2 * m + b + 1)
                        nc.vector.tensor_tensor(GATE[:, b, m, :], GATE[:, b, m, :], acc(c % SLOTS, SEQ),
                                                ALU.mult).then_inc(ps_free[c % SLOTS], 1)
                    for b in range(2):
                        c = j_merge.chunk0 + 8 * n + 4 + 2 * m + b
                        dve.wait_ge(ps_free[c % SLOTS], c // SLOTS + 1)
                    nc.vector.tensor_tensor(GATE[:, 0, m, :], GATE[:, 0, m, :], GATE[:, 1, m, :],
                                            ALU.add).then_inc(merged_done, 1)
                for m in range(2):
                    dve.wait_ge(mh_done, 2 * n + m + 1)
                    nc.vector.tensor_tensor(ML[:, 2 * n + m, :], GATE[:, 0, m, :], MH[:, 2 * n + m, :].bitcast(F32),
                                            ALU.subtract).then_inc(ml_done, 1)
            for k in range(KC):
                slot, uses = chunk_of(j_wout, 0, k // 2, k % 2)
                dve.wait_ge(done, tick_of(j_wout, 0, k // 2, k % 2))
                nc.vector.tensor_tensor(RES[:, k, SEQ_COLS], RES[:, k, SEQ_COLS], acc(slot, SEQ), ALU.add).then_inc(
                    ps_free[slot], 1)
                if k:
                    add_square(norms["ffn2"][3] + k - 1, k == 1, SEQ, (k - 1) % 2)
            add_square(norms["ffn2"][3] + KC - 1, False, SEQ, 1)
            spread("ffn2")
            apply("ffn2", 7 * KC)
            ffn_dve("ffn2", 1, "final")
            dve.wait_ge(hl_done, 44)
            spread("final")
            slot = (at_final[1] + 1) % SLOTS
            dve.wait_ge(done, at_final[2] + 2)
            for k in range(KC):
                nc.vector.scalar_tensor_tensor(out=FN[:, k, :], in0=RES[:, k, SEQ_COLS],
                                               scalar=GAINS[:, 8 * KC + k:8 * KC + k + 1], in1=acc(slot, SEQ),
                                               op0=ALU.mult, op1=ALU.mult).then_inc(f_done, 1)
            nc.vector.tensor_copy(STAT[:, 0, 7:8], PS[:, 2 * slot, 0:1]).then_inc(ps_free[slot], 1)
            for t in range(1, NT, 2):
                slot = (at_rows[1] + t) % SLOTS
                dve.wait_ge(done, at_rows[2] + t + 1)
                nc.vector.tensor_copy(OUTR[:, t, :], PS[:, 2 * slot:2 * slot + 2, :].rearrange("p a n -> p (a n)")).then_inc(
                    ps_free[slot], 1)

        @block.tensor
        def _(pe):
            def mm(o, a, b, start=True, stop=True, **kw):
                return nc.tensor.matmul(o, a, b, start=start, stop=stop, **kw)

            def turn(o, x, n):
                return nc.tensor.transpose(o, x, IDENT[0:n, 0:n])

            def project(jb, xh, xl, cols, kc=KC, k_ready=None):
                width = width_of(cols)
                parts = [cols] if width <= 512 else [slice(0, HALF), slice(HALF, TOK)]

                def body(i, j):
                    u = jb.unit0 + j
                    b = u % SPLITS
                    pe.wait_ge(lo_done, 4 * i + u + 1)
                    f = j % jb.fold
                    for m in range(2):
                        slot, uses = chunk_of(jb, i, j, m)
                        if f == 0:
                            slot_free(pe, slot, uses)
                        for k in range(kc):
                            kx = f * kc + k
                            wcols = slice(k * UCOL + m * P, k * UCOL + (m + 1) * P)
                            if k_ready is not None and m == 0:
                                pe.wait_ge(k_ready[0], k_ready[1] + kx + 1)
                            first, final = kx == 0, f == jb.fold - 1 and k == kc - 1
                            for w, x, pss in ((WH, xh, 0), (WH, xl, 1), (WL, xh, 2)):
                                for a, part in enumerate(parts):
                                    o = PS[:, 2 * slot + a, 0:part.stop - part.start]
                                    last = mm(o, w[:, b, wcols], x[:, kx, part], start=first and pss == 0,
                                              stop=final and pss == 2)
                        last.then_inc(done, 1)
                each(pe, jb, body)

            def project_rows(jb, xh, xl, col0):
                def body(i, j):
                    u = jb.unit0 + j
                    b = u % SPLITS
                    pe.wait_ge(lo_done, 4 * i + u + 1)
                    for m in range(2):
                        slot, uses = chunk_of(jb, i, j, m)
                        slot_free(pe, slot, uses)
                        for t in range(2):
                            c = slice(col0 + (2 * m + t) * P, col0 + (2 * m + t + 1) * P)
                            o = PS[:, 2 * slot, t * UCOL:(t + 1) * UCOL]
                            for k in range(KC):
                                w = slice(k * UCOL, (k + 1) * UCOL)
                                mm(o, xh[:, k, c], WH[:, b, w], start=k == 0, stop=False)
                                mm(o, xh[:, k, c], WL[:, b, w], start=False, stop=False)
                                last = mm(o, xl[:, k, c], WH[:, b, w], start=False, stop=k == KC - 1)
                        last.then_inc(done, 1)
                each(pe, jb, body)

            def norm_products(name):
                n, (_, chunk, tick), cols, before, squares, _ = norms[name]
                k, w = token_tiles(width_of(cols))
                slot = chunk % SLOTS
                slot_free(pe, slot, chunk // SLOTS)
                pe.wait_ge(sq_added, before + squares)
                for t in range(k):
                    last = mm(PS[0:w, 2 * slot, t:t + 1], SUMSQ[:, t * w:(t + 1) * w], ONES[:, 0:1])
                last.then_inc(done, 1)
                slot = (chunk + 1) % SLOTS
                slot_free(pe, slot, (chunk + 1) // SLOTS)
                pe.wait_ge(diag_done, n + 1)
                width = width_of(cols)
                if width <= 512:
                    last = mm(PS[:, 2 * slot, 0:width], ONES[0:w, :], DIAG[0:w, 0:width])
                else:
                    for a in range(2):
                        last = mm(PS[:, 2 * slot + a, 0:HALF], ONES[0:w, :], DIAG[0:w, a * HALF:(a + 1) * HALF])
                last.then_inc(done, 1)

            pe.wait_ge(s_ident, 16)
            pe.wait_ge(s_ones, 1)
            pe.wait_ge(s_x, 16)
            pe.wait_ge(s_meta, 16)
            for k in range(KC):
                c = at_x[1] + k
                slot_free(pe, c % SLOTS, c // SLOTS)
                for t in range(NT):
                    last = turn(PS[:, 2 * (c % SLOTS), t * P:(t + 1) * P], X0[:, t, k * P:(k + 1) * P], P)
                last.then_inc(done, 1)
            c = at_x[1] + KC
            slot_free(pe, c % SLOTS, c // SLOTS)
            for k in range(KC):
                turn(PS[:, 2 * (c % SLOTS), k * META:(k + 1) * META], M0[:, k * P:(k + 1) * P], META)
            pe.wait_ge(s_gain, 16 * (len(GAIN_ROWS) + len(other_rows(A)) + 1))
            last = turn(PS[:, 2 * (c % SLOTS), P:P + N_ROWS], GROW[0:N_ROWS, :], N_ROWS)
            last.then_inc(done, 1)
            norm_products("norm0")
            pe.wait_ge(lam_step, 3)
            c = at_lam[1]
            slot_free(pe, c % SLOTS, c // SLOTS)
            mm(PS[:, 2 * (c % SLOTS), 0:1], ONES[0:1, :], LAMS[0:1, 4:5]).then_inc(done, 1)
            project(j_ret_qk, UH, UL, SEQ_COLS, k_ready=(ul_done, 0))
            project_rows(j_ret_v, UH, UL, META)

            for s in range(SLOTS):
                pe.wait_ge(ps_free[s], len([c for c in range(j_ret_v.end[1]) if c % SLOTS == s]))
            pe.wait_ge(rope_done, 2 * HEADS)
            OFF = [0, 512, 896, 1152]
            for h in range(HEADS + 2):
                if h < HEADS:
                    if h:
                        pe.wait_ge(ra_m, NT * h)
                    for b in range(NT):
                        last = mm(PS[:, b, P * b:SEQ], QK[:, 2 * h + 1, P * b:P * (b + 1)], QK[:, 2 * h, P * b:SEQ])
                    last.then_inc(ra_s, 1)
                if 1 <= h <= HEADS:
                    g = h - 1
                    pe.wait_ge(ra_m, NT * (g + 1))
                    if g:
                        pe.wait_ge(ra_on, g)
                    for t in range(NT):
                        for b in range(t + 1):
                            o = OFF[b] + P * (t - b)
                            last = mm(PS[:, 4 + t // 2, RET_DV * (t % 2):RET_DV * (t % 2 + 1)],
                                      SC[:, g % 2, o:o + P], V[:, b, RET_DV * g:RET_DV * (g + 1)],
                                      start=b == 0, stop=b == t)
                    last.then_inc(ra_pv, 1)
                if h >= 2:
                    g = h - 2
                    pe.wait_ge(ra_on, g + 1)
                    if g:
                        pe.wait_ge(ra_e, g)
                    for e in range(2):
                        for t in range(NT):
                            last = turn(PS[:, 6 + e, P * t:P * (t + 1)], ON[:, t, P * e:P * (e + 1)], P)
                    last.then_inc(ra_t, 1)
            pe.wait_ge(ra_e, HEADS)
            project(j_ret_gate, UH, UL, SEQ_COLS)
            project(j_ret_out, YH, YL, PLAIN, k_ready=(yl_done, 0))
            norm_products("post0")
            norm_products("norm1")
            project(j_kv_k, UH, UL, SEQ_COLS, k_ready=(ul_done, applied["norm1"]))
            project_rows(j_kv_v, UH, UL, META)
            project(j_diff_q, UH, UL, SEQ_COLS, k_ready=(ul_done, applied["norm1q"]))

            pe.wait_ge(s_rows, 3)
            for s, n in enumerate(uses_before(j_diff_q.end[1])):
                pe.wait_ge(ps_free[s], n)
            pe.wait_ge(rope_done, 32)
            for s in range(ITEMS + HEAD_LAG):
                if s < 4 * HEADS:
                    h, b = s // NT, s % NT
                    n = P * (b + 1)
                    if s >= 2:
                        pe.wait_ge(da_e, 2 * (s - 1))
                    for t in range(2):
                        r = slice(64 * t, 64 * t + 64)
                        o = PS[:, 2 * (s % 2) + t, :]
                        mm(o[:, 0:n], DQK[r, h, P * b:P * (b + 1)], DQK[r, HEADS + h, 0:n], start=True, stop=False)
                        last = mm(o[:, n - 64:n], ROWS[:, 0:P], ROWS[:, P:P + 64], start=False, stop=True)
                    last.then_inc(da_s, 1)
                for kind, g in [x for x in (("item", s - 1), ("head", (s - HEAD_LAG) / NT)) if x in turn_no]:
                    g = int(g)
                    no = turn_no[kind, g]
                    if no >= 2:
                        pe.wait_ge(da_wt, no - 1)
                    if kind == "item":
                        pe.wait_ge(da_w, g + 1)
                        for c in range(g % NT + 1):
                            last = turn(PS[:, 4 + no % 2, P * c:P * (c + 1)], DW[:, g % 2, P * c:P * (c + 1)], P)
                    else:
                        pe.wait_ge(da_on, 2 * g + 2)
                        for c in range(NT):
                            last = turn(PS[:, 4 + no % 2, P * c:P * (c + 1)], DON[:, g % 2, c, :], P)
                    last.then_inc(da_t, 1)
                if 2 <= s <= 4 * HEADS + 1:
                    g = s - 2
                    h, b = g // NT, g % NT
                    pe.wait_ge(da_wt, turn_no["item", g] + 1)
                    if b == 0 and h >= 2:
                        pe.wait_ge(da_on, 2 * (h - 2) + 1)
                    for c in range(b + 1):
                        last = mm(PS[:, 6 + h % 2, P * b:P * (b + 1)], DWT[:, g % 2, P * c:P * (c + 1)],
                                  DV[:, c, P * h:P * (h + 1)], start=c == 0, stop=c == b)
                    last.then_inc(da_pv, 1)
            pe.wait_ge(da_wt, len(turns))
            project(j_diff_gate, UH, UL, SEQ_COLS)
            project(j_diff_out, DYH, DYL, PLAIN, k_ready=(yl_done, 16))
            norm_products("post1")

            def ffn_pe(name, number):
                cols = norms[name][2]
                hcols = ALL_COLS if cols == ALL_COLS else PLAIN
                for part, (jg, jd) in enumerate(ffns[name]):
                    project(jg, UH, UL, cols, k_ready=(ul_done, applied[name]))
                    project(jd, HH, HL, hcols, kc=FFN_PARTS[part] // 2,
                            k_ready=(hl_done, 22 * number + (FFN_PARTS[0] if part else 0)))

            norm_products("ffn1")
            ffn_pe("ffn1", 0)

            norm_products("mix")
            project(j_cq, UH, UL, SEQ_COLS, k_ready=(ul_done, applied["mix"]))
            project(j_kvm, UH, UL, ALL_COLS)
            norm_products("cq")
            norm_products("ckv")

            def three(o, wh, wl, xh, xl, first, final):
                mm(o, wh, xh, start=first, stop=False)
                mm(o, wh, xl, start=False, stop=False)
                return mm(o, wl, xh, start=False, stop=final)

            b = j_uq.unit0 % SPLITS
            pe.wait_ge(lo_done, j_uq.unit0 + 1)
            pe.wait_ge(ul_done, applied["cq"] + 2)
            for n, off in enumerate((512, 768, 640, 896, 0, 128, 256, 384)):
                c = j_uq.chunk0 + n
                slot = c % SLOTS
                slot_free(pe, slot, c // SLOTS)
                for k in range(2):
                    w = slice(1024 * k + off, 1024 * k + off + P)
                    last = three(PS[:, 2 * slot, :], WH[:, b, w], WL[:, b, w], CQH[:, k, :], CQL[:, k, :],
                                 k == 0, k == 1)
                last.then_inc(done, 1)
            b = j_ukv.unit0 % SPLITS
            pe.wait_ge(lo_done, j_ukv.unit0 + 1)
            pe.wait_ge(ul_done, applied["ckv"] + 1)
            for n in range(4):
                c = j_ukv.chunk0 + n
                slot = c % SLOTS
                slot_free(pe, slot, c // SLOTS)
                w = slice(P * n, P * (n + 1))
                for a in range(2):
                    x = slice(a * HALF, (a + 1) * HALF)
                    last = three(PS[:, 2 * slot + a, 0:HALF], WH[:, b, w], WL[:, b, w], CKH[:, 0, x], CKL[:, 0, x],
                                 True, True)
                last.then_inc(done, 1)
            for t in range(NT + 1):
                c = j_ukv.chunk0 + 4 + t
                slot = c % SLOTS
                slot_free(pe, slot, c // SLOTS)
                x = slice(0, META) if t == 0 else slice(META + P * (t - 1), META + P * t)
                w = slice(512, 1024)
                o = PS[0:x.stop - x.start, 2 * slot, :]
                mm(o, CKH[:, 0, x], WH[:, b, w], start=True, stop=False)
                mm(o, CKL[:, 0, x], WH[:, b, w], start=False, stop=False)
                mm(o, CKH[:, 0, x], WL[:, b, w], start=False, stop=True).then_inc(done, 1)

            for s, n in enumerate(uses_before(j_ukv.end[1])):
                pe.wait_ge(ps_free[s], n)
            pe.wait_ge(kr_done, 4)
            pe.wait_ge(qr_done, 8)
            pe.wait_ge(s_cmask, 16)
            R = MLA_NOPE + MLA_ROPE
            for s in range(HEADS * NT + MLA_LAG):
                if s < HEADS * NT:
                    h, b = s // NT, s % NT
                    n = META + P * (b + 1)
                    if s >= 2:
                        pe.wait_ge(ma_e, s - 1)
                    k = 2 * (s % 2)
                    q = QC[0:R, h, P * b:P * (b + 1)]
                    if n <= 512:
                        mm(PS[:, k, 0:n], q, KCAT[0:R, h, 0:n], start=True, stop=False)
                        o = PS[:, k, n - P:n]
                    else:
                        mm(PS[:, k, 0:HALF], q, KCAT[0:R, h, 0:HALF])
                        mm(PS[:, k + 1, 0:HALF], q, KCAT[0:R, h, HALF:TOK], start=True, stop=False)
                        o = PS[:, k + 1, HALF - P:HALF]
                    mm(o, IDENT[:, :], CMASK[:, :], start=False, stop=True).then_inc(ma_s, 1)
                for kind, g in mla_step_turns(s):
                    no = mla_turn_no[kind, g]
                    if no >= 2:
                        pe.wait_ge(ma_pt, no - 1)
                    if kind == "item":
                        b = g % NT
                        pe.wait_ge(ma_e, g + 1)
                        for c in range(b + 1):
                            turn(PS[:, 4 + no % 2, P * c:P * (c + 1)], ME[:, g % 2, META + P * c:META + P * (c + 1)], P)
                        if b < NT - 1:
                            o = PS[0:META, 4 + no % 2, P * (b + 1):P * (b + 2)]
                        else:
                            if g >= NT:
                                pe.wait_ge(ma_pt, mla_turn_no["item", g - NT] + 1)
                            o = PS[0:META, 7, 0:P]
                        last = turn(o, ME[:, g % 2, 0:META], P)
                    else:
                        pe.wait_ge(ma_on, 2 * g + 2)
                        for c in range(NT):
                            last = turn(PS[:, 4 + no % 2, P * c:P * (c + 1)], MON[:, g % 2, c, :], P)
                    last.then_inc(ma_t, 1)
                if 2 <= s <= HEADS * NT + 1:
                    g = s - 2
                    h, b = g // NT, g % NT
                    pe.wait_ge(ma_pt, mla_turn_no["item", g] + 1)
                    if b == 0 and h:
                        pe.wait_ge(ma_on, h)
                    o = PS[:, 6, 64 * b:64 * (b + 1)]
                    hv = slice(64 * h, 64 * h + 64)
                    for c in range(b + 1):
                        mm(o, MPT[:, g % 2, P * c:P * (c + 1)], MV[:, 1 + c, hv], start=c == 0, stop=False)
                    mm(o, MPT[0:META, g % 2, P * (b + 1):P * (b + 2)], MV[0:META, 0, hv],
                       start=False, stop=True).then_inc(ma_pv, 1)
            pe.wait_ge(ma_pt, len(mla_turns))
            pe.wait_ge(ma_on, HEADS)
            pe.wait_ge(ma_e, HEADS * NT)
            project(j_gqkv, UH, UL, ALL_COLS)
            project(j_z, UH, UL, SEQ_COLS)
            for s, n in enumerate(uses_before(j_z.end[1])):
                pe.wait_ge(ps_free[s], n)
            pe.wait_ge(s_al, 32)
            mm(PS[:, 1, 0:16], ONES[0:1, :], ALROW[0:1, :])
            for t in range(NT + 1):
                w, cols = tile(t)
                last = nc.tensor.transpose(PS[0:w, 0, 16 * t:16 * t + 16], MISC[64:80, cols], IDENT[64:80, 64:80])
            last.then_inc(g_pe, 1)
            pe.wait_ge(g_dve, N_PRE_DVE)
            pe.wait_ge(s_tri, 16)
            mm(PS[:, 2, 0:32], TRI[:, 0, :], GG[:, 1:NT + 1, :])
            mm(PS[:, 2, 32:64], TRI[:, 1, :], GG[:, 1:NT + 1, :])
            for c in range(2):
                r = slice(64 * c, 64 * c + 64)
                for par in range(2):
                    mm(PS[64 * par:64 * par + 64, 2 + c, 64 + 16 * c:80 + 16 * c], ONES[r, 0:64],
                       GG[r, 1:NT + 1, :].rearrange("p t (h a) -> p t h a", a=2)[:, :, :, par])
            mm(PS[0:META, 2, 96:104], TRI[0:META, 0, 0:META], GG[0:META, 0, :])
            mm(PS[0:META, 2, 104:112], TRI[0:META, 1, 0:META], GG[0:META, 0, :]).then_inc(g_pe, 1)
            pe.wait_ge(gexp_done, 1)
            for t in range(NT + 1):
                w, cols = tile(t)
                if t:
                    pe.wait_ge(g_dve, DVE_AT[t - 1, ("s", 0 if t == 1 else 1)])
                if t > 1:
                    pe.wait_ge(g_dve, DVE_AT[t - 1, "out_norm"])
                for part in range(0 if t else 1, 3):
                    for c in range(4):
                        last = turn(PS[0:w, part, P * c:P * (c + 1)], CVS[:, 4 * part + c, cols], P)
                last.then_inc(g_pe, one("pe", t, "turn_in"))
                pe.wait_ge(g_pool, POOL_AT[t, "ug"])
                pe.wait_ge(g_act, ACT_AT[t, "rows"])
                for b in range(2):
                    last = mm(PS[0:w, b, 0:4 * w], TRI[0:w, 1, 0:w], UG[0:w, 4 * b:4 * b + 4, 0:w])
                last.then_inc(g_pe, one("pe", t, "decay"))
                pe.wait_ge(g_dve, DVE_AT[t, "qg" if t else "nk"])
                for bank, src in ((3, NK), (4, NQ), (5, KB), (6, QG)):
                    if t or bank in (3, 5):
                        for c in range(4):
                            last = turn(PS[:, bank, w * c:w * (c + 1)], src[0:w, P * c:P * (c + 1)], w)
                last.then_inc(g_pe, one("pe", t, "turn_scaled"))
                pe.wait_ge(g_act, ACT_AT[t, "turned"])
                if t > 1:
                    pe.wait_ge(g_dve, DVE_AT[t - 1, "out_gate"])

                def scores(banks, x):
                    for h in range(HEADS):
                        r = slice(64 * (h % 2), 64 * (h % 2) + 64)
                        last = mm(PS[0:w, banks[h % 2], w * (h // 2):w * (h // 2 + 1)], KT[r, h // 2, 0:w], x[r, h // 2, 0:w])
                    return last
                scores((2, 7), KBT).then_inc(g_pe, one("pe", t, "kk"))
                if t:
                    scores((3, 4), QT).then_inc(g_pe, one("pe", t, "kq"))
                pe.wait_ge(g_act, ACT_AT[t, "decay"])
                pe.wait_ge(g_pool, POOL_AT[t, "eye"])
                for n, s in enumerate(levels(t)):
                    for g in range(2):
                        pe.wait_ge(g_dve, DVE_AT[t, ("d", levels(t)[n - 1], g)] if n else DVE_AT[t, "at" if t else "lt"])
                        for h in range(4 * g, 4 * g + 4):
                            last = mm(PS[0:w, g, w * (h % 4):w * (h % 4 + 1)], LT[0:w, h, 0:w], TI[0:w, h, 0:w])
                        last.then_inc(g_pe, one("pe", t, ("x", s, g)))
                    for g in range(2):
                        pe.wait_ge(g_dve, DVE_AT[t, ("x", s, g)])
                        if n:
                            pe.wait_ge(g_dve, DVE_AT[t, ("e", levels(t)[n - 1], g)])
                        for h in range(4 * g, 4 * g + 4):
                            o = slice(w // 2 * (h % 4), w // 2 * (h % 4 + 1))
                            if s != levels(t)[-1]:
                                mm(PS[0:w, (2, 7)[g], o], TIT[0:w, h, 0:w], joined(XX[0:w, h, 0:w], s, 0))
                            last = mm(PS[0:w, 3 + g, o], XX[0:w, h, 0:w], joined(TIT[0:w, h, 0:w], s, 1))
                        last.then_inc(g_pe, one("pe", t, ("y", s, g)))
                pe.wait_ge(g_dve, DVE_AT[t, ("e", levels(t)[-1], 1)])
                for h in range(HEADS):
                    hv = slice(64 * h, 64 * h + 64)
                    last = mm(PS[0:w, 5, hv], TIT[0:w, h, 0:w], ROWQ[0:w, 2, hv])
                    if t:
                        last = mm(PS[64 * (h % 2):64 * (h % 2) + 64, 6, P * (h // 2):P * (h // 2 + 1)], KBG[:, hv], TIT[:, h, :])
                last.then_inc(g_pe, one("pe", t, "uw"))
                for c in range(2 if t else 1):
                    r = slice(64 * c, 64 * c + 64) if t else slice(0, META)
                    old = (2 * (t - 1) + c) % 2
                    pe.wait_ge(g_act, ACT_AT[t, "uw"])
                    if t:
                        pe.wait_ge(g_dve, DVE_AT[t if c else t - 1, ("s", 0 if c or t == 1 else 1)])
                        for h in range(HEADS):
                            d = slice(64 * (h % 2), 64 * (h % 2) + 64)
                            last = mm(PS[r, 3 * (h % 2), GDN_D * (h // 2):GDN_D * (h // 2 + 1)], WTT[d, h // 2, r], ST[d, old, h // 2, :])
                        last.then_inc(g_pe, one("pe", t, ("ws", c)))
                        pe.wait_ge(g_dve, DVE_AT[t, ("vn", c)])
                    x = VN if t else UU
                    for h in range(HEADS):
                        hv = slice(64 * h, 64 * h + 64)
                        last = mm(PS[64 * (h % 2):64 * (h % 2) + 64, 1, GDN_D * (h // 2):GDN_D * (h // 2 + 1)],
                                  KD[r, hv], x[r, hv])
                    last.then_inc(g_pe, one("pe", t, ("state", c)))
                    if t:
                        pe.wait_ge(g_pool, POOL_AT[t, "at"])
                        for h in range(HEADS):
                            d = slice(64 * (h % 2), 64 * (h % 2) + 64)
                            hv = slice(64 * h, 64 * h + 64)
                            mm(PS[r, 4 + h % 2, GDN_D * (h // 2):GDN_D * (h // 2 + 1)], QGT[d, h // 2, r], ST[d, old, h // 2, :])
                            last = mm(PS[r, 2, hv], AT[r, h, r], VN[r, hv])
                        last.then_inc(g_pe, one("pe", t, ("out", c)))
                if t:
                    pe.wait_ge(g_dve, DVE_AT[t, "out_norm"])
                    for c in range(4):
                        last = turn(PS[:, 7, P * c:P * (c + 1)], GON[:, P * c:P * (c + 1)], P)
                    last.then_inc(g_pe, one("pe", t, "turn_out"))
            pe.wait_ge(g_dve, DVE_AT[NT, "out_gate"])
            for n in range(4):
                for q in range(3):
                    u = j_merge.unit0 + 3 * n + q
                    b = u % SPLITS
                    pe.wait_ge(lo_done, u + 1)
                    if q == 2 and n == 0:
                        pe.wait_ge(ol_done, 4)
                        pe.wait_ge(gl_done, 4)
                    if q < 2:
                        todo = [(range(KC), m, UH, UL, SEQ_COLS) for m in range(2)]
                    else:
                        todo = [(range(4 * br, 4 * br + 4), m, (OMH, GOH)[br], (OML, GOL)[br], PLAIN)
                                for m in range(2) for br in range(2)]
                    for i, (ks, m, xh, xl, cols) in enumerate(todo):
                        c = j_merge.chunk0 + 8 * n + 2 * q + i
                        slot = c % SLOTS
                        slot_free(pe, slot, c // SLOTS)
                        for k in ks:
                            w = slice(k * UCOL + m * P, k * UCOL + (m + 1) * P)
                            x = k - ks[0]
                            last = three(acc(slot, SEQ), WH[:, b, w], WL[:, b, w], xh[:, x, cols], xl[:, x, cols],
                                         k == ks[0], k == ks[-1])
                        last.then_inc(done, 1)
            project(j_wout, MH, ML, PLAIN, k_ready=(ml_done, 0))
            norm_products("ffn2")
            ffn_pe("ffn2", 1)
            norm_products("final")
            pe.wait_ge(f_done, KC)
            for t in range(NT):
                c = at_rows[1] + t
                slot_free(pe, c % SLOTS, c // SLOTS)
                for k in range(KC):
                    last = turn(PS[:, 2 * (c % SLOTS) + k // 4, P * (k % 4):P * (k % 4 + 1)], FN[:, k, P * t:P * (t + 1)], P)
                last.then_inc(done, 1)


INPUTS = [
    "x", "pre_norm", "post_norm", "w_in_a", "w_out_a", "kv_norm", "w_kv", "w_in_b", "lam_q1", "lam_k1", "lam_q2",
    "lam_k2", "sub_norm_b", "w_out_b", "meta_tokens_2", "ffn1_norm_2", "ffn1_w_gate_2", "ffn1_w_up_2",
    "ffn1_w_down_2", "mix_norm_2", "w_in_2", "q_norm_2", "w_uq_2", "kv_norm_2", "w_ukv_2", "w_mla_o_2",
    "conv_w_2", "a_log_2", "dt_bias_2", "gdn_norm_2", "w_gdn_o_2", "w_out_2", "ffn2_norm_2", "ffn2_w_gate_2",
    "ffn2_w_up_2", "ffn2_w_down_2", "final_norm_2",
]

GAIN_ROWS = [("pre_norm", 0), ("post_norm", 0), ("kv_norm", None), ("pre_norm", 1), ("post_norm", 1),
             ("ffn1_norm_2", 0), ("mix_norm_2", 0), ("ffn2_norm_2", 0), ("final_norm_2", None)]

SUB_ROW, GDN_ROW, QN_ROW, KVN_ROW, CONV_ROW = 72, 73, 74, 76, 77
N_ROWS = 125


def other_rows(A):
    return [(SUB_ROW, A["sub_norm_b"]), (GDN_ROW, A["gdn_norm_2"]),
            (QN_ROW, A["q_norm_2"].rearrange("a (c p) -> (a c) p", p=P)), (KVN_ROW, A["kv_norm_2"]),
            (CONV_ROW, A["conv_w_2"][0].rearrange("t (c p) -> (t c) p", p=P))]


def kernel(**inputs):
    from concourse import bacc
    from concourse.bass_utils import run_bass_kernel_spmd

    nc = bacc.Bacc("TRN2", target_bir_lowering=False, num_devices=1)
    arrays, A = {}, {}
    for name in INPUTS:
        a = np.ascontiguousarray(inputs[name])
        arrays[f"in_{name}"] = a
        A[name] = nc.dram_tensor(f"in_{name}", a.shape, mybir.dt.from_np(a.dtype), kind="ExternalInput").ap()
    out = nc.dram_tensor("out", (1, SEQ, D), F32, kind="ExternalOutput").ap()
    build(nc, A, out)
    r = run_bass_kernel_spmd(nc, [arrays], core_ids=[0])
    return r.results[0]["out"]
```

```python
from contextlib import ExitStack

import numpy as np

import concourse.bass as bass
from concourse import mybir

F32 = mybir.dt.float32
F32R = mybir.dt.float32r
ALU = mybir.AluOpType
ACT = mybir.ActivationFunctionType
AX = mybir.AxisListType

P = 128
D = 1024
KC = D // P
SEQ = 512
META = 16
TOK = META + SEQ
HALF = TOK // 2
NT = SEQ // P
EPS = 1e-6
NEG = -float(2.0 ** 100)
HEADS = 8
RET_DK, RET_DV = 128, 256
DIFF_DH = 64
LAMBDA_INIT = 0.8 - 0.6 * float(np.exp(-0.3))
FFN = 2816
MLA_Q_RANK, MLA_KV_RANK = 256, 128
MLA_NOPE, MLA_ROPE, MLA_V = 64, 32, 64
GDN_D = 64
GDN_WIDTH = HEADS * GDN_D
CONV = 4
FFN_PARTS = (12, 10)

UCOL = 256
UNIT = KC * UCOL
RAWS = 4
SPLITS = 2
SLOTS = 4


def rope_tables(half, reps, positions):
    inv = (np.float32(10000.0) ** (-np.arange(half, dtype=np.float32) / np.float32(half))).astype(np.float32)
    ang = (np.arange(positions, dtype=np.float32)[:, None] * inv[None, :]).astype(np.float32)
    cos = np.cos(ang.astype(np.float64)).T
    sin = np.sin(ang.astype(np.float64)).T
    c = np.concatenate([cos, cos] * reps, axis=0)
    s = np.concatenate([-sin, sin] * reps, axis=0)
    return np.ascontiguousarray(np.stack([c, s], axis=1)).astype(np.float32)


def retention_decay():
    j = np.arange(P)[:, None]
    c = np.arange(SEQ)[None, :]
    out = np.zeros((HEADS, P, SEQ), np.float64)
    for h in range(HEADS):
        out[h] = np.where(c >= j, np.exp(np.log1p(-2.0 ** (-5.0 - h)) * (c - j)), 0.0) * RET_DK ** -0.5
    return out.astype(np.float32)


def chunk_masks():
    r, c = np.arange(P)[:, None], np.arange(P)[None, :]
    same = r // 64 == c // 64
    masks = [same & (r <= c), same & (r > c), (c == r + 1) & (r % 2 == 0)]
    for s in (2, 4, 8, 16, 32):
        masks.append((r // (2 * s) == c // (2 * s)) & (r // s % 2 == 1) & (c // s % 2 == 0))
    return np.ascontiguousarray(np.stack(masks, axis=1)).astype(np.float32)




class Job:

    def __init__(self, units, at, fold=1, loop=True, chunks=None, kc=KC):
        self.units, self.fold, self.size = units, fold, kc * UCOL
        self.unit0, self.chunk0, self.tick0 = at
        self.turns = units // 4 if loop and units >= 8 else 0
        self.end = (self.unit0 + units, self.chunk0 + (chunks or 2 * units // fold), self.tick0 + (chunks or 2 * units))


def build(nc, A, out):
    ctx = ExitStack()
    with ctx:
        def sem(name):
            return ctx.enter_context(nc.semaphore(name))

        FIRST, LAST = 16512, 229344
        ends, starts = {None: FIRST}, {}

        def place(name, shape, after, dt=F32, over=None):
            size = (int(np.prod(shape[1:])) * 4 + 31) // 32 * 32
            at = ends[after] if over is None else starts[over]
            assert at + size <= LAST, (name, at + size - LAST)
            starts[name], ends[name] = at, at + size
            return nc.alloc_sbuf_tensor_at(name, list(shape), dt, offset=at)

        RES = place("residual", [P, KC, TOK], None)
        UH = place("u_hi", [P, KC, TOK], "residual", F32R)
        UL = place("u_lo", [P, KC, TOK], "u_hi", F32R)
        RAW = place("w_raw", [P, RAWS, UNIT], "u_lo")
        WH = place("w_hi", [P, SPLITS, UNIT], "w_raw", F32R)
        WL = place("w_lo", [P, SPLITS, UNIT], "w_hi", F32R)
        IDENT = place("ident", [P, P], "w_lo")
        ONES = place("ones", [P, P], "ident")
        SUMSQ = place("sumsq", [P, TOK], "ones")
        SQ = place("sq", [P, 2, TOK], "sumsq")
        TMP = place("tmp", [P, 2, TOK], "sq")
        SG = place("sg", [P, 2, TOK], "tmp")
        DIAG = place("diag", [P, TOK], None, over="sg")
        GAINS = place("gains", [P, P], "sg")
        GROW = place("gain_rows", [P, P], None, over="tmp")
        STAT = place("stat", [P, 3, 8], "gains")
        BN6 = place("bn6", [P, NT, 6], "stat")
        BNA = place("bn_mv", [P, NT, 2], "bn6")
        VEPS = place("var_eps", [P, 8], "bn_mv")
        RSTD = place("rstd", [P, 8], "var_eps")
        MHALF = place("minus_half", [P, 8], "rstd")
        LAMS = place("lam_cols", [P, 8], "minus_half")
        LAMV = place("lam_vectors", [1, 4, 64], "lam_cols")
        NEGM2 = place("neg_max2", [P, 8], "lam_vectors")
        ESUM2 = place("exp_sum2", [P, 4, NT], "neg_max2")
        RSUM2 = place("inv_sum2", [P, 4, NT], "exp_sum2")
        SEL = place("head_rows", [P, 8], "inv_sum2")
        ROWS = place("mask_rows", [1, 256], "head_rows")
        arena = "mask_rows"

        QK = place("ret_qk", [P, 2 * HEADS, SEQ], arena)
        V = place("ret_v", [P, NT, HEADS * RET_DV], "ret_qk")
        SC = place("ret_scores", [P, 2, 1280], "ret_v")
        TAB = place("ret_rope", [P, 2, SEQ], None, over="ret_scores")
        DECAY = place("ret_decay", [P, 2, SEQ], None, over="sg")
        ON = place("ret_norm", [P, 2, NT, RET_DV], None, over="sq")
        assert ends["ret_norm"] <= ends["tmp"]
        X0 = place("x_rows", [P, NT, D], None, over="ret_v")
        M0 = place("meta_rows", [META, D], "x_rows")
        YL = place("ret_y_lo", [P, 2 * HEADS, SEQ], None, F32R, over="ret_qk")
        YH = place("ret_y_hi", [P, 2 * HEADS, SEQ], None, F32R, over="ret_v")
        Y2 = place("proj_out", [P, KC, SEQ], None, over="u_hi")

        DQK = place("diff_qk", [P, 2 * HEADS, SEQ], arena)
        DYL = place("diff_y_lo", [P, HEADS, SEQ], None, F32R, over="diff_qk")
        DYH = place("diff_y_hi", [P, HEADS, SEQ], "diff_y_lo", F32R)
        DV = place("diff_v", [P, NT, D], "diff_qk")
        RB = place("inv_rms", [P, SEQ], "diff_v")
        DTAB = place("diff_rope", [P, 2, SEQ], "inv_rms")
        DE = place("diff_exp", [P, 2, 2, SEQ], "diff_rope")
        DW = place("diff_w", [P, 2, SEQ], "diff_exp")
        DWT = place("diff_wt", [P, 2, SEQ], "diff_w")
        DON = place("diff_norm", [P, 2, NT, P], "diff_wt")
        NEGM = place("neg_max", [P, 2, 2], "diff_norm")
        ESUM = place("exp_sum", [P, 2, 2], "neg_max")
        RSUM = place("inv_sum", [P, 2, NT, 2], "exp_sum")
        COEF = place("coef", [P, 2], "inv_sum")
        SSQ = place("ssq", [P, NT], "coef")
        DSQ = place("diff_sq", [P, NT, P], None, over="sq")

        HH = place("hidden_hi", [P, FFN_PARTS[0], TOK], arena, F32R)
        HL = place("hidden_lo", [P, FFN_PARTS[0], TOK], "hidden_hi", F32R)

        MISC = place("mix_misc", [P, TOK], arena)
        OMF = place("mla_out", [P, 4, SEQ], "mix_misc")
        MPT = place("mla_pt", [P, 2, 640], "mla_out")
        ME = place("mla_exp", [P, 3, TOK], "mla_pt")
        MON = place("mla_norm", [P, 2, NT, P], "mla_exp")
        CQF = place("cq", [P, 2, SEQ], "mix_misc")
        CQH = place("cq_hi", [P, 2, SEQ], "cq", F32R)
        CQL = place("cq_lo", [P, 2, SEQ], "cq_hi", F32R)
        CKF = place("ckv", [P, 1, TOK], "cq_lo")
        CKH = place("ckv_hi", [P, 1, TOK], "ckv", F32R)
        CKL = place("ckv_lo", [P, 1, TOK], "ckv_hi", F32R)
        MTAB = place("mla_rope", [P, 2, TOK], "ckv_lo")
        assert ends["mla_rope"] <= ends["mla_norm"]
        QC = place("mla_q", [P, HEADS, SEQ], "mla_norm")
        KCAT = place("mla_k", [P, HEADS, TOK], "mla_q")
        MV = place("mla_v", [P, NT + 1, SEQ], "mla_k")
        CMASK = place("causal", [P, P], "mla_v")

        CVS = place("gdn_conv", [P, 12, TOK], "mla_out")
        ZS = place("gdn_gate", [P, 4, SEQ], "gdn_conv")
        ROWQ = place("gdn_rows", [P, 3, GDN_WIDTH], "gdn_gate")
        NQ = place("gdn_nq", [P, GDN_WIDTH], "gdn_rows")
        NK = place("gdn_nk", [P, GDN_WIDTH], "gdn_nq")
        KT = place("gdn_kt", [P, 4, P], "gdn_nk")
        QT = place("gdn_qt", [P, 4, P], "gdn_kt")
        KBT = place("gdn_kbt", [P, 4, P], "gdn_qt")
        KB = place("gdn_kb", [P, GDN_WIDTH], "gdn_kbt")
        QGT = place("gdn_qgt", [P, 4, P], "gdn_kb")
        KBG = place("gdn_kbg", [P, GDN_WIDTH], "gdn_qgt")
        KD = place("gdn_kd", [P, GDN_WIDTH], "gdn_kbg")
        QG = place("gdn_qg", [P, GDN_WIDTH], "gdn_kd")
        DEC = place("gdn_dec", [P, HEADS, P], "gdn_qg")
        SMALL = place("gdn_small", [P, 640], "gdn_dec")
        PRE = place("gdn_pre", [P, 2, TOK + 8], None, over="gdn_kt")
        GSQ = place("gdn_sq", [P, 2, GDN_WIDTH], None, over="gdn_dec")
        GON = place("gdn_on", [P, GDN_WIDTH], None, over="gdn_dec")
        TI = place("gdn_inv", [P, HEADS, P], None, over="gdn_kt")
        TIT = place("gdn_inv_t", [P, HEADS, P], None, over="gdn_kbt")
        XX = place("gdn_x", [P, HEADS, P], None, over="gdn_rows")
        UU = place("gdn_u", [P, GDN_WIDTH], None, over="gdn_nq")
        VN = place("gdn_vn", [P, GDN_WIDTH], None, over="gdn_nk")
        WTT = place("gdn_wt", [P, 4, P], None, over="gdn_qg")
        LT = place("gdn_lt", [P, HEADS, P], None, over="tmp")
        AT = place("gdn_at", [P, HEADS, P], "gdn_lt")
        assert ends["gdn_at"] <= ends["sg"]
        UG = place("gdn_ug", [P, HEADS, P], None, over="gdn_lt")
        TRI = place("gdn_tri", [P, HEADS, P], None, over="sumsq")
        SS = place("gdn_ss", [P, 4, GDN_D], "gdn_tri")
        FACT = place("gdn_factors", [P, 5 * HEADS * (NT + 1)], "gdn_ss")
        assert ends["gdn_factors"] <= ends["sq"]
        ST = place("gdn_state", [P, 2, 4, GDN_D], None, over="mix_misc")

        OML = place("mla_out_lo", [P, 4, SEQ], None, F32R, over="mla_out")
        MH = place("merged_hi", [P, KC, SEQ], None, F32R, over="gdn_conv")
        OMH = place("mla_out_hi", [P, 4, SEQ], "merged_hi", F32R)
        assert ends["mla_out_hi"] <= ends["gdn_conv"]
        GOL = place("gdn_out_lo", [P, 4, SEQ], None, F32R, over="gdn_gate")
        ML = place("merged_lo", [P, KC, SEQ], "gdn_gate", F32R)
        GOH = place("gdn_out_hi", [P, 4, SEQ], "merged_lo", F32R)
        GATE = place("branch_gates", [P, 2, 2, SEQ], "gdn_out_hi")

        FN = place("final_normed", [P, KC, SEQ], arena)
        OUTR = place("out_rows", [P, NT, D], "final_normed")

        PS = ctx.enter_context(nc.psum_tensor("ps", [P, 8, 512], F32))

        s_ident, s_ones, s_x, s_meta, s_gain, s_tab = [
            sem(n) for n in ("ident_in", "ones_set", "x_in", "meta_in", "gain_in", "rope_in")]
        raw_in = [sem(f"raw_in{i}") for i in range(RAWS)]
        hi_done, lo_done = sem("w_hi_done"), sem("w_lo_done")
        done = sem("pe_done")
        ps_free = [sem(f"ps_free{i}") for i in range(SLOTS)]
        sq_done, sq_added = sem("sq_done"), sem("sq_added")
        ms_done, root_done, diag_done = [
            sem(n) for n in ("mean_square", "root_done", "diag_done")]
        sum_zeroed = sem("sum_zeroed")
        t_done, uh_done, ul_done = sem("scaled_done"), sem("u_hi_done"), sem("u_lo_done")
        post_t, res_done = sem("post_scaled"), sem("residual_done")
        shift_done, sin_done, rope_done = sem("shift_done"), sem("sin_done"), sem("rope_done")
        dec_in = [sem(f"decay_in{i}") for i in range(2)]
        ra_s, ra_m, ra_pv, ra_bn, ra_ve, ra_rs, ra_on, ra_t, ra_e = [sem(n) for n in (
            "ret_scored", "ret_masked", "ret_pv", "ret_stats", "ret_vareps", "ret_rstd", "ret_normed",
            "ret_turned", "ret_out")]
        y_done, yh_done, yl_done = sem("y_done"), sem("y_hi_done"), sem("y_lo_done")
        s_half, s_rows, s_lamv, lam_step, lam_exp = [
            sem(n) for n in ("half_set", "rows_set", "lam_in", "lam_step", "lam_exp")]
        s_dtab, rb_done = sem("diff_rope_in"), sem("inv_rms_kept")
        da_s, da_max, da_e, da_c, da_w, da_t, da_wt, da_pv, da_sq, da_ve, da_rs, da_on = [sem(n) for n in (
            "diff_scored", "diff_max", "diff_exp_done", "diff_coef", "diff_w_done", "diff_w_turned", "diff_wt_out",
            "diff_pv", "diff_sq_done", "diff_vareps", "diff_rstd", "diff_normed")]
        s_mtab, kr_done, s_cmask = sem("mla_rope_in"), sem("key_rope"), sem("causal_in")
        qr_done = sem("query_rope")
        ma_s, ma_max, ma_e, ma_t, ma_pt, ma_pv, ma_rs, ma_on = [sem(n) for n in (
            "mla_scored", "mla_max", "mla_exp_done", "mla_turned", "mla_turned_out", "mla_pv", "mla_inv_sum",
            "mla_normed")]
        s_tri, s_al, z_done = sem("tri_in"), sem("gdn_vectors_in"), sem("gdn_gate_done")
        pre_zero, pre_in, tap_done, conv_done = [sem(n) for n in ("pre_zeroed", "pre_in", "tap_done", "conv_done")]
        sp_done = sem("softplus_done")
        gexp_done = sem("gdn_exp_done")
        s_sel, gsq_done, ss_done, rn_done = [sem(n) for n in (
            "head_rows_set", "gdn_squares", "gdn_sums", "gdn_inverse_norms")]
        ss_mm = sem("gdn_summed")
        fac_done = sem("gdn_factors_done")
        ba_zero = sem("ba_zeroed")
        g_pe, g_act, g_dve, g_pool = [sem(f"gdn_{n}") for n in ("pe", "act", "dve", "pool")]
        oh_done, ol_done, gh_done, gl_done = [sem(n) for n in (
            "mla_hi_done", "mla_lo_done", "gdn_hi_done", "gdn_lo_done")]
        merged_done, mh_done, ml_done, f_done, kept_done = [sem(n) for n in (
            "merged", "merged_hi_done", "merged_lo_done", "final_scaled", "rows_kept")]
        hh_done, hl_done = sem("hidden_hi_done"), sem("hidden_lo_done")
        s_out = sem("out_stored")

        c_ident = nc.inline_tensor(np.eye(P, dtype=np.float32), "c_ident").ap()
        c_rope_ret = nc.inline_tensor(rope_tables(RET_DK // 2, 1, SEQ), "c_rope_ret").ap()
        c_rope_diff = nc.inline_tensor(rope_tables(DIFF_DH // 2, 2, SEQ), "c_rope_diff").ap()
        c_rope_mla = nc.inline_tensor(rope_tables(MLA_ROPE // 2, 4, TOK), "c_rope_mla").ap()
        c_causal = nc.inline_tensor(np.where(np.arange(P)[None, :] > np.arange(P)[:, None], np.float32(NEG),
                                             np.float32(0.0)).astype(np.float32), "c_causal").ap()
        c_tri = nc.inline_tensor(chunk_masks(), "c_tri").ap()
        c_decay = nc.inline_tensor(retention_decay(), "c_decay").ap()

        at = [0, 0, 0]

        jobs = []

        def job(units, **kw):
            j = Job(units, tuple(at), **kw)
            at[:] = j.end
            jobs.append(j)
            return j

        def size_of(u):
            return next(j.size for j in jobs if j.unit0 <= u < j.unit0 + j.units)

        def size_after(jb, i, j):
            if isinstance(i, int):
                return size_of(jb.unit0 + 4 * i + j + 1)
            return jb.size if j < 3 else max(jb.size, size_of(jb.unit0 + jb.units))

        def chunks(n):
            c = tuple(at)
            at[1] += n
            at[2] += n
            return c

        at_x = chunks(9)
        at_norm0 = chunks(2)
        j_ret_qk, j_ret_v, j_ret_gate = job(8), job(8), job(8)
        j_ret_out = job(8, fold=2)
        at_post0 = chunks(2)
        at_norm1 = chunks(2)
        j_kv_k, j_kv_v, j_diff_q = job(4), job(4), job(4)
        at_lam = chunks(1)
        j_diff_gate, j_diff_out = job(4), job(4)
        at_post1 = chunks(2)
        ffns = {}

        def ffn_jobs(name, last):
            ffns[name] = []
            for n, part in enumerate(FFN_PARTS):
                ffns[name].append((job(part), job(8, fold=2, loop=not (last and n), kc=part // 2)))

        at_ffn1 = chunks(2)
        ffn_jobs("ffn1", False)
        at_mix = chunks(2)
        j_cq, j_kvm = job(1), job(1)
        at_cq, at_ckv = chunks(2), chunks(2)
        j_uq, j_ukv = job(1, chunks=8), job(1, chunks=9)
        j_gqkv = job(6, loop=False)
        at_gss = (at[0], at[1])
        at[1] += 1
        j_z = job(2)
        j_merge = job(12, loop=False, chunks=32)
        j_wout = job(4)
        at_ffn2 = chunks(2)
        ffn_jobs("ffn2", True)
        at_final = chunks(2)
        at_rows = chunks(NT)
        n_units = at[0]

        w_in_a = A["w_in_a"][0].rearrange("(c p) n -> p c n", p=P)
        w_out_a = A["w_out_a"][0].rearrange("(c p) n -> p c n", p=P)
        w_kv = A["w_kv"].rearrange("(c p) n -> p c n", p=P)
        w_in_b = A["w_in_b"][0].rearrange("(c p) n -> p c n", p=P)
        w_out_b = A["w_out_b"][0].rearrange("(c p) n -> p c n", p=P)
        w_in = A["w_in_2"][0].rearrange("(c p) n -> p c n", p=P)
        w_uq = A["w_uq_2"][0].rearrange("(c p) (h n) -> p c h n", p=P, h=HEADS)
        w_ukv = A["w_ukv_2"][0].rearrange("p (h n) -> p h n", h=HEADS)
        w_mla_o = A["w_mla_o_2"][0].rearrange("(c p) n -> p c n", p=P)
        w_gdn_o = A["w_gdn_o_2"][0].rearrange("(c p) n -> p c n", p=P)
        w_out2 = A["w_out_2"][0].rearrange("(c p) n -> p c n", p=P)
        w_ffn = {f"ffn{n}": [A[f"ffn{n}_w_{k}_2"][0].rearrange("(c p) n -> p c n", p=P) for k in ("gate", "up", "down")]
                 for n in (1, 2)}

        def each(eng, jb, body, peel=0):
            for u in range(4 * peel if jb.turns else 0):
                body(u // 4, u % 4)
            if jb.turns > peel:
                with eng.Fori(peel, jb.turns) as i:
                    for j in range(4):
                        body(i, j)
            for u in range(4 * jb.turns, jb.units):
                body(u // 4, u % 4)

        def wait(eng, semaphore, value):
            if not isinstance(value, int) or value > 0:
                eng.wait_ge(semaphore, value)

        def chunk_of(jb, i, j, m):
            c = jb.chunk0 + 2 * (j // jb.fold) + m
            return c % SLOTS, c // SLOTS + 2 // jb.fold * i

        def tick_of(jb, i, j, m):
            return jb.tick0 + 8 * i + 2 * j + m + 1

        def slot_free(eng, slot, uses):
            if not isinstance(uses, int) or uses:
                eng.wait_ge(ps_free[slot], uses)

        def acc(slot, width):
            return PS[:, 2 * slot, 0:width] if width <= 512 else PS[:, 2 * slot:2 * slot + 2, 0:width // 2]

        def halves(ap):
            return ap.rearrange("p (a n) -> p a n", a=2) if ap.shape[-1] > 512 else ap

        def token_tiles(width):
            return (4, 128) if width == SEQ else (6, 88)

        SEQ_COLS, ALL_COLS, PLAIN = slice(META, TOK), slice(0, TOK), slice(0, SEQ)

        norms = {}

        def norm(name, at_norm, cols, squares=KC, features=D):
            before = sum(x[4] for x in norms.values())
            norms[name] = (len(norms), at_norm, cols, before, squares, features)

        norm("norm0", at_norm0, SEQ_COLS)
        norm("post0", at_post0, SEQ_COLS)
        applied = {"norm0": 0, "norm1": 8, "norm1q": 16, "ffn1": 24, "mix": 32, "cq": 40, "ckv": 42, "ffn2": 43,
                   "final": 51}
        norm("norm1", at_norm1, SEQ_COLS)
        norm("post1", at_post1, SEQ_COLS)
        norm("ffn1", at_ffn1, ALL_COLS)
        norm("mix", at_mix, ALL_COLS)
        norm("cq", at_cq, PLAIN, 2, MLA_Q_RANK)
        norm("ckv", at_ckv, ALL_COLS, 2, MLA_KV_RANK)
        norm("ffn2", at_ffn2, SEQ_COLS)
        norm("final", at_final, SEQ_COLS)

        BY_CHUNK = ("norm1", "ffn1")
        norms["norm1q"] = norms.get("norm1")

        several = {j_kvm.unit0: 3, j_uq.unit0: 7, j_ukv.unit0: 1}
        several.update({j_merge.unit0 + 3 * n + 2: 1 for n in range(4)})

        def extra_loads(u):
            return sum(n for v, n in several.items() if v <= u and v % RAWS == u % RAWS)

        def uses_before(chunk):
            return [len([c for c in range(chunk) if c % SLOTS == s]) for s in range(SLOTS)]

        MLA_LAG = 2 * NT + 5
        mla_turns = []
        for s in range(HEADS * NT + MLA_LAG):
            if 2 <= s <= HEADS * NT + 1:
                mla_turns.append(("item", s - 2))
            if s >= MLA_LAG and (s - MLA_LAG) % (2 * NT) == 0 and (s - MLA_LAG) // (2 * NT) < HEADS // 2:
                mla_turns.append(("pair", (s - MLA_LAG) // (2 * NT)))
        mla_turn_no = {what: n for n, what in enumerate(mla_turns)}

        def mla_step_turns(s):
            found = [("item", s - 2)] if ("item", s - 2) in mla_turn_no else []
            if s >= MLA_LAG and (s - MLA_LAG) % (2 * NT) == 0 and ("pair", (s - MLA_LAG) // (2 * NT)) in mla_turn_no:
                found.append(("pair", (s - MLA_LAG) // (2 * NT)))
            return found

        def levels(t):
            return [2, 4, 8] if t == 0 else [2, 4, 8, 16, 32]

        pe_steps, act_steps, dve_steps, pool_steps = [(0, "turn_in")], [(0, "rows")], [], [(0, "ug")]
        for t in range(NT + 1):
            full = t > 0
            lev = [(kind, n, g) for n in levels(t) for kind in ("x", "y") for g in range(2)]
            pe_steps += [(t, n) for n in ["decay", "turn_k"] + ["turn_q"] * full + ["kk"] + ["kq"] * full + ["d1"] + lev + ["uw"]]
            pe_steps += [(t, (n, c)) for c in range(1 + full) for n in ["ws"] * full + ["state"] + ["out"] * full]
            pe_steps += [(t + 1, "turn_in")] * (t < NT) + [(t, "turn_out")] * full
            act_steps += [(t, n) for n in ["decay", "turned_k", "d1", "uw"] + ["out_square"] * full]
            act_steps += [(t + 1, "rows")] * (t < NT)
            pool_steps += [(t, n) for n in ["kbg", "kd", "vb"] + ["at"] * full]
            pool_steps += [(t + 1, "ug")] * (t < NT) + [(t, "out_rnorm")] * full
            if t == 0:
                dve_steps += [(t, n) for n in ("kb", "nk")]
            dve_steps += [(t, n) for n in ["turned_q"] * full + ["lt", "e1a", "e1b"] + ["at"] * full]
            dve_steps += [(t, n) for s in levels(t) for n in [("x", s, 0), ("x", s, 1)]
                          + [(kind, s, g) for g in range(2) for kind in ["d"] * (s != levels(t)[-1]) + ["e"]]]
            dve_steps += [(t, (n, c)) for c in range(1 + full) for n in ["vn", "sd"] * full + ["s"]]
            dve_steps += [(t, n) for n in [("out_inter", 0), ("out_inter", 1), "out_join", "out_sum", "out_eps"] * full]
            dve_steps += [(t + 1, n) for n in ("kb", "nk", "nq", "qg")] * (t < NT)
            dve_steps += [(t, n) for n in ["out_norm", "out_gate"] * full]
        N_PRE_PE, N_PRE_ACT, N_PRE_DVE = 2, 5, 7
        N_FACTORS = 8
        PE_AT = {key: n + 1 + N_PRE_PE for n, key in enumerate(pe_steps)}
        ACT_AT = {key: n + 1 + N_PRE_ACT for n, key in enumerate(act_steps)}
        DVE_AT = {key: n + 1 + N_PRE_DVE for n, key in enumerate(dve_steps)}
        POOL_AT = {key: n + 1 for n, key in enumerate(pool_steps)}
        progress = {"pe": list(pe_steps), "act": list(act_steps), "dve": list(dve_steps), "pool": list(pool_steps)}

        def one(eng, t, name):
            assert progress[eng].pop(0) == (t, name), (eng, t, name)
            return 1

        def tile(t):
            return (META, slice(0, META)) if t == 0 else (P, slice(META + P * (t - 1), META + P * t))

        BA = SMALL[:, 0:80].rearrange("p (t n) -> p t n", t=NT + 1)
        BETA = SMALL[:, 80:120].rearrange("p (t n) -> p t n", t=NT + 1)
        GG = SMALL[:, 120:160].rearrange("p (t n) -> p t n", t=NT + 1)
        GEXP = SMALL[:, 160:272]
        XA = SMALL[:, 272:312].rearrange("p (t n) -> p t n", t=NT + 1)
        RELU = SMALL[:, 312:352].rearrange("p (t n) -> p t n", t=NT + 1)
        EN = SMALL[:, 352:392].rearrange("p (t n) -> p t n", t=NT + 1)
        EAL = SMALL[:, 392:400]
        ALROW = SMALL[0:1, 400:416]
        RN = SMALL[:, 416:496].rearrange("p (t n) -> p t n", t=NT + 1)
        FQ, FQG, FKB, FKBG, FKD = [FACT[:, 40 * n:40 * n + 40].rearrange("p (t n) -> p t n", t=NT + 1) for n in range(5)]
        LNE = SMALL[:, 496:536].rearrange("p (t n) -> p t n", t=NT + 1)
        OSS, ORN = SMALL[:, 536:544], SMALL[:, 544:552]

        def over_heads(ap, w, n):
            return ap.unsqueeze(2).to_broadcast([w, HEADS, n])

        def by_head(ap):
            return ap.rearrange("p (h n) -> p h n", h=HEADS)

        def every_other(ap, which):
            return ap.rearrange("p (h a) c -> p h a c", a=2)[:, :, which, :]

        def joined(ap, size, which):
            if len(ap.shape) == 2:
                return ap.rearrange("p (b a s) -> p b a s", a=2, s=size)[:, :, which, :]
            return ap.rearrange("p h (b a s) -> p h b a s", a=2, s=size)[:, :, :, which, :]

        OFF = [0, 512, 896, 1152]
        SCORE_AT = [(0, 0), (1, 0), (2, 0), (1, 384)]

        ITEMS, HEAD_LAG = HEADS * NT, 10
        turns = []
        for s in range(ITEMS + HEAD_LAG):
            if 2 <= s <= ITEMS + 1:
                turns.append(("item", s - 2))
            if s >= HEAD_LAG and (s - HEAD_LAG) % NT == 0 and (s - HEAD_LAG) // NT < HEADS:
                turns.append(("head", (s - HEAD_LAG) // NT))
        turn_no = {what: n for n, what in enumerate(turns)}

        def width_of(cols):
            return cols.stop - cols.start

        block = ctx.enter_context(nc.Block())

        @block.sync
        def _(sp):
            sp.dma_start(IDENT[:, :], c_ident).then_inc(s_ident, 16)
            sp.dma_start(X0[:, :, :], A["x"][0].rearrange("(t p) n -> p t n", p=P)).then_inc(s_x, 16)
            sp.dma_start(M0[:, :], A["meta_tokens_2"]).then_inc(s_meta, 16)
            for g, (name, row) in enumerate(GAIN_ROWS):
                src = A[name] if row is None else A[name][row]
                sp.dma_start(GROW[g * KC:(g + 1) * KC, :], src.rearrange("(c p) -> c p", p=P)).then_inc(s_gain, 16)
            for row, src in other_rows(A):
                sp.dma_start(GROW[row:row + src.shape[0], 0:src.shape[1]], src).then_inc(s_gain, 16)
            gdn_gain = A["gdn_norm_2"]
            sp.dma_start(GROW[GDN_ROW:GDN_ROW + 1, 64:128], gdn_gain).then_inc(s_gain, 16)
            sp.dma_start(TAB[:, :, :], c_rope_ret).then_inc(s_tab, 16)
            for n, name in enumerate(("lam_q1", "lam_q2", "lam_k1", "lam_k2")):
                sp.dma_start(LAMV[:, n, :], A[name]).then_inc(s_lamv, 16)

            def load(jb, src):
                def body(i, j):
                    u = jb.unit0 + j
                    need = u - RAWS + 1 + 4 * i
                    if not isinstance(need, int) or need > 0:
                        sp.wait_ge(lo_done, need)
                    src(i, j, RAW[:, u % RAWS, :], raw_in[u % RAWS])
                if jb.unit0:
                    each(sp, jb, body)
                else:
                    for u in range(jb.units):
                        body(u // 4, u % 4)

            def cols(w, first):
                def f(i, j, dst, s):
                    sp.dma_start(dst.rearrange("p (c n) -> p c n", c=KC),
                                 w[:, :, bass.ds(4 * UCOL * i + (first + j * UCOL), UCOL)]).then_inc(s, 16)
                return f

            def folded(w, first, kc):
                def f(i, j, dst, s):
                    a = first + (j % 2) * kc
                    sp.dma_start(dst[:, 0:kc * UCOL].rearrange("p (c n) -> p c n", c=kc),
                                 w[:, a:a + kc, bass.ds(2 * UCOL * i + (j // 2) * UCOL, UCOL)]).then_inc(s, 16)
                return f

            load(j_ret_qk, cols(w_in_a, 0))
            load(j_ret_v, cols(w_in_a, 2 * HEADS * RET_DK))
            load(j_ret_gate, cols(w_in_a, 2 * HEADS * RET_DK + HEADS * RET_DV))
            load(j_ret_out, folded(w_out_a, 0, KC))
            load(j_kv_k, cols(w_kv, 0))
            sp.wait_ge(yl_done, 2 * HEADS)
            sp.wait_ge(done, j_ret_out.end[2])
            sp.dma_start(DTAB[:, :, :], c_rope_diff).then_inc(s_dtab, 16)
            load(j_kv_v, cols(w_kv, D))
            load(j_diff_q, cols(w_in_b, 0))
            load(j_diff_gate, cols(w_in_b, D))
            load(j_diff_out, cols(w_out_b, 0))

            def pairs(w_gate, w_up, first):
                def f(i, j, dst, s):
                    w = (w_gate, w_up)[j % 2]
                    sp.dma_start(dst.rearrange("p (c n) -> p c n", c=KC),
                                 w[:, :, bass.ds(2 * UCOL * i + (first + (j // 2) * UCOL), UCOL)]).then_inc(s, 16)
                return f

            def load_ffn(name):
                f0 = 0
                wg, wu, wd = w_ffn[name]
                for part, (jg, jd) in zip(FFN_PARTS, ffns[name]):
                    load(jg, pairs(wg, wu, f0 * P))
                    load(jd, folded(wd, f0, part // 2))
                    f0 += part

            load_ffn("ffn1")

            def unit_dst(jb, n=0):
                u = jb.unit0 + n
                sp.wait_ge(lo_done, u - RAWS + 1)
                return RAW[:, u % RAWS, :], raw_in[u % RAWS]

            load(j_cq, cols(w_in, 0))
            dst, s = unit_dst(j_kvm)
            d3 = dst.rearrange("p (c n) -> p c n", c=KC)
            kr = MLA_Q_RANK + MLA_KV_RANK
            for a, b, n in ((0, MLA_Q_RANK, MLA_KV_RANK + MLA_ROPE), (160, kr + 16, 16), (176, kr, 16),
                            (192, kr + MLA_ROPE + 3 * GDN_WIDTH, 64)):
                sp.dma_start(d3[:, :, a:a + n], w_in[:, :, b:b + n]).then_inc(s, 16)
            dst, s = unit_dst(j_uq)
            for k in range(2):
                d3 = dst[:, 1024 * k:1024 * (k + 1)]
                for off, a, b, n in ((0, 0, 0, MLA_NOPE), (512, 0, MLA_NOPE, 32), (768, 0, MLA_NOPE + 16, 16),
                                     (768, 16, MLA_NOPE, 16)):
                    wide = MLA_NOPE if off == 0 else 32
                    sp.dma_start(d3[:, off:off + HEADS * wide].rearrange("p (h n) -> p h n", h=HEADS)[:, :, a:a + n],
                                 w_uq[:, k, :, b:b + n]).then_inc(s, 16)
            dst, s = unit_dst(j_ukv)
            for k in range(2):
                sp.dma_start(dst[:, 512 * k:512 * (k + 1)].rearrange("p (h n) -> p h n", h=HEADS),
                             w_ukv[:, :, MLA_NOPE * k:MLA_NOPE * (k + 1)]).then_inc(s, 16)
            sp.wait_ge(done, at_mix[2])
            sp.dma_start(MTAB[:, :, :], c_rope_mla).then_inc(s_mtab, 16)
            sp.dma_start(CMASK[:, :], c_causal).then_inc(s_cmask, 16)
            first = MLA_Q_RANK + MLA_KV_RANK + MLA_ROPE
            load(j_gqkv, cols(w_in, first))
            sp.wait_ge(kr_done, 4)
            sp.dma_start(TRI[:, :, :], c_tri).then_inc(s_tri, 16)
            sp.wait_ge(ma_pt, len(mla_turns))
            sp.dma_start(ALROW[:, 0:8], A["a_log_2"]).then_inc(s_al, 16)
            sp.dma_start(ALROW[:, 8:16], A["dt_bias_2"]).then_inc(s_al, 16)
            load(j_z, cols(w_in, first + 3 * GDN_WIDTH + 16))
            first += 3 * GDN_WIDTH + 16 + GDN_WIDTH
            for u in range(j_merge.units):
                n, q = u // 3, u % 3
                dst, s = unit_dst(j_merge, u)
                if q < 2:
                    a = first + q * D + n * UCOL
                    sp.dma_start(dst.rearrange("p (c n) -> p c n", c=KC), w_in[:, :, a:a + UCOL]).then_inc(s, 16)
                else:
                    d3 = dst.rearrange("p (b c n) -> p b c n", b=2, c=4)
                    for b, w in enumerate((w_mla_o, w_gdn_o)):
                        sp.dma_start(d3[:, b, :, :], w[:, :, n * UCOL:(n + 1) * UCOL]).then_inc(s, 16)
            load(j_wout, cols(w_out2, 0))
            load_ffn("ffn2")
            for t in range(NT):
                sp.wait_ge(ps_free[(at_rows[1] + t) % SLOTS], (at_rows[1] + t) // SLOTS + 1)
                sp.dma_start(out[0, P * t:P * (t + 1), :], OUTR[:, t, :]).then_inc(s_out, 16)
            sp.wait_ge(s_out, 16 * NT)

        @block.gpsimd
        def _(pool):
            pool.memset(ONES[:, :], 1.0).then_inc(s_ones, 1)
            pool.memset(MHALF[:, :], -0.5).then_inc(s_half, 1)
            pool.memset(ROWS[:, 0:64], 1.0).then_inc(s_rows, 1)
            pool.memset(ROWS[:, 64:128], 0.0).then_inc(s_rows, 1)
            pool.memset(ROWS[:, 128:192], NEG).then_inc(s_rows, 1)
            pool.memset(SEL[:, :], 0.0).then_inc(s_sel, 1)
            for a in range(2):
                pool.wait_ge(s_sel, a + 1)
                pool.memset(SEL[64 * a:64 * a + 64, a:a + 1], 1.0).then_inc(s_sel, 1)
            pool.wait_ge(s_sel, 3)
            pool.wait_ge(s_half, 1)

            def lo(u, i, size=UNIT):
                pool.wait_ge(hi_done, u + 1 + 4 * i)
                pool.tensor_tensor(WL[:, u % SPLITS, 0:size], RAW[:, u % RAWS, 0:size], WH[:, u % SPLITS, 0:size].bitcast(F32),
                                   ALU.subtract).then_inc(lo_done, 1)

            def split(jb):
                def body(i, j):
                    if not isinstance(i, int) or jb.unit0 + 4 * i + j + 1 < n_units:
                        lo(jb.unit0 + j + 1, i, size_after(jb, i, j))
                each(pool, jb, body)

            def root(name):
                n, _, cols = norms[name][:3]
                k, w = token_tiles(width_of(cols))
                pool.wait_ge(ms_done, n + 1)
                pool.tensor_tensor(STAT[0:w, 2, 0:k], STAT[0:w, 0, 0:k], MHALF[0:w, 0:k], ALU.pow).then_inc(root_done, 1)

            lo(0, 0)
            root("norm0")
            split(j_ret_qk)
            split(j_ret_v)
            for h in range(HEADS):
                pool.wait_ge(ra_ve, h + 1)
                pool.tensor_tensor(RSTD[:, 0:NT], VEPS[:, 0:NT], MHALF[:, 0:NT], ALU.pow).then_inc(ra_rs, 1)
            split(j_ret_gate)
            split(j_ret_out)
            root("post0")
            root("norm1")
            split(j_kv_k)
            split(j_kv_v)
            split(j_diff_q)
            for h in range(HEADS):
                pool.wait_ge(da_ve, 2 * h + 2)
                pool.tensor_tensor(RSTD[:, 0:NT], VEPS[:, 0:NT], MHALF[:, 0:NT], ALU.pow).then_inc(da_rs, 1)
            split(j_diff_gate)
            split(j_diff_out)
            root("post1")
            root("ffn1")
            for jg, jd in ffns["ffn1"]:
                split(jg)
                split(jd)
            root("mix")
            split(j_cq)
            split(j_kvm)
            root("cq")
            root("ckv")
            split(j_uq)
            split(j_ukv)
            pool.wait_ge(ma_pt, len(mla_turns))
            pool.memset(BA[:, :, :], 0.0).then_inc(ba_zero, 1)
            pool.memset(PRE[:, :, 0:CONV - 1], 0.0).then_inc(pre_zero, 1)
            split(j_gqkv)
            pool.wait_ge(ss_done, 1)
            pool.tensor_tensor(RN[0:META, 0, 8:16], RN[0:META, 0, 8:16], MHALF[0:META, :], ALU.pow).then_inc(rn_done, 1)
            lo(j_z.unit0 + 1, 0)
            pool.tensor_tensor(RN[:, 1:3, :], RN[:, 1:3, :], MHALF[:, 0:1].unsqueeze(2).to_broadcast([P, 2, 16]),
                               ALU.pow).then_inc(rn_done, 1)
            lo(j_z.unit0 + 2, 0)
            pool.tensor_tensor(RN[:, 3:5, :], RN[:, 3:5, :], MHALF[:, 0:1].unsqueeze(2).to_broadcast([P, 2, 16]),
                               ALU.pow).then_inc(rn_done, 1)

            def decay_inputs(t):
                w, _ = tile(t)
                if t:
                    pool.wait_ge(g_pe, PE_AT[t - 1, ("x", levels(t - 1)[-1], 1)])
                pool.tensor_tensor(UG[0:w, :, 0:w], TRI[0:w, 0:1, 0:w].to_broadcast([w, HEADS, w]),
                                   over_heads(GG[0:w, t, :], w, w), ALU.mult).then_inc(g_pool, one("pool", t, "ug"))
            pool.wait_ge(g_dve, N_PRE_DVE)
            pool.wait_ge(s_tri, 16)
            pool.wait_ge(conv_done, 12)
            decay_inputs(0)
            pool.wait_ge(fac_done, N_FACTORS)
            for t in range(NT + 1):
                w, _ = tile(t)
                pool.wait_ge(g_act, ACT_AT[t, "rows"])
                pool.tensor_tensor(by_head(KBG[0:w, :]), by_head(ROWQ[0:w, 1, :]), over_heads(FKBG[0:w, t, :], w, GDN_D),
                                   ALU.mult).then_inc(g_pool, one("pool", t, "kbg"))
                pool.tensor_tensor(by_head(KD[0:w, :]), by_head(ROWQ[0:w, 1, :]), over_heads(FKD[0:w, t, :], w, GDN_D),
                                   ALU.mult).then_inc(g_pool, one("pool", t, "kd"))
                pool.tensor_tensor(by_head(ROWQ[0:w, 2, :]), by_head(ROWQ[0:w, 2, :]), over_heads(BETA[0:w, t, :], w, GDN_D),
                                   ALU.mult).then_inc(g_pool, one("pool", t, "vb"))
                if t:
                    pool.wait_ge(g_dve, DVE_AT[t, "at"])
                    pool.wait_ge(g_act, ACT_AT[t, "decay"])
                    pool.tensor_tensor(AT[:, :, :], AT[:, :, :], DEC[:, :, :], ALU.mult).then_inc(g_pool, one("pool", t, "at"))
                if t < NT:
                    decay_inputs(t + 1)
                if t:
                    pool.wait_ge(g_dve, DVE_AT[t, "out_eps"])
                    pool.tensor_tensor(ORN[:, :], OSS[:, :], MHALF[:, :], ALU.pow).then_inc(g_pool, one("pool", t, "out_rnorm"))
            for u in range(j_merge.units):
                lo(j_merge.unit0 + u + 1, 0)
            split(j_wout)
            root("ffn2")
            for jg, jd in ffns["ffn2"]:
                split(jg)
                split(jd)
            root("final")

        @block.scalar
        def _(act):
            def hi(u, i, used, size=UNIT):
                act.wait_ge(raw_in[u % RAWS], 16 * i + 16 * (u // RAWS + 1) + 16 * extra_loads(u))
                if used is not None:
                    act.wait_ge(done, used)
                nc.scalar.activation(WH[:, u % SPLITS, 0:size], RAW[:, u % RAWS, 0:size], ACT.Copy).then_inc(hi_done, 1)

            def next_hi(jb, i, j):
                if not isinstance(i, int) or jb.unit0 + 4 * i + j + 1 < n_units:
                    hi(jb.unit0 + j + 1, i, jb.tick0 + 8 * i + 2 * j, size_after(jb, i, j))

            def square(src, q, width):
                if not isinstance(q, int) or q >= 2:
                    act.wait_ge(sq_added, q - 1)
                par = q % 2 if isinstance(q, int) else square.par
                nc.scalar.activation(halves(SQ[:, par, 0:width]), src, ACT.Square).then_inc(sq_done, 1)

            def u_hi(name, jb_before, dst=UH, count=KC):
                cols = norms[name][2]
                if jb_before is not None:
                    act.wait_ge(done, jb_before.end[2])
                for k in range(count):
                    act.wait_ge(t_done, applied[name] + k + 1)
                    nc.scalar.activation(dst[:, k, cols], TMP[:, k % 2, 0:width_of(cols)], ACT.Copy).then_inc(uh_done, 1)

            for k in range(KC):
                slot = (at_x[1] + k) % SLOTS
                act.wait_ge(done, at_x[2] + k + 1)
                square(acc(slot, SEQ), k, SEQ)
                nc.scalar.activation(RES[:, k, SEQ_COLS], acc(slot, SEQ), ACT.Copy).then_inc(ps_free[slot], 1)
            slot = (at_x[1] + KC) % SLOTS
            act.wait_ge(done, at_x[2] + KC + 1)
            nc.scalar.activation(GAINS[:, 0:N_ROWS], PS[:, 2 * slot, P:P + N_ROWS], ACT.Copy)
            nc.scalar.activation(RES[:, :, 0:META], PS[:, 2 * slot, 0:KC * META].rearrange("p (k n) -> p k n", k=KC),
                                 ACT.Copy).then_inc(ps_free[slot], 1)
            hi(0, 0, None)
            u_hi("norm0", None)

            jb = j_ret_qk

            def body(i, j):
                next_hi(jb, i, j)
                for m in range(2):
                    slot, uses = chunk_of(jb, i, j, m)
                    act.wait_ge(done, tick_of(jb, i, j, m))
                    wait(act, rope_done, 8 * i + max(2 * j + m - 1, 0))
                    nc.scalar.activation(SG[0:64, m, 0:SEQ], PS[64:128, 2 * slot, :], ACT.Copy).then_inc(shift_done, 1)
                    nc.scalar.activation(SG[64:128, m, 0:SEQ], PS[0:64, 2 * slot, :], ACT.Copy).then_inc(shift_done, 1)
            each(act, jb, body, peel=1)

            jb = j_ret_v

            def body(i, j):
                next_hi(jb, i, j)
                for m in range(2):
                    slot, uses = chunk_of(jb, i, j, m)
                    act.wait_ge(done, tick_of(jb, i, j, m))
                    nc.scalar.activation(V[:, 2 * m:2 * m + 2, bass.ds(4 * UCOL * i + j * UCOL, UCOL)],
                                         PS[:, 2 * slot, :].rearrange("p (t n) -> p t n", t=2),
                                         ACT.Copy).then_inc(ps_free[slot], 1)
            each(act, jb, body)

            act.wait_ge(rope_done, 2 * HEADS)
            for h in range(2):
                act.dma_start(DECAY[:, h % 2, 0:SEQ], c_decay[h]).then_inc(dec_in[h % 2], 16)
            for h in range(HEADS + 3):
                if h and h + 1 < HEADS:
                    act.wait_ge(ra_m, NT * h)
                    act.dma_start(DECAY[:, (h + 1) % 2, 0:SEQ], c_decay[h + 1]).then_inc(dec_in[(h + 1) % 2], 16)
                for g, e in ((h - 3, 1), (h - 2, 0)):
                    if 0 <= g < HEADS:
                        act.wait_ge(ra_t, 2 * g + e + 1)
                        nc.scalar.activation(QK[:, 2 * g + e, :], PS[:, 7, :], ACT.Copy).then_inc(ra_e, 1)

            jb = j_ret_gate

            def body(i, j):
                next_hi(jb, i, j)
                for m in range(2):
                    slot, uses = chunk_of(jb, i, j, m)
                    act.wait_ge(done, tick_of(jb, i, j, m))
                    wait(act, y_done, 8 * i + max(2 * j + m - 1, 0))
                    nc.scalar.activation(SG[:, m, 0:SEQ], acc(slot, SEQ), ACT.Silu).then_inc(ps_free[slot], 1)
                    act.wait_ge(y_done, 8 * i + 2 * j + m + 1)
                    nc.scalar.activation(YH[:, bass.ds(8 * i + (2 * j + m), 1), :],
                                         TMP[:, m:m + 1, 0:SEQ], ACT.Copy).then_inc(yh_done, 1)
            each(act, jb, body, peel=1)

            jb = j_ret_out
            q0 = norms["post0"][3]

            def body(i, j):
                next_hi(jb, i, j)
                if j % 2:
                    for m in range(2):
                        slot, uses = chunk_of(jb, i, j, m)
                        act.wait_ge(done, tick_of(jb, i, j, m))
                        square.par = m
                        square(acc(slot, SEQ), q0 + 4 * i + (j - 1 + m), SEQ)
                        nc.scalar.activation(Y2[:, bass.ds(4 * i + (j - 1 + m), 1), :],
                                             PS[:, 2 * slot:2 * slot + 1, :], ACT.Copy).then_inc(ps_free[slot], 1)
            each(act, jb, body)

            def residual_squares(name, ready):
                cols, q0 = norms[name][2:4]
                for k in range(KC):
                    act.wait_ge(*ready(k))
                    square(halves(RES[:, k, cols]), q0 + k, width_of(cols))

            def swap_quarters(jb, n0, scale):
                def body(i, j):
                    next_hi(jb, i, j)
                    for m in range(2):
                        slot, uses = chunk_of(jb, i, j, m)
                        act.wait_ge(done, tick_of(jb, i, j, m))
                        act.wait_ge(rope_done, n0 + 8 * i + 2 * j + m - 1)
                        for a, b in ((0, 32), (32, 0), (64, 96), (96, 64)):
                            nc.scalar.activation(SG[a:a + 32, m, 0:SEQ], PS[b:b + 32, 2 * slot, :], ACT.Copy,
                                                 scale=scale).then_inc(shift_done, 1)
                each(act, jb, body)

            def keep_rows(jb, dst):
                def body(i, j):
                    next_hi(jb, i, j)
                    for m in range(2):
                        slot, uses = chunk_of(jb, i, j, m)
                        act.wait_ge(done, tick_of(jb, i, j, m))
                        nc.scalar.activation(dst[:, 2 * m:2 * m + 2, bass.ds(4 * UCOL * i + j * UCOL, UCOL)],
                                             PS[:, 2 * slot, :].rearrange("p (t n) -> p t n", t=2),
                                             ACT.Copy).then_inc(ps_free[slot], 1)
                each(act, jb, body)

            residual_squares("norm1", lambda k: (res_done, k + 1))
            u_hi("norm1", j_ret_out)
            swap_quarters(j_kv_k, 16, 1.0)
            keep_rows(j_kv_v, DV)
            u_hi("norm1q", j_kv_v)
            swap_quarters(j_diff_q, 24, DIFF_DH ** -0.5)
            act.wait_ge(lam_step, 2)
            nc.scalar.activation(LAMS[0:1, 2:4], LAMS[0:1, 0:2], ACT.Exp).then_inc(lam_exp, 1)

            for s in range(ITEMS + HEAD_LAG):
                if s < ITEMS:
                    h, b = s // NT, s % NT
                    n = P * (b + 1)
                    act.wait_ge(da_max, s + 1)
                    if s >= 2:
                        act.wait_ge(da_w, s - 1)
                    for t in range(2):
                        nc.scalar.activation(DE[:, s % 2, t, 0:n], PS[:, 2 * (s % 2) + t, 0:n], ACT.Exp,
                                             bias=NEGM[:, s % 2, t:t + 1],
                                             accum_out=ESUM[:, s % 2, t:t + 1]).then_inc(da_e, 1)
                for kind, g in [x for x in (("item", s - 2), ("head", (s - HEAD_LAG) / NT)) if x in turn_no]:
                    g = int(g)
                    no = turn_no[kind, g]
                    act.wait_ge(da_t, no + 1)
                    if kind == "item":
                        if g >= 2:
                            act.wait_ge(da_pv, g - 1)
                        n = P * (g % NT + 1)
                        nc.scalar.activation(DWT[:, g % 2, 0:n], PS[:, 4 + no % 2, 0:n], ACT.Copy).then_inc(da_wt, 1)
                    else:
                        nc.scalar.activation(DQK[:, g, :], PS[:, 4 + no % 2, :], ACT.Copy).then_inc(da_wt, 1)
                if s >= 7 and (s - 7) % NT == 0 and (s - 7) // NT < HEADS:
                    h = (s - 7) // NT
                    act.wait_ge(da_on, 2 * h + 1)
                    if h:
                        act.wait_ge(da_ve, 2 * h)
                    nc.scalar.activation(DSQ[:, :, :], DON[:, h % 2, :, :], ACT.Square).then_inc(da_sq, 1)

            jb = j_diff_gate

            def body(i, j):
                next_hi(jb, i, j)
                for m in range(2):
                    slot, uses = chunk_of(jb, i, j, m)
                    n = 8 * i + 2 * j + m
                    act.wait_ge(done, tick_of(jb, i, j, m))
                    act.wait_ge(y_done, 16 + n - 1)
                    nc.scalar.activation(SG[:, m, 0:SEQ], acc(slot, SEQ), ACT.Silu).then_inc(ps_free[slot], 1)
                    act.wait_ge(y_done, 16 + n + 1)
                    nc.scalar.activation(DYH[:, n, :], TMP[:, m, 0:SEQ], ACT.Copy).then_inc(yh_done, 1)
            each(act, jb, body)

            jb = j_diff_out

            def body(i, j):
                next_hi(jb, i, j)
                for m in range(2):
                    slot, uses = chunk_of(jb, i, j, m)
                    act.wait_ge(done, tick_of(jb, i, j, m))
                    n = 2 * (4 * i + j) + m
                    square(acc(slot, SEQ), norms["post1"][3] + n, SEQ)
                    nc.scalar.activation(Y2[:, n, :], acc(slot, SEQ), ACT.Copy).then_inc(ps_free[slot], 1)
            each(act, jb, body)

            def res_chunk(k, cols):
                ap = RES[:, bass.ds(k, 1), cols]
                if width_of(cols) > 512:
                    return ap.rearrange("p o (a n) -> p (o a) n", a=2)
                return ap.rearrange("p o n -> p (o n)")

            def ffn_act(name, number, after):
                cols = norms[name][2]
                width = width_of(cols)
                for part, (jg, jd) in enumerate(ffns[name]):
                    h0 = 22 * number + (FFN_PARTS[0] if part else 0)
                    if part:
                        act.wait_ge(done, ffns[name][0][1].end[2])

                    def body(i, j):
                        next_hi(jg, i, j)
                        for m in range(2):
                            n = 2 * (j // 2) + m
                            slot, uses = chunk_of(jg, i, j, m)
                            if j % 2 == 0:
                                act.wait_ge(done, tick_of(jg, i, j, m))
                                wait(act, hl_done, h0 + 4 * i + max(n - 1, 0))
                                nc.scalar.activation(halves(SG[:, m, 0:width]), acc(slot, width),
                                                     ACT.Silu).then_inc(ps_free[slot], 1)
                            else:
                                act.wait_ge(ps_free[slot], uses + 1)
                                nc.scalar.activation(HH[:, bass.ds(4 * i + n, 1), 0:width], TMP[:, m:m + 1, 0:width],
                                                     ACT.Copy).then_inc(hh_done, 1)
                    each(act, jg, body, peel=int(h0 == 0))

                    def body(i, j):
                        next_hi(jd, i, j)
                        if j % 2 and part:
                            for m in range(2):
                                slot, uses = chunk_of(jd, i, j, m)
                                act.wait_ge(ps_free[slot], uses + 1)
                                square.par = m
                                square(res_chunk(4 * i + (j - 1 + m), cols), norms[after][3] + 4 * i + (j - 1 + m), width)
                    if after is None:
                        def body(i, j):
                            next_hi(jd, i, j)
                    each(act, jd, body)

            residual_squares("ffn1", lambda k: (res_done, KC + k + 1))
            u_hi("ffn1", j_diff_out)
            ffn_act("ffn1", 0, "mix")

            u_hi("mix", ffns["ffn1"][-1][0])
            next_hi(j_cq, 0, 0)
            q0 = norms["cq"][3]
            for m in range(2):
                slot, _ = chunk_of(j_cq, 0, 0, m)
                act.wait_ge(done, tick_of(j_cq, 0, 0, m))
                square(acc(slot, SEQ), q0 + m, SEQ)
                nc.scalar.activation(CQF[:, m, :], acc(slot, SEQ), ACT.Copy).then_inc(ps_free[slot], 1)
            next_hi(j_kvm, 0, 0)
            slot, _ = chunk_of(j_kvm, 0, 0, 0)
            act.wait_ge(done, tick_of(j_kvm, 0, 0, 0))
            q0 = norms["ckv"][3]
            for a in range(2):
                square(PS[:, 2 * slot + a, 0:HALF], q0 + a, HALF)
            nc.scalar.activation(halves(CKF[:, 0, :]), acc(slot, TOK), ACT.Copy).then_inc(ps_free[slot], 1)
            slot, _ = chunk_of(j_kvm, 0, 0, 1)
            act.wait_ge(done, tick_of(j_kvm, 0, 0, 1))
            nc.scalar.activation(halves(MISC[:, :]), acc(slot, TOK), ACT.Copy).then_inc(ps_free[slot], 1)
            u_hi("cq", None, CQH, 2)
            u_hi("ckv", None, CKH, 1)
            next_hi(j_uq, 0, 0)
            scale = float(MLA_NOPE + MLA_ROPE) ** -0.5
            for n in range(4):
                c = j_uq.chunk0 + 4 + n
                slot = c % SLOTS
                act.wait_ge(done, j_uq.tick0 + 4 + n + 1)
                nc.scalar.activation(QC[0:64, 2 * n, :], PS[0:64, 2 * slot, :], ACT.Copy, scale=scale)
                nc.scalar.activation(QC[0:64, 2 * n + 1, :], PS[64:128, 2 * slot, :], ACT.Copy,
                                     scale=scale).then_inc(ps_free[slot], 1)
            next_hi(j_ukv, 0, 0)
            for n in range(4):
                c = j_ukv.chunk0 + n
                slot = c % SLOTS
                act.wait_ge(done, j_ukv.tick0 + n + 1)
                nc.scalar.activation(halves(KCAT[0:64, 2 * n, :]), PS[0:64, 2 * slot:2 * slot + 2, 0:HALF], ACT.Copy)
                nc.scalar.activation(halves(KCAT[0:64, 2 * n + 1, :]), PS[64:128, 2 * slot:2 * slot + 2, 0:HALF],
                                     ACT.Copy).then_inc(ps_free[slot], 1)
            for t in range(NT + 1):
                c = j_ukv.chunk0 + 4 + t
                slot = c % SLOTS
                w = META if t == 0 else P
                act.wait_ge(done, j_ukv.tick0 + 4 + t + 1)
                nc.scalar.activation(MV[0:w, t, :], PS[0:w, 2 * slot, :], ACT.Copy).then_inc(ps_free[slot], 1)
            for s in range(HEADS * NT + MLA_LAG):
                if s < HEADS * NT:
                    b = s % NT
                    n = META + P * (b + 1)
                    act.wait_ge(ma_max, s + 1)
                    if s >= 3:
                        act.wait_ge(ma_t, mla_turn_no["item", s - 3] + 1)
                    k = 2 * (s % 2)
                    src = PS[:, k, 0:n] if n <= 512 else PS[:, k:k + 2, 0:HALF]
                    nc.scalar.activation(halves(ME[:, s % 3, 0:n]), src, ACT.Exp, bias=NEGM2[:, s % 2:s % 2 + 1],
                                         accum_out=ESUM2[:, (s // NT) % 4, b:b + 1]).then_inc(ma_e, 1)
                for kind, g in mla_step_turns(s):
                    no = mla_turn_no[kind, g]
                    act.wait_ge(ma_t, no + 1)
                    if kind == "item":
                        b = g % NT
                        if g >= 2:
                            act.wait_ge(ma_pv, g - 1)
                        if b < NT - 1:
                            n = P * (b + 2)
                            nc.scalar.activation(MPT[:, g % 2, 0:n], PS[:, 4 + no % 2, 0:n], ACT.Copy).then_inc(ma_pt, 1)
                        else:
                            nc.scalar.activation(MPT[:, g % 2, 0:SEQ], PS[:, 4 + no % 2, :], ACT.Copy)
                            nc.scalar.activation(MPT[0:META, g % 2, SEQ:640], PS[0:META, 7, 0:P],
                                                 ACT.Copy).then_inc(ma_pt, 1)
                    else:
                        nc.scalar.activation(OMF[:, g, :], PS[:, 4 + no % 2, :], ACT.Copy).then_inc(ma_pt, 1)

            jb = j_gqkv
            for n in range(14):
                if n < 12:
                    i, j, m = n // 8, n // 2 % 4, n % 2
                    if m == 0:
                        next_hi(jb, 0, n // 2)
                    slot, uses = chunk_of(jb, 0, n // 2, m)
                    act.wait_ge(done, tick_of(jb, 0, n // 2, m))
                    if n >= 2:
                        act.wait_ge(tap_done, 4 * (n - 1))
                    nc.scalar.activation(halves(PRE[:, m, CONV - 1:CONV - 1 + TOK]), acc(slot, TOK),
                                         ACT.Copy).then_inc(ps_free[slot], 1)
                if n >= 1 and n <= 12:
                    act.wait_ge(tap_done, 4 * n)
                    nc.scalar.activation(CVS[:, n - 1, :], TMP[:, (n - 1) % 2, :], ACT.Silu).then_inc(conv_done, 1)
            for n in range(8):
                act.wait_ge(conv_done, n + 1)
                if n >= 2:
                    act.wait_ge(ss_mm, n - 1)
                nc.scalar.activation(SG[:, n % 2, :], CVS[:, n, :], ACT.Square).then_inc(gsq_done, 1)
            jb = j_z
            for j in range(2):
                next_hi(jb, 0, j)
                for m in range(2):
                    slot, uses = chunk_of(jb, 0, j, m)
                    act.wait_ge(done, tick_of(jb, 0, j, m))
                    nc.scalar.activation(ZS[:, 2 * j + m, :], acc(slot, SEQ), ACT.Silu).then_inc(ps_free[slot], 1)
            act.wait_ge(g_pe, 1)
            act.wait_ge(ba_zero, 1)
            nc.scalar.activation(BA[:, 1:NT + 1, :], PS[:, 0, 16:80].rearrange("p (t n) -> p t n", t=NT), ACT.Copy)
            nc.scalar.activation(BA[0:META, 0, :], PS[0:META, 0, 0:16], ACT.Copy).then_inc(g_act, 1)
            nc.scalar.activation(EAL[:, :], PS[:, 1, 0:8], ACT.Exp).then_inc(g_act, 1)
            act.wait_ge(g_act, 1)
            nc.scalar.activation(BETA[:, :, :], BA[:, :, 0:8], ACT.Exp, scale=-1.0).then_inc(g_act, 1)
            act.wait_ge(g_dve, 3)
            nc.scalar.activation(EN[:, :, :], XA[:, :, :], ACT.Exp).then_inc(g_act, 1)
            act.wait_ge(g_dve, 6)
            nc.scalar.activation(LNE[:, :, :], EN[:, :, :], ACT.Ln).then_inc(g_act, 1)
            act.wait_ge(g_pe, N_PRE_PE)
            nc.scalar.activation(GEXP[:, 0:80], PS[:, 2, 0:80], ACT.Exp)
            nc.scalar.activation(GEXP[:, 80:96], PS[:, 3, 80:96], ACT.Exp)
            nc.scalar.activation(GEXP[0:META, 96:112], PS[0:META, 2, 96:112], ACT.Exp).then_inc(gexp_done, 1)
            def keep_tile(t):
                w, _ = tile(t)
                q0 = 0 if t else 1
                act.wait_ge(g_pe, PE_AT[t, "turn_in"])
                nc.scalar.activation(ROWQ[0:w, q0:3, :], PS[0:w, q0:3, :], ACT.Copy).then_inc(g_act, one("act", t, "rows"))

            act.wait_ge(g_pool, POOL_AT[0, "ug"])
            keep_tile(0)
            for t in range(NT + 1):
                w, cols = tile(t)
                act.wait_ge(g_pe, PE_AT[t, "decay"])
                if t > 1:
                    act.wait_ge(g_pe, PE_AT[t - 1, "turn_out"])
                for b in range(2):
                    last = nc.scalar.activation(DEC[0:w, 4 * b:4 * b + 4, 0:w],
                                                PS[0:w, b, 0:4 * w].rearrange("p (h c) -> p h c", h=4), ACT.Exp)
                last.then_inc(g_act, one("act", t, "decay"))
                act.wait_ge(g_pe, PE_AT[t, "turn_k"])
                for bank, dst in ((3, KT), (5, KBT)):
                    last = nc.scalar.activation(dst[:, :, 0:w], PS[:, bank, 0:4 * w].rearrange("p (h c) -> p h c", h=4), ACT.Copy)
                last.then_inc(g_act, one("act", t, "turned_k"))
                act.wait_ge(g_pe, PE_AT[t, "d1"])
                for b in range(2):
                    last = nc.scalar.activation(TI[0:w, 4 * b:4 * b + 4, 0:w],
                                                PS[0:w, b, 0:4 * w].rearrange("p (h c) -> p h c", h=4), ACT.Copy)
                last.then_inc(g_act, one("act", t, "d1"))
                act.wait_ge(g_pe, PE_AT[t, "uw"])
                if t:
                    nc.scalar.activation(WTT[:, :, :], PS[:, 6, :].rearrange("p (h c) -> p h c", h=4), ACT.Copy)
                nc.scalar.activation(UU[0:w, :], PS[0:w, 5, :], ACT.Copy).then_inc(g_act, one("act", t, "uw"))
                if t:
                    act.wait_ge(g_dve, DVE_AT[t, "out_join"])
                    nc.scalar.activation(GSQ[:, 1, :], GON[:, :], ACT.Square).then_inc(g_act, one("act", t, "out_square"))
                if t < NT:
                    keep_tile(t + 1)

            def merge_chunk(n, c):
                chunk = j_merge.chunk0 + 8 * n + c
                return chunk % SLOTS, chunk // SLOTS, j_merge.tick0 + 8 * n + c + 1

            act.wait_ge(g_dve, DVE_AT[NT, "out_gate"])
            next_hi(j_merge, 0, 0)
            for k in range(4):
                nc.scalar.activation(OMH[:, k, :], OMF[:, k, :], ACT.Copy).then_inc(oh_done, 1)
            for k in range(4):
                nc.scalar.activation(GOH[:, k, :], ZS[:, k, :], ACT.Copy).then_inc(gh_done, 1)
            for n in range(4):
                for q in range(3):
                    if n or q:
                        hi(j_merge.unit0 + 3 * n + q + 1, 0, j_merge.tick0 + 8 * n + 2 * q)
                    if q < 2:
                        for m in range(2):
                            slot, uses, tick = merge_chunk(n, 2 * q + m)
                            act.wait_ge(done, tick)
                            if n:
                                act.wait_ge(ml_done, 2 * n)
                            nc.scalar.activation(GATE[:, q, m, :], acc(slot, SEQ), ACT.Sigmoid).then_inc(ps_free[slot], 1)
                for m in range(2):
                    act.wait_ge(merged_done, 2 * n + m + 1)
                    nc.scalar.activation(MH[:, 2 * n + m, :], GATE[:, 0, m, :], ACT.Copy).then_inc(mh_done, 1)
            q0 = norms["ffn2"][3]
            for j in range(j_wout.units):
                next_hi(j_wout, 0, j)
                for m in range(2):
                    slot, uses = chunk_of(j_wout, 0, j, m)
                    act.wait_ge(ps_free[slot], uses + 1)
                    square(RES[:, 2 * j + m, SEQ_COLS], q0 + 2 * j + m, SEQ)
            u_hi("ffn2", j_merge)
            ffn_act("ffn2", 1, "final")
            for t in range(0, NT, 2):
                slot = (at_rows[1] + t) % SLOTS
                act.wait_ge(done, at_rows[2] + t + 1)
                nc.scalar.activation(OUTR[:, t, :], PS[:, 2 * slot:2 * slot + 2, :].rearrange("p a n -> p (a n)"),
                                     ACT.Copy).then_inc(ps_free[slot], 1)

        @block.vector
        def _(dve):
            def add_square(q, first, width, par):
                dve.wait_ge(sq_done, q + 1)
                if first:
                    nc.vector.tensor_copy(SUMSQ[:, 0:width], SQ[:, par, 0:width]).then_inc(sq_added, 1)
                else:
                    dve.wait_ge(sq_added, q)
                    nc.vector.tensor_tensor(SUMSQ[:, 0:width], SUMSQ[:, 0:width], SQ[:, par, 0:width],
                                            ALU.add).then_inc(sq_added, 1)

            def spread(name):
                n, (_, chunk, tick), cols, _, _, features = norms[name]
                k, w = token_tiles(width_of(cols))
                slot = chunk % SLOTS
                dve.wait_ge(done, tick + 1)
                sums = PS[0:w, 2 * slot, 0:k]
                if name in BY_CHUNK:
                    sums = STAT[0:w, 1, 0:k]
                    nc.vector.tensor_reduce(sums, PS[0:w, 2 * slot, 0:KC * k].rearrange("p (t q) -> p t q", q=KC), AX.X,
                                            ALU.add).then_inc(ps_free[slot], 1)
                    dve.wait_ge(ps_free[slot], chunk // SLOTS + 1)
                nc.vector.tensor_scalar(STAT[0:w, 0, 0:k], sums, 1.0 / features, EPS, ALU.mult, ALU.add).then_inc(ms_done, 1)
                if name not in BY_CHUNK:
                    dve.wait_ge(ms_done, n + 1)
                    nc.vector.tensor_copy(STAT[0:w, 1, 0:1], PS[0:w, 2 * slot, 0:1]).then_inc(ps_free[slot], 1)
                dve.wait_ge(root_done, n + 1)
                for t in range(k):
                    last = nc.vector.tensor_scalar(DIAG[0:w, t * w:(t + 1) * w], IDENT[0:w, 0:w],
                                                   STAT[0:w, 2, t:t + 1], None, ALU.mult)
                last.then_inc(diag_done, 1)

            def apply(name, gain, x=RES, lo=UL, hi=UH, count=KC, kept=None, keep=None):
                n, (_, chunk, tick), cols = norms[name][:3]
                width = width_of(cols)
                slot = (chunk + 1) % SLOTS
                a = applied[name]
                src = acc(slot, width) if kept is None else kept
                if kept is None:
                    dve.wait_ge(done, tick + 2)

                def low(k):
                    dve.wait_ge(uh_done, a + k + 1)
                    nc.vector.tensor_tensor(lo[:, k, cols], TMP[:, k % 2, 0:width], hi[:, k, cols].bitcast(F32),
                                            ALU.subtract).then_inc(ul_done, 1)
                for k in range(count):
                    if k >= 2:
                        low(k - 2)
                        dve.wait_ge(ul_done, a + k - 1)
                    nc.vector.scalar_tensor_tensor(
                        out=halves(TMP[:, k % 2, 0:width]), in0=halves(x[:, k, cols]),
                        scalar=GAINS[:, gain + k:gain + k + 1], in1=src, op0=ALU.mult, op1=ALU.mult).then_inc(t_done, 1)
                if keep is not None:
                    nc.vector.tensor_copy(keep, acc(slot, width)).then_inc(ps_free[slot], 1)
                elif kept is None:
                    nc.vector.tensor_copy(STAT[:, 0, 7:8], PS[:, 2 * slot, 0:1]).then_inc(ps_free[slot], 1)
                for k in range(max(count - 2, 0), count):
                    low(k)

            def post(name, gain, squares):
                n, (_, chunk, tick), cols = norms[name][:3]
                slot = (chunk + 1) % SLOTS
                b = KC * squares
                dve.wait_ge(done, tick + 2)
                for k in range(KC):
                    if k >= 2:
                        dve.wait_ge(res_done, b + k - 1)
                    nc.vector.scalar_tensor_tensor(
                        out=TMP[:, k % 2, 0:SEQ], in0=Y2[:, k, :], scalar=GAINS[:, gain * KC + k:gain * KC + k + 1],
                        in1=acc(slot, SEQ), op0=ALU.mult, op1=ALU.mult).then_inc(post_t, 1)
                    if k >= 1:
                        dve.wait_ge(post_t, b + k)
                        nc.vector.tensor_tensor(RES[:, k - 1, cols], RES[:, k - 1, cols], TMP[:, (k - 1) % 2, 0:SEQ],
                                                ALU.add).then_inc(res_done, 1)
                nc.vector.tensor_copy(STAT[:, 0, 7:8], PS[:, 2 * slot, 0:1]).then_inc(ps_free[slot], 1)
                dve.wait_ge(post_t, b + KC)
                nc.vector.tensor_tensor(RES[:, KC - 1, cols], RES[:, KC - 1, cols], TMP[:, (KC - 1) % 2, 0:SEQ],
                                        ALU.add).then_inc(res_done, 1)

            for k in range(KC):
                add_square(k, k == 0, SEQ, k % 2)
            dve.wait_ge(s_ident, 16)
            spread("norm0")
            for k in range(KC + 1):
                dve.wait_ge(ps_free[(at_x[1] + k) % SLOTS], (at_x[1] + k) // SLOTS + 1)
            apply("norm0", 0 * KC)
            jb = j_ret_qk
            dve.wait_ge(s_tab, 16)

            def body(i, j):
                for m in range(2):
                    slot, uses = chunk_of(jb, i, j, m)
                    n = 2 * j + m
                    dve.wait_ge(done, tick_of(jb, i, j, m))
                    dve.wait_ge(shift_done, 16 * i + 2 * n + 2)
                    wait(dve, rope_done, 8 * i + max(n - 1, 0))
                    nc.vector.tensor_tensor(TMP[:, m, 0:SEQ], acc(slot, SEQ), TAB[:, 0, :], ALU.mult).then_inc(ps_free[slot], 1)
                    nc.vector.tensor_tensor(SG[:, m, 0:SEQ], SG[:, m, 0:SEQ], TAB[:, 1, :], ALU.mult).then_inc(sin_done, 1)
                    dve.wait_ge(ps_free[slot], uses + 1)
                    dve.wait_ge(sin_done, 8 * i + n + 1)
                    nc.vector.tensor_tensor(QK[:, bass.ds(i + 2 * n, 1), :], TMP[:, m:m + 1, 0:SEQ],
                                            SG[:, m:m + 1, 0:SEQ], ALU.add).then_inc(rope_done, 1)
            each(dve, jb, body, peel=1)

            for h in range(HEADS + 1):
                if h < HEADS:
                    dve.wait_ge(dec_in[h % 2], 16 * (h // 2 + 1))
                    dve.wait_ge(ra_s, h + 1)
                    if h >= 2:
                        dve.wait_ge(ra_pv, h - 1)
                    for b in range(NT):
                        w = SEQ - P * b
                        bank, first = SCORE_AT[b]
                        nc.vector.tensor_tensor(SC[:, h % 2, OFF[b]:OFF[b] + w], PS[:, bank, first:first + w],
                                                DECAY[:, h % 2, 0:w], ALU.mult).then_inc(ra_m, 1)
                if h:
                    g = h - 1
                    dve.wait_ge(ra_pv, g + 1)
                    for b in range(NT):
                        nc.vector.bn_stats(BN6[:, b, :], PS[:, 3 + 2 * (g % 2) + b // 2, RET_DV * (b % 2):RET_DV * (b % 2 + 1)]).then_inc(ra_bn, 1)
                    dve.wait_ge(ra_bn, 2 * NT * g + NT)
                    for b in range(NT):
                        nc.vector.bn_aggr(BNA[:, b, :], BN6[:, b, :]).then_inc(ra_bn, 1)
                    dve.wait_ge(ra_bn, 2 * NT * (g + 1))
                    nc.vector.tensor_scalar(VEPS[:, 0:NT], BNA[:, :, 1], EPS, None, ALU.add).then_inc(ra_ve, 1)
                    dve.wait_ge(ra_rs, g + 1)
                    if g >= 2:
                        dve.wait_ge(ra_t, 2 * g - 2)
                    for b in range(NT):
                        last = nc.vector.tensor_scalar(
                            ON[:, g % 2, b, :], PS[:, 3 + 2 * (g % 2) + b // 2, RET_DV * (b % 2):RET_DV * (b % 2 + 1)],
                            BNA[:, b, 0:1], RSTD[:, b:b + 1], ALU.subtract, ALU.mult)
                    last.then_inc(ra_on, 1)

            jb = j_ret_gate
            dve.wait_ge(ra_e, 2 * HEADS)

            def body(i, j):
                for m in range(2):
                    slot, uses = chunk_of(jb, i, j, m)
                    n = 2 * j + m
                    dve.wait_ge(ps_free[slot], uses + 1)
                    nc.vector.tensor_tensor(TMP[:, m:m + 1, 0:SEQ], SG[:, m:m + 1, 0:SEQ],
                                            QK[:, bass.ds(8 * i + n, 1), :], ALU.mult).then_inc(y_done, 1)
                    dve.wait_ge(yh_done, 8 * i + n + 1)
                    nc.vector.tensor_tensor(YL[:, bass.ds(8 * i + n, 1), :], TMP[:, m:m + 1, 0:SEQ],
                                            YH[:, bass.ds(8 * i + n, 1), :].bitcast(F32), ALU.subtract).then_inc(yl_done, 1)
            each(dve, jb, body)

            jb = j_ret_out
            q0 = norms["post0"][3]
            add_square(q0, True, SEQ, 0)
            for k in range(1, KC):
                add_square(q0 + k, False, SEQ, k % 2)
            spread("post0")
            for s in range(SLOTS):
                dve.wait_ge(ps_free[s], len([c for c in range(at_post0[1]) if c % SLOTS == s]))
            post("post0", 1, 0)

            def rotate(jb, r0, tab, dst, scale):
                sh0 = 32 + 4 * (r0 - 16)

                def body(i, j):
                    for m in range(2):
                        slot, uses = chunk_of(jb, i, j, m)
                        n = 8 * i + 2 * j + m
                        dve.wait_ge(shift_done, sh0 + 4 * n + 4)
                        dve.wait_ge(rope_done, r0 + n - 1)
                        nc.vector.scalar_tensor_tensor(out=TMP[:, m, 0:SEQ], in0=acc(slot, SEQ), scalar=scale,
                                                       in1=tab[:, 0, :], op0=ALU.mult, op1=ALU.mult).then_inc(ps_free[slot], 1)
                        nc.vector.tensor_tensor(SG[:, m, 0:SEQ], SG[:, m, 0:SEQ], tab[:, 1, :], ALU.mult).then_inc(sin_done, 1)
                        dve.wait_ge(ps_free[slot], uses + 1)
                        dve.wait_ge(sin_done, r0 + n + 1)
                        nc.vector.tensor_tensor(dst(n), TMP[:, m, 0:SEQ], SG[:, m, 0:SEQ], ALU.add).then_inc(rope_done, 1)
                each(dve, jb, body)

            spread("norm1")
            apply("norm1", 2 * KC, keep=RB[:, :])
            dve.wait_ge(s_dtab, 16)
            rotate(j_kv_k, 16, DTAB, lambda n: DQK[:, HEADS + n, :], 1.0)
            dve.wait_ge(done, j_kv_v.end[2])
            dve.wait_ge(rope_done, 24)
            apply("norm1q", 3 * KC, kept=RB[:, :])
            rotate(j_diff_q, 24, DTAB, lambda n: DQK[:, n, :], DIFF_DH ** -0.5)
            dve.wait_ge(s_lamv, 64)
            nc.vector.tensor_tensor(LAMV[:, 0:2, :], LAMV[:, 0:2, :], LAMV[:, 2:4, :], ALU.mult).then_inc(lam_step, 1)
            dve.wait_ge(lam_step, 1)
            nc.vector.tensor_reduce(LAMS[0:1, 0:2], LAMV[:, 0:2, :], AX.X, ALU.add).then_inc(lam_step, 1)
            dve.wait_ge(lam_exp, 1)
            nc.vector.tensor_scalar(LAMS[0:1, 4:5], LAMS[0:1, 3:4], LAMS[0:1, 2:3], -LAMBDA_INIT,
                                    ALU.subtract, ALU.add).then_inc(lam_step, 1)
            slot = at_lam[1] % SLOTS
            dve.wait_ge(done, at_lam[2] + 1)
            nc.vector.tensor_scalar(LAMS[:, 6:7], GAINS[:, SUB_ROW:SUB_ROW + 1], 1.0 - LAMBDA_INIT, None,
                                    ALU.mult).then_inc(lam_step, 1)
            nc.vector.tensor_copy(LAMS[:, 5:6], PS[:, 2 * slot, 0:1]).then_inc(ps_free[slot], 1)
            dve.wait_ge(ps_free[slot], at_lam[1] // SLOTS + 1)
            nc.vector.tensor_copy(LAMS[:, 7:8], LAMS[:, 5:6]).then_inc(lam_step, 1)

            dve.wait_ge(lam_step, 5)
            for s in range(ITEMS + HEAD_LAG):
                if s < 4 * HEADS:
                    n = P * (s % NT + 1)
                    dve.wait_ge(da_s, s + 1)
                    if s >= 2:
                        dve.wait_ge(da_e, 2 * (s - 1))
                    nc.vector.tensor_reduce(NEGM[:, s % 2, :], PS[:, 2 * (s % 2):2 * (s % 2) + 2, 0:n], AX.X, ALU.max,
                                            negate=True).then_inc(da_max, 1)
                if 1 <= s <= 4 * HEADS:
                    g = s - 1
                    h, b = g // NT, g % NT
                    n = P * (b + 1)
                    dve.wait_ge(da_e, 2 * g + 2)
                    if b == 0 and h >= 2:
                        dve.wait_ge(da_on, 2 * (h - 1) - 1)
                    nc.vector.reciprocal(RSUM[:, h % 2, b, :], ESUM[:, g % 2, :]).then_inc(da_c, 1)
                    dve.wait_ge(da_c, 2 * g + 1)
                    dve.wait_ge(da_w, g)
                    nc.vector.scalar_tensor_tensor(out=COEF[:, 0:1], in0=ESUM[:, g % 2, 0:1],
                                                   scalar=RSUM[:, h % 2, b, 1:2], in1=LAMS[:, 5:6],
                                                   op0=ALU.mult, op1=ALU.mult).then_inc(da_c, 1)
                    dve.wait_ge(da_c, 2 * g + 2)
                    if g >= 2:
                        dve.wait_ge(da_t, turn_no["item", g - 2] + 1)
                    nc.vector.scalar_tensor_tensor(out=DW[:, g % 2, 0:n], in0=DE[:, g % 2, 1, 0:n], scalar=COEF[:, 0:1],
                                                   in1=DE[:, g % 2, 0, 0:n], op0=ALU.mult, op1=ALU.add).then_inc(da_w, 1)
                if s >= 7 and (s - 7) % NT == 0 and (s - 7) // NT < HEADS:
                    h = (s - 7) // NT
                    dve.wait_ge(da_pv, NT * (h + 1))
                    if h >= 2:
                        dve.wait_ge(da_t, turn_no["head", h - 2] + 1)
                    nc.vector.tensor_tensor(DON[:, h % 2, :, :], PS[:, 6 + h % 2, :].rearrange("p (t n) -> p t n", t=NT),
                                            RSUM[:, h % 2, :, 0:1].to_broadcast([P, NT, P]), ALU.mult).then_inc(da_on, 1)
                if s >= 8 and (s - 8) % NT == 0 and (s - 8) // NT < HEADS:
                    h = (s - 8) // NT
                    dve.wait_ge(da_sq, h + 1)
                    nc.vector.tensor_reduce(SSQ[:, :], DSQ[:, :, :], AX.X, ALU.add).then_inc(da_ve, 1)
                    dve.wait_ge(da_ve, 2 * h + 1)
                    nc.vector.tensor_scalar(VEPS[:, 0:NT], SSQ[:, :], 1.0 / P, EPS, ALU.mult, ALU.add).then_inc(da_ve, 1)
                if s >= 9 and (s - 9) % NT == 0 and (s - 9) // NT < HEADS:
                    h = (s - 9) // NT
                    dve.wait_ge(da_rs, h + 1)
                    nc.vector.tensor_tensor(DON[:, h % 2, :, :], DON[:, h % 2, :, :],
                                            RSTD[:, 0:NT].unsqueeze(2).to_broadcast([P, NT, P]), ALU.mult).then_inc(da_on, 1)

            jb = j_diff_gate
            dve.wait_ge(da_wt, len(turns))

            def body(i, j):
                for m in range(2):
                    slot, uses = chunk_of(jb, i, j, m)
                    n = 8 * i + 2 * j + m
                    dve.wait_ge(ps_free[slot], uses + 1)
                    if n >= 2:
                        dve.wait_ge(yl_done, 16 + n - 1)
                    nc.vector.scalar_tensor_tensor(out=TMP[:, m, 0:SEQ], in0=DQK[:, n, :], scalar=LAMS[:, 6:7],
                                                   in1=SG[:, m, 0:SEQ], op0=ALU.mult, op1=ALU.mult).then_inc(y_done, 1)
                    dve.wait_ge(yh_done, 16 + n + 1)
                    nc.vector.tensor_tensor(DYL[:, n, :], TMP[:, m, 0:SEQ], DYH[:, n, :].bitcast(F32),
                                            ALU.subtract).then_inc(yl_done, 1)
            each(dve, jb, body)
            q0 = norms["post1"][3]
            dve.wait_ge(yl_done, 24)
            for k in range(KC):
                add_square(q0 + k, k == 0, SEQ, k % 2)
            spread("post1")
            for s, n in enumerate(uses_before(at_post1[1])):
                dve.wait_ge(ps_free[s], n)
            post("post1", 4, 1)

            def res_chunk(k, cols):
                ap = RES[:, bass.ds(k, 1), cols]
                if width_of(cols) > 512:
                    return ap.rearrange("p o (a n) -> p (o a) n", a=2)
                return ap.rearrange("p o n -> p (o n)")

            def ffn_dve(name, number, after):
                cols = norms[name][2]
                width = width_of(cols)
                for part, (jg, jd) in enumerate(ffns[name]):
                    h0 = 22 * number + (FFN_PARTS[0] if part else 0)
                    if part:
                        dve.wait_ge(done, ffns[name][0][1].end[2])

                    def body(i, j):
                        if j % 2:
                            for m in range(2):
                                n = 2 * (j // 2) + m
                                slot, uses = chunk_of(jg, i, j, m)
                                gslot, guses = chunk_of(jg, i, j - 1, m)
                                dve.wait_ge(done, tick_of(jg, i, j, m))
                                dve.wait_ge(ps_free[gslot], guses + 1)
                                wait(dve, hl_done, h0 + 4 * i + max(n - 1, 0))
                                nc.vector.tensor_tensor(halves(TMP[:, m, 0:width]), halves(SG[:, m, 0:width]),
                                                        acc(slot, width), ALU.mult).then_inc(ps_free[slot], 1)
                                dve.wait_ge(hh_done, h0 + 4 * i + n + 1)
                                nc.vector.tensor_tensor(HL[:, bass.ds(4 * i + n, 1), 0:width], TMP[:, m:m + 1, 0:width],
                                                        HH[:, bass.ds(4 * i + n, 1), 0:width].bitcast(F32),
                                                        ALU.subtract).then_inc(hl_done, 1)
                    each(dve, jg, body, peel=int(h0 == 0))

                    squares = part and after is not None
                    if squares:
                        nc.vector.memset(SUMSQ[:, 0:width], 0.0).then_inc(sum_zeroed, 1)
                        dve.wait_ge(sum_zeroed, number + 1)

                    def body(i, j):
                        if j % 2:
                            for m in range(2):
                                k = 4 * i + (j - 1 + m)
                                slot, uses = chunk_of(jd, i, j, m)
                                dve.wait_ge(done, tick_of(jd, i, j, m))
                                nc.vector.scalar_tensor_tensor(out=res_chunk(k, cols), in0=acc(slot, width), scalar=0.5,
                                                               in1=res_chunk(k, cols), op0=ALU.mult,
                                                               op1=ALU.add).then_inc(ps_free[slot], 1)
                            if squares:
                                for m in range(2):
                                    add_square(4 * i + (norms[after][3] + j - 1 + m), False, width, m)
                    each(dve, jd, body)

            spread("ffn1")
            apply("ffn1", 5 * KC)
            ffn_dve("ffn1", 0, "mix")

            dve.wait_ge(hl_done, 22)
            spread("mix")
            apply("mix", 6 * KC)
            q0 = norms["cq"][3]
            add_square(q0, True, SEQ, 0)
            add_square(q0 + 1, False, SEQ, 1)
            dve.wait_ge(done, at_cq[2] + 1)
            for a in range(2):
                q = norms["ckv"][3] + a
                dve.wait_ge(sq_done, q + 1)
                nc.vector.tensor_copy(SUMSQ[:, a * HALF:(a + 1) * HALF], SQ[:, a, 0:HALF]).then_inc(sq_added, 1)
            dve.wait_ge(ul_done, applied["cq"])
            spread("cq")
            dve.wait_ge(ps_free[chunk_of(j_cq, 0, 0, 1)[0]], chunk_of(j_cq, 0, 0, 1)[1] + 1)
            apply("cq", QN_ROW, CQF, CQL, CQH, 2)
            dve.wait_ge(ul_done, applied["ckv"])
            spread("ckv")
            dve.wait_ge(ps_free[chunk_of(j_kvm, 0, 0, 0)[0]], chunk_of(j_kvm, 0, 0, 0)[1] + 1)
            apply("ckv", KVN_ROW, CKF, CKL, CKH, 1)
            dve.wait_ge(s_mtab, 16)
            dve.wait_ge(ps_free[chunk_of(j_kvm, 0, 0, 1)[0]], chunk_of(j_kvm, 0, 0, 1)[1] + 1)
            dve.wait_ge(ul_done, applied["ffn2"])
            dve.wait_ge(done, at_ckv[2] + 2)
            nc.vector.tensor_tensor(TMP[0:32, 0, :], MISC[0:32, :], MTAB[0:32, 0, :], ALU.mult).then_inc(kr_done, 1)
            nc.vector.tensor_tensor(SG[0:32, 0, :], MISC[32:64, :], MTAB[32:64, 1, :], ALU.mult).then_inc(kr_done, 1)
            dve.wait_ge(kr_done, 2)
            nc.vector.tensor_tensor(KCAT[64:96, 0, :], TMP[0:32, 0, :], SG[0:32, 0, :], ALU.add).then_inc(kr_done, 1)
            dve.wait_ge(kr_done, 3)
            nc.vector.tensor_copy(KCAT[64:96, 1:HEADS, :], KCAT[64:96, 0:1, :].to_broadcast([32, HEADS - 1, TOK])).then_inc(kr_done, 1)
            scale = float(MLA_NOPE + MLA_ROPE) ** -0.5
            for r in range(2):
                c = j_uq.chunk0 + 2 * r
                sa, sb = c % SLOTS, (c + 1) % SLOTS
                dve.wait_ge(done, j_uq.tick0 + 2 * r + 2)
                if r:
                    dve.wait_ge(qr_done, 4)
                nc.vector.scalar_tensor_tensor(out=TMP[:, 0, 0:SEQ], in0=acc(sa, SEQ), scalar=scale,
                                               in1=MTAB[:, 0, META:TOK], op0=ALU.mult, op1=ALU.mult).then_inc(ps_free[sa], 1)
                nc.vector.scalar_tensor_tensor(out=SG[:, 0, 0:SEQ], in0=acc(sb, SEQ), scalar=scale,
                                               in1=MTAB[:, 1, META:TOK], op0=ALU.mult, op1=ALU.mult).then_inc(ps_free[sb], 1)
                dve.wait_ge(ps_free[sa], c // SLOTS + 1)
                dve.wait_ge(ps_free[sb], (c + 1) // SLOTS + 1)
                for g in range(4):
                    q = slice(32 * g, 32 * g + 32)
                    nc.vector.tensor_tensor(QC[64:96, 4 * r + g, :], TMP[q, 0, 0:SEQ], SG[q, 0, 0:SEQ],
                                            ALU.add).then_inc(qr_done, 1)
            for s in range(HEADS * NT + MLA_LAG):
                if s < HEADS * NT:
                    b = s % NT
                    n = META + P * (b + 1)
                    dve.wait_ge(ma_s, s + 1)
                    if s >= 2:
                        dve.wait_ge(ma_e, s - 1)
                    k = 2 * (s % 2)
                    if n <= 512:
                        nc.vector.tensor_reduce(NEGM2[:, s % 2:s % 2 + 1], PS[:, k, 0:n], AX.X, ALU.max,
                                                negate=True).then_inc(ma_max, 1)
                    else:
                        nc.vector.tensor_reduce(NEGM2[:, s % 2:s % 2 + 1], PS[:, k:k + 2, 0:HALF], AX.XY, ALU.max,
                                                negate=True).then_inc(ma_max, 1)
                if s >= 7 and (s - 7) % NT == 0 and (s - 7) // NT < HEADS:
                    h = (s - 7) // NT
                    if h >= 4:
                        dve.wait_ge(ma_on, h - 3)
                    dve.wait_ge(ma_e, NT * (h + 1))
                    nc.vector.reciprocal(RSUM2[:, h % 4, :], ESUM2[:, h % 4, :]).then_inc(ma_rs, 1)
                    dve.wait_ge(ma_rs, h + 1)
                    dve.wait_ge(ma_pv, NT * (h + 1))
                    pair = h // 2
                    if pair >= 2:
                        dve.wait_ge(ma_t, mla_turn_no["pair", pair - 2] + 1)
                    nc.vector.tensor_tensor(MON[:, pair % 2, :, 64 * (h % 2):64 * (h % 2) + 64],
                                            PS[:, 6, 0:256].rearrange("p (t n) -> p t n", t=NT),
                                            RSUM2[:, h % 4, :].unsqueeze(2).to_broadcast([P, NT, 64]),
                                            ALU.mult).then_inc(ma_on, 1)

            dve.wait_ge(pre_zero, 1)
            dve.wait_ge(qr_done, 8)
            for n in range(12):
                slot, uses = chunk_of(j_gqkv, 0, n // 2, n % 2)
                dve.wait_ge(ps_free[slot], uses + 1)
                if n >= 2:
                    dve.wait_ge(conv_done, n - 1)
                for tap in range(CONV):
                    x = PRE[:, n % 2, tap:tap + TOK]
                    c = CONV_ROW + 12 * tap + n
                    o = TMP[:, n % 2, :]
                    if tap:
                        dve.wait_ge(tap_done, 4 * n + tap)
                        nc.vector.scalar_tensor_tensor(out=o, in0=x, scalar=GAINS[:, c:c + 1], in1=o, op0=ALU.mult,
                                                       op1=ALU.add).then_inc(tap_done, 1)
                    else:
                        nc.vector.tensor_scalar(o, x, GAINS[:, c:c + 1], None, ALU.mult).then_inc(tap_done, 1)
            slot = at_gss[1] % SLOTS
            dve.wait_ge(ss_mm, 8)
            nc.vector.tensor_scalar(RN[:, 1:NT + 1, :], PS[:, 2 * slot, 16:80].rearrange("p (t n) -> p t n", t=NT), EPS, None,
                                    ALU.add)
            nc.vector.tensor_scalar(RN[0:META, 0, 8:16], PS[0:META, 2 * slot, 8:16], EPS, None, ALU.add).then_inc(ss_done, 1)
            dve.wait_ge(ss_done, 1)
            nc.vector.tensor_copy(STAT[0:META, 0, 7:8], PS[0:META, 2 * slot, 8:9]).then_inc(ps_free[slot], 1)
            wide = [P, NT + 1, HEADS]
            dve.wait_ge(g_act, 2)
            nc.vector.tensor_tensor(XA[:, :, :], BA[:, :, 8:16], PS[:, 1, 8:16].unsqueeze(1).to_broadcast(wide),
                                    ALU.add).then_inc(g_dve, 1)
            dve.wait_ge(g_dve, 1)
            nc.vector.tensor_scalar(RELU[:, :, :], XA[:, :, :], 0.0, None, ALU.max).then_inc(g_dve, 1)
            dve.wait_ge(g_dve, 2)
            nc.vector.scalar_tensor_tensor(out=XA[:, :, :], in0=RELU[:, :, :], scalar=-2.0, in1=XA[:, :, :], op0=ALU.mult,
                                           op1=ALU.add).then_inc(g_dve, 1)
            dve.wait_ge(g_act, 3)
            nc.vector.tensor_scalar(BETA[:, :, :], BETA[:, :, :], 1.0, None, ALU.add).then_inc(g_dve, 1)
            dve.wait_ge(g_dve, 4)
            nc.vector.reciprocal(BETA[:, :, :], BETA[:, :, :]).then_inc(g_dve, 1)
            dve.wait_ge(g_act, 4)
            nc.vector.tensor_scalar(EN[:, :, :], EN[:, :, :], 1.0, None, ALU.add).then_inc(g_dve, 1)
            dve.wait_ge(g_act, 5)
            nc.vector.tensor_tensor(LNE[:, :, :], LNE[:, :, :], RELU[:, :, :], ALU.add).then_inc(sp_done, 1)
            dve.wait_ge(sp_done, 1)
            nc.vector.scalar_tensor_tensor(out=GG[:, :, :], in0=LNE[:, :, :], scalar=-1.0,
                                           in1=EAL[:, :].unsqueeze(1).to_broadcast(wide), op0=ALU.mult,
                                           op1=ALU.mult).then_inc(g_dve, 1)
            dve.wait_ge(gexp_done, 1)
            for s, n in enumerate(uses_before(j_z.end[1])):
                dve.wait_ge(ps_free[s], n)
            dve.wait_ge(rn_done, 3)

            RQ, RK = RN[:, :, 0:8], RN[:, :, 8:16]
            main, meta = (slice(0, P), slice(1, NT + 1)), (slice(0, META), slice(0, 1))

            def gexp(first, where):
                if where is main:
                    return GEXP[:, 32 * first:32 * first + 32].rearrange("p (t n) -> p t n", t=NT)
                return GEXP[0:META, 96 + 8 * first:104 + 8 * first].unsqueeze(1)

            nc.vector.tensor_scalar(FQ[:, 1:NT + 1, :], RQ[:, 1:NT + 1, :], GDN_D ** -0.5, None, ALU.mult).then_inc(fac_done, 1)
            for r, ts in (main, meta):
                nc.vector.tensor_tensor(FKB[r, ts, :], RK[r, ts, :], BETA[r, ts, :], ALU.mult).then_inc(fac_done, 1)
            for where in (main, meta):
                r, ts = where
                nc.vector.tensor_tensor(FKD[r, ts, :], RK[r, ts, :], gexp(1, where), ALU.mult).then_inc(fac_done, 1)
            dve.wait_ge(fac_done, 3)
            nc.vector.tensor_tensor(FQG[:, 1:NT + 1, :], FQ[:, 1:NT + 1, :], gexp(0, main), ALU.mult).then_inc(fac_done, 1)
            for where in (main, meta):
                r, ts = where
                nc.vector.tensor_tensor(FKBG[r, ts, :], FKB[r, ts, :], gexp(0, where), ALU.mult).then_inc(fac_done, 1)
            dve.wait_ge(fac_done, N_FACTORS)

            def scaled_rows(t):
                w, _ = tile(t)
                dve.wait_ge(g_act, ACT_AT[t, "rows"])
                if t:
                    dve.wait_ge(g_pe, PE_AT[t - 1, ("state", 0 if t == 1 else 1)])
                    if t > 1:
                        dve.wait_ge(g_pe, PE_AT[t - 1, ("out", 1)])
                todo = [("kb", KB, 1, FKB), ("nk", NK, 1, RK)]
                if t:
                    todo += [("nq", NQ, 0, FQ), ("qg", QG, 0, FQG)]
                for name, dst, part, f in todo:
                    nc.vector.tensor_tensor(by_head(dst[0:w, :]), by_head(ROWQ[0:w, part, :]), over_heads(f[0:w, t, :], w, GDN_D),
                                            ALU.mult).then_inc(g_dve, one("dve", t, name))

            scaled_rows(0)
            for t in range(NT + 1):
                w, cols = tile(t)
                if t:
                    dve.wait_ge(g_pe, PE_AT[t, "turn_q"])
                    for bank, dst in ((4, QT), (6, QGT)):
                        last = nc.vector.tensor_copy(dst[:, :, :], PS[:, bank, :].rearrange("p (h c) -> p h c", h=4))
                    last.then_inc(g_dve, one("dve", t, "turned_q"))
                dve.wait_ge(g_act, ACT_AT[t, "decay"])
                dve.wait_ge(g_pe, PE_AT[t, "kk"])

                def scores(dst, bank, b, factor):
                    return nc.vector.tensor_tensor(every_other(dst[0:w, :, 0:w], b),
                                                   PS[0:w, bank, 0:4 * w].rearrange("p (h c) -> p h c", h=4),
                                                   factor, ALU.mult)
                for b in range(2):
                    last = scores(LT, (2, 7)[b], b, every_other(DEC[0:w, :, 0:w], b))
                last.then_inc(g_dve, one("dve", t, "lt"))
                dve.wait_ge(g_dve, DVE_AT[t, "lt"])
                nc.vector.tensor_tensor(TIT[0:w, :, 0:w], LT[0:w, :, 0:w], TRI[0:w, 2:3, 0:w].to_broadcast([w, HEADS, w]),
                                        ALU.mult).then_inc(g_dve, one("dve", t, "e1a"))
                dve.wait_ge(g_dve, DVE_AT[t, "e1a"])
                nc.vector.tensor_tensor(TIT[0:w, :, 0:w], IDENT[0:w, 0:w].unsqueeze(1).to_broadcast([w, HEADS, w]),
                                        TIT[0:w, :, 0:w], ALU.subtract).then_inc(g_dve, one("dve", t, "e1b"))
                if t:
                    dve.wait_ge(g_pe, PE_AT[t, "kq"])
                    for b in range(2):
                        last = scores(AT, 3 + b, b, TRI[0:w, 0:1, 0:w].to_broadcast([w, 4, w]))
                    last.then_inc(g_dve, one("dve", t, "at"))
                for n, s in enumerate(levels(t)):
                    for g in range(2):
                        hs = slice(4 * g, 4 * g + 4)
                        dve.wait_ge(g_pe, PE_AT[t, ("x", s, g)])
                        if n == 0:
                            dve.wait_ge(g_pool, POOL_AT[t, "vb"])
                            dve.wait_ge(g_dve, DVE_AT[t, "qg" if t else "nk"])
                        nc.vector.tensor_tensor(XX[0:w, hs, 0:w], PS[0:w, g, 0:4 * w].rearrange("p (h c) -> p h c", h=4),
                                                TRI[0:w, 3 + n:4 + n, 0:w].to_broadcast([w, 4, w]),
                                                ALU.mult).then_inc(g_dve, one("dve", t, ("x", s, g)))
                    for g in range(2):
                        hs = slice(4 * g, 4 * g + 4)
                        dve.wait_ge(g_pe, PE_AT[t, ("y", s, g)])
                        for name, dst, bank, which in (("d", TI, (2, 7)[g], 0), ("e", TIT, 3 + g, 1)):
                            if name == "d" and s == levels(t)[-1]:
                                continue
                            if n == 0 and name == "d":
                                dve.wait_ge(g_act, ACT_AT[t, "d1"])
                            if n:
                                dve.wait_ge(g_dve, DVE_AT[t, (name, levels(t)[n - 1], g)])
                            o = joined(dst[0:w, hs, 0:w], s, which)
                            y = PS[0:w, bank, 0:2 * w].rearrange("p (h b s) -> p h b s", h=4, s=s)
                            nc.vector.tensor_tensor(o, o, y, ALU.subtract).then_inc(g_dve, one("dve", t, (name, s, g)))
                for c in range(2 if t else 1):
                    r = slice(64 * c, 64 * c + 64)
                    no = 2 * (t - 1) + c + 1 if t else 0
                    if t:
                        dve.wait_ge(g_act, ACT_AT[t, "uw"])
                        dve.wait_ge(g_pe, PE_AT[t, ("ws", c)])
                        for par in range(2):
                            last = nc.vector.tensor_tensor(
                                every_other(by_head(VN[r, :]), par), every_other(by_head(UU[r, :]), par),
                                PS[r, 3 * par, 0:4 * GDN_D].rearrange("p (h n) -> p h n", h=4), ALU.subtract)
                        last.then_inc(g_dve, one("dve", t, ("vn", c)))
                        col = 64 + 16 * c + 4 * (t - 1)
                        dve.wait_ge(g_dve, DVE_AT[t if c else t - 1, ("s", 0 if c or t == 1 else 1)])
                        nc.vector.tensor_tensor(SS[:, :, :], ST[:, (no - 1) % 2, :, :],
                                                GEXP[:, col:col + 4].unsqueeze(2).to_broadcast([P, 4, GDN_D]),
                                                ALU.mult).then_inc(g_dve, one("dve", t, ("sd", c)))
                        dve.wait_ge(g_dve, DVE_AT[t, ("sd", c)])
                    dve.wait_ge(g_pe, PE_AT[t, ("state", c)])
                    new = PS[:, 1, 0:4 * GDN_D].rearrange("p (h n) -> p h n", h=4)
                    if t:
                        nc.vector.tensor_tensor(ST[:, no % 2, :, :], SS[:, :, :], new, ALU.add).then_inc(
                            g_dve, one("dve", t, ("s", c)))
                    else:
                        nc.vector.tensor_copy(ST[:, no % 2, :, :], new).then_inc(g_dve, one("dve", t, ("s", c)))
                if t:
                    dve.wait_ge(g_pe, PE_AT[t, ("out", 1)])
                    for par in range(2):
                        nc.vector.tensor_copy(every_other(by_head(GON[:, :]), par),
                                              PS[:, 4 + par, 0:4 * GDN_D].rearrange("p (h n) -> p h n", h=4)).then_inc(
                                                  g_dve, one("dve", t, ("out_inter", par)))
                    dve.wait_ge(g_dve, DVE_AT[t, ("out_inter", 1)])
                    nc.vector.tensor_tensor(GON[:, :], GON[:, :], PS[:, 2, :], ALU.add).then_inc(
                        g_dve, one("dve", t, "out_join"))
                    dve.wait_ge(g_act, ACT_AT[t, "out_square"])
                    nc.vector.tensor_reduce(OSS[:, :], by_head(GSQ[:, 1, :]), AX.X, ALU.add).then_inc(
                        g_dve, one("dve", t, "out_sum"))
                    dve.wait_ge(g_dve, DVE_AT[t, "out_sum"])
                    nc.vector.tensor_scalar(OSS[:, :], OSS[:, :], 1.0 / GDN_D, EPS, ALU.mult, ALU.add).then_inc(
                        g_dve, one("dve", t, "out_eps"))
                if t < NT:
                    scaled_rows(t + 1)
                if t:
                    dve.wait_ge(g_pool, POOL_AT[t, "out_rnorm"])
                    nc.vector.tensor_tensor(by_head(GON[:, :]), by_head(GON[:, :]), over_heads(ORN[:, :], P, GDN_D),
                                            ALU.mult).then_inc(g_dve, one("dve", t, "out_norm"))
                    dve.wait_ge(g_pe, PE_AT[t, "turn_out"])
                    o = ZS[:, :, P * (t - 1):P * t]
                    nc.vector.scalar_tensor_tensor(out=o, in0=PS[:, 7, :].rearrange("p (h c) -> p h c", h=4),
                                                   scalar=GAINS[:, GDN_ROW:GDN_ROW + 1], in1=o, op0=ALU.mult,
                                                   op1=ALU.mult).then_inc(g_dve, one("dve", t, "out_gate"))

            for src, hi_part, lo_part, hi_sem, lo_sem in ((OMF, OMH, OML, oh_done, ol_done),
                                                          (ZS, GOH, GOL, gh_done, gl_done)):
                for k in range(4):
                    dve.wait_ge(hi_sem, k + 1)
                    nc.vector.tensor_tensor(lo_part[:, k, :], src[:, k, :], hi_part[:, k, :].bitcast(F32),
                                            ALU.subtract).then_inc(lo_sem, 1)
            for n in range(4):
                for m in range(2):
                    for b in range(2):
                        c = j_merge.chunk0 + 8 * n + 4 + 2 * m + b
                        gate = j_merge.chunk0 + 8 * n + 2 * b + m
                        dve.wait_ge(ps_free[gate % SLOTS], gate // SLOTS + 1)
                        dve.wait_ge(done, j_merge.tick0 + 8 * n + 4 + 2 * m + b + 1)
                        nc.vector.tensor_tensor(GATE[:, b, m, :], GATE[:, b, m, :], acc(c % SLOTS, SEQ),
                                                ALU.mult).then_inc(ps_free[c % SLOTS], 1)
                    for b in range(2):
                        c = j_merge.chunk0 + 8 * n + 4 + 2 * m + b
                        dve.wait_ge(ps_free[c % SLOTS], c // SLOTS + 1)
                    nc.vector.tensor_tensor(GATE[:, 0, m, :], GATE[:, 0, m, :], GATE[:, 1, m, :],
                                            ALU.add).then_inc(merged_done, 1)
                for m in range(2):
                    dve.wait_ge(mh_done, 2 * n + m + 1)
                    nc.vector.tensor_tensor(ML[:, 2 * n + m, :], GATE[:, 0, m, :], MH[:, 2 * n + m, :].bitcast(F32),
                                            ALU.subtract).then_inc(ml_done, 1)
            for k in range(KC):
                slot, uses = chunk_of(j_wout, 0, k // 2, k % 2)
                dve.wait_ge(done, tick_of(j_wout, 0, k // 2, k % 2))
                nc.vector.tensor_tensor(RES[:, k, SEQ_COLS], RES[:, k, SEQ_COLS], acc(slot, SEQ), ALU.add).then_inc(
                    ps_free[slot], 1)
                if k:
                    add_square(norms["ffn2"][3] + k - 1, k == 1, SEQ, (k - 1) % 2)
            add_square(norms["ffn2"][3] + KC - 1, False, SEQ, 1)
            spread("ffn2")
            apply("ffn2", 7 * KC)
            ffn_dve("ffn2", 1, "final")
            dve.wait_ge(hl_done, 44)
            spread("final")
            slot = (at_final[1] + 1) % SLOTS
            dve.wait_ge(done, at_final[2] + 2)
            for k in range(KC):
                nc.vector.scalar_tensor_tensor(out=FN[:, k, :], in0=RES[:, k, SEQ_COLS],
                                               scalar=GAINS[:, 8 * KC + k:8 * KC + k + 1], in1=acc(slot, SEQ),
                                               op0=ALU.mult, op1=ALU.mult).then_inc(f_done, 1)
            nc.vector.tensor_copy(STAT[:, 0, 7:8], PS[:, 2 * slot, 0:1]).then_inc(ps_free[slot], 1)
            for t in range(1, NT, 2):
                slot = (at_rows[1] + t) % SLOTS
                dve.wait_ge(done, at_rows[2] + t + 1)
                nc.vector.tensor_copy(OUTR[:, t, :], PS[:, 2 * slot:2 * slot + 2, :].rearrange("p a n -> p (a n)")).then_inc(
                    ps_free[slot], 1)

        @block.tensor
        def _(pe):
            def mm(o, a, b, start=True, stop=True, **kw):
                return nc.tensor.matmul(o, a, b, start=start, stop=stop, **kw)

            def turn(o, x, n):
                return nc.tensor.transpose(o, x, IDENT[0:n, 0:n])

            def project(jb, xh, xl, cols, kc=KC, k_ready=None):
                width = width_of(cols)
                parts = [cols] if width <= 512 else [slice(0, HALF), slice(HALF, TOK)]

                def body(i, j):
                    u = jb.unit0 + j
                    b = u % SPLITS
                    pe.wait_ge(lo_done, 4 * i + u + 1)
                    f = j % jb.fold
                    slots = [chunk_of(jb, i, j, m) for m in range(2)]
                    if j == 0 and k_ready is not None and k_ready[0] is ul_done:
                        order = [(m, k) for k in range(kc) for m in range(2)]
                    else:
                        order = [(m, k) for m in range(2) for k in range(kc)]
                    for m, k in order:
                        slot, uses = slots[m]
                        if f == 0 and k == 0:
                            slot_free(pe, slot, uses)
                        kx = f * kc + k
                        wcols = slice(k * UCOL + m * P, k * UCOL + (m + 1) * P)
                        if k_ready is not None and m == 0:
                            pe.wait_ge(k_ready[0], k_ready[1] + kx + 1)
                        first, final = kx == 0, f == jb.fold - 1 and k == kc - 1
                        for w, x, pss in ((WH, xh, 0), (WH, xl, 1), (WL, xh, 2)):
                            for a, part in enumerate(parts):
                                o = PS[:, 2 * slot + a, 0:part.stop - part.start]
                                last = mm(o, w[:, b, wcols], x[:, kx, part], start=first and pss == 0,
                                          stop=final and pss == 2)
                        if k == kc - 1:
                            last.then_inc(done, 1)
                each(pe, jb, body)

            def project_rows(jb, xh, xl, col0):
                def body(i, j):
                    u = jb.unit0 + j
                    b = u % SPLITS
                    pe.wait_ge(lo_done, 4 * i + u + 1)
                    for m in range(2):
                        slot, uses = chunk_of(jb, i, j, m)
                        slot_free(pe, slot, uses)
                        for t in range(2):
                            c = slice(col0 + (2 * m + t) * P, col0 + (2 * m + t + 1) * P)
                            o = PS[:, 2 * slot, t * UCOL:(t + 1) * UCOL]
                            for k in range(KC):
                                w = slice(k * UCOL, (k + 1) * UCOL)
                                mm(o, xh[:, k, c], WH[:, b, w], start=k == 0, stop=False)
                                mm(o, xh[:, k, c], WL[:, b, w], start=False, stop=False)
                                last = mm(o, xl[:, k, c], WH[:, b, w], start=False, stop=k == KC - 1)
                        last.then_inc(done, 1)
                each(pe, jb, body)

            def norm_products(name):
                n, (_, chunk, tick), cols, before, squares, _ = norms[name]
                k, w = token_tiles(width_of(cols))
                slot = chunk % SLOTS
                slot_free(pe, slot, chunk // SLOTS)
                if name in BY_CHUNK:
                    for q in range(squares):
                        pe.wait_ge(sq_done, before + q + 1)
                        for t in range(k):
                            last = mm(PS[0:w, 2 * slot, KC * t + q:KC * t + q + 1], SQ[:, (before + q) % 2, t * w:(t + 1) * w],
                                      ONES[:, 0:1])
                            if t == (k - 2 if q == squares - 1 else k - 1):
                                last.then_inc(sq_added, 1)
                else:
                    pe.wait_ge(sq_added, before + squares)
                    for t in range(k):
                        last = mm(PS[0:w, 2 * slot, t:t + 1], SUMSQ[:, t * w:(t + 1) * w], ONES[:, 0:1])
                last.then_inc(done, 1)
                slot = (chunk + 1) % SLOTS
                slot_free(pe, slot, (chunk + 1) // SLOTS)
                pe.wait_ge(diag_done, n + 1)
                width = width_of(cols)
                if width <= 512:
                    last = mm(PS[:, 2 * slot, 0:width], ONES[0:w, :], DIAG[0:w, 0:width])
                else:
                    for a in range(2):
                        last = mm(PS[:, 2 * slot + a, 0:HALF], ONES[0:w, :], DIAG[0:w, a * HALF:(a + 1) * HALF])
                last.then_inc(done, 1)

            pe.wait_ge(s_ident, 16)
            pe.wait_ge(s_ones, 1)
            pe.wait_ge(s_x, 16)
            pe.wait_ge(s_meta, 16)
            for k in range(KC):
                c = at_x[1] + k
                slot_free(pe, c % SLOTS, c // SLOTS)
                for t in range(NT):
                    last = turn(PS[:, 2 * (c % SLOTS), t * P:(t + 1) * P], X0[:, t, k * P:(k + 1) * P], P)
                last.then_inc(done, 1)
            c = at_x[1] + KC
            slot_free(pe, c % SLOTS, c // SLOTS)
            for k in range(KC):
                turn(PS[:, 2 * (c % SLOTS), k * META:(k + 1) * META], M0[:, k * P:(k + 1) * P], META)
            pe.wait_ge(s_gain, 16 * (len(GAIN_ROWS) + len(other_rows(A)) + 1))
            last = turn(PS[:, 2 * (c % SLOTS), P:P + N_ROWS], GROW[0:N_ROWS, :], N_ROWS)
            last.then_inc(done, 1)
            norm_products("norm0")
            project(j_ret_qk, UH, UL, SEQ_COLS, k_ready=(ul_done, 0))
            project_rows(j_ret_v, UH, UL, META)

            for s in range(SLOTS):
                pe.wait_ge(ps_free[s], len([c for c in range(j_ret_v.end[1]) if c % SLOTS == s]))
            pe.wait_ge(rope_done, 2 * HEADS)
            for h in range(HEADS + 3):
                if h < HEADS:
                    if h:
                        pe.wait_ge(ra_m, NT * h)
                    for b in range(NT):
                        bank, first = SCORE_AT[b]
                        last = mm(PS[:, bank, first:first + SEQ - P * b], QK[:, 2 * h + 1, P * b:P * (b + 1)],
                                  QK[:, 2 * h, P * b:SEQ])
                    last.then_inc(ra_s, 1)
                for what, g, e in (("turn", h - 3, 1), ("sum", h - 1, 0), ("turn", h - 2, 0)):
                    if not 0 <= g < HEADS:
                        continue
                    if what == "turn":
                        pe.wait_ge(ra_on, g + 1)
                        if 2 * g + e:
                            pe.wait_ge(ra_e, 2 * g + e)
                        for t in range(NT):
                            last = turn(PS[:, 7, P * t:P * (t + 1)], ON[:, g % 2, t, P * e:P * (e + 1)], P)
                        last.then_inc(ra_t, 1)
                        continue
                    pe.wait_ge(ra_m, NT * (g + 1))
                    if g >= 2:
                        pe.wait_ge(ra_on, g - 1)
                    for t in range(NT):
                        for b in range(t + 1):
                            o = OFF[b] + P * (t - b)
                            last = mm(PS[:, 3 + 2 * (g % 2) + t // 2, RET_DV * (t % 2):RET_DV * (t % 2 + 1)],
                                      SC[:, g % 2, o:o + P], V[:, b, RET_DV * g:RET_DV * (g + 1)],
                                      start=b == 0, stop=b == t)
                    last.then_inc(ra_pv, 1)
            pe.wait_ge(ra_e, 2 * HEADS)
            project(j_ret_gate, UH, UL, SEQ_COLS)
            project(j_ret_out, YH, YL, PLAIN, k_ready=(yl_done, 0))
            norm_products("post0")
            norm_products("norm1")
            project(j_kv_k, UH, UL, SEQ_COLS, k_ready=(ul_done, applied["norm1"]))
            project_rows(j_kv_v, UH, UL, META)
            project(j_diff_q, UH, UL, SEQ_COLS, k_ready=(ul_done, applied["norm1q"]))

            pe.wait_ge(lam_step, 3)
            c = at_lam[1]
            slot_free(pe, c % SLOTS, c // SLOTS)
            mm(PS[:, 2 * (c % SLOTS), 0:1], ONES[0:1, :], LAMS[0:1, 4:5]).then_inc(done, 1)
            pe.wait_ge(s_rows, 3)
            for s, n in enumerate(uses_before(at_lam[1] + 1)):
                pe.wait_ge(ps_free[s], n)
            pe.wait_ge(rope_done, 32)
            for s in range(ITEMS + HEAD_LAG):
                if s < 4 * HEADS:
                    h, b = s // NT, s % NT
                    n = P * (b + 1)
                    if s >= 2:
                        pe.wait_ge(da_e, 2 * (s - 1))
                    for t in range(2):
                        r = slice(64 * t, 64 * t + 64)
                        o = PS[:, 2 * (s % 2) + t, :]
                        mm(o[:, 0:n], DQK[r, h, P * b:P * (b + 1)], DQK[r, HEADS + h, 0:n], start=True, stop=False)
                        last = mm(o[:, n - 64:n], ROWS[:, 0:P], ROWS[:, P:P + 64], start=False, stop=True)
                    last.then_inc(da_s, 1)
                for kind, g in [x for x in (("item", s - 2), ("head", (s - HEAD_LAG) / NT)) if x in turn_no]:
                    g = int(g)
                    no = turn_no[kind, g]
                    if no >= 2:
                        pe.wait_ge(da_wt, no - 1)
                    if kind == "item":
                        pe.wait_ge(da_w, g + 1)
                        for c in range(g % NT + 1):
                            last = turn(PS[:, 4 + no % 2, P * c:P * (c + 1)], DW[:, g % 2, P * c:P * (c + 1)], P)
                    else:
                        pe.wait_ge(da_on, 2 * g + 2)
                        for c in range(NT):
                            last = turn(PS[:, 4 + no % 2, P * c:P * (c + 1)], DON[:, g % 2, c, :], P)
                    last.then_inc(da_t, 1)
                if 3 <= s <= ITEMS + 2:
                    g = s - 3
                    h, b = g // NT, g % NT
                    pe.wait_ge(da_wt, turn_no["item", g] + 1)
                    if b == 0 and h >= 2:
                        pe.wait_ge(da_on, 2 * (h - 2) + 1)
                    for c in range(b + 1):
                        last = mm(PS[:, 6 + h % 2, P * b:P * (b + 1)], DWT[:, g % 2, P * c:P * (c + 1)],
                                  DV[:, c, P * h:P * (h + 1)], start=c == 0, stop=c == b)
                    last.then_inc(da_pv, 1)
            pe.wait_ge(da_wt, len(turns))
            project(j_diff_gate, UH, UL, SEQ_COLS)
            project(j_diff_out, DYH, DYL, PLAIN, k_ready=(yl_done, 16))
            norm_products("post1")

            def ffn_pe(name, number):
                cols = norms[name][2]
                hcols = ALL_COLS if cols == ALL_COLS else PLAIN
                for part, (jg, jd) in enumerate(ffns[name]):
                    project(jg, UH, UL, cols, k_ready=(ul_done, applied[name]))
                    project(jd, HH, HL, hcols, kc=FFN_PARTS[part] // 2,
                            k_ready=(hl_done, 22 * number + (FFN_PARTS[0] if part else 0)))

            norm_products("ffn1")
            ffn_pe("ffn1", 0)

            norm_products("mix")
            project(j_cq, UH, UL, SEQ_COLS, k_ready=(ul_done, applied["mix"]))
            project(j_kvm, UH, UL, ALL_COLS)
            norm_products("cq")
            norm_products("ckv")

            def three(o, wh, wl, xh, xl, first, final):
                mm(o, wh, xh, start=first, stop=False)
                mm(o, wh, xl, start=False, stop=False)
                return mm(o, wl, xh, start=False, stop=final)

            b = j_uq.unit0 % SPLITS
            pe.wait_ge(lo_done, j_uq.unit0 + 1)
            pe.wait_ge(ul_done, applied["cq"] + 2)
            for n, off in enumerate((512, 768, 640, 896, 0, 128, 256, 384)):
                c = j_uq.chunk0 + n
                slot = c % SLOTS
                slot_free(pe, slot, c // SLOTS)
                for k in range(2):
                    w = slice(1024 * k + off, 1024 * k + off + P)
                    last = three(PS[:, 2 * slot, :], WH[:, b, w], WL[:, b, w], CQH[:, k, :], CQL[:, k, :],
                                 k == 0, k == 1)
                last.then_inc(done, 1)
            b = j_ukv.unit0 % SPLITS
            pe.wait_ge(lo_done, j_ukv.unit0 + 1)
            pe.wait_ge(ul_done, applied["ckv"] + 1)
            for n in range(4):
                c = j_ukv.chunk0 + n
                slot = c % SLOTS
                slot_free(pe, slot, c // SLOTS)
                w = slice(P * n, P * (n + 1))
                for a in range(2):
                    x = slice(a * HALF, (a + 1) * HALF)
                    last = three(PS[:, 2 * slot + a, 0:HALF], WH[:, b, w], WL[:, b, w], CKH[:, 0, x], CKL[:, 0, x],
                                 True, True)
                last.then_inc(done, 1)
            for t in range(NT + 1):
                c = j_ukv.chunk0 + 4 + t
                slot = c % SLOTS
                slot_free(pe, slot, c // SLOTS)
                x = slice(0, META) if t == 0 else slice(META + P * (t - 1), META + P * t)
                w = slice(512, 1024)
                o = PS[0:x.stop - x.start, 2 * slot, :]
                mm(o, CKH[:, 0, x], WH[:, b, w], start=True, stop=False)
                mm(o, CKL[:, 0, x], WH[:, b, w], start=False, stop=False)
                mm(o, CKH[:, 0, x], WL[:, b, w], start=False, stop=True).then_inc(done, 1)

            for s, n in enumerate(uses_before(j_ukv.end[1])):
                pe.wait_ge(ps_free[s], n)
            pe.wait_ge(kr_done, 4)
            pe.wait_ge(qr_done, 8)
            pe.wait_ge(s_cmask, 16)
            R = MLA_NOPE + MLA_ROPE
            for s in range(HEADS * NT + MLA_LAG):
                if s < HEADS * NT:
                    h, b = s // NT, s % NT
                    n = META + P * (b + 1)
                    if s >= 2:
                        pe.wait_ge(ma_e, s - 1)
                    k = 2 * (s % 2)
                    q = QC[0:R, h, P * b:P * (b + 1)]
                    if n <= 512:
                        mm(PS[:, k, 0:n], q, KCAT[0:R, h, 0:n], start=True, stop=False)
                        o = PS[:, k, n - P:n]
                    else:
                        mm(PS[:, k, 0:HALF], q, KCAT[0:R, h, 0:HALF])
                        mm(PS[:, k + 1, 0:HALF], q, KCAT[0:R, h, HALF:TOK], start=True, stop=False)
                        o = PS[:, k + 1, HALF - P:HALF]
                    mm(o, IDENT[:, :], CMASK[:, :], start=False, stop=True).then_inc(ma_s, 1)
                for kind, g in mla_step_turns(s):
                    no = mla_turn_no[kind, g]
                    if no >= 2:
                        pe.wait_ge(ma_pt, no - 1)
                    if kind == "item":
                        b = g % NT
                        pe.wait_ge(ma_e, g + 1)
                        for c in range(b + 1):
                            turn(PS[:, 4 + no % 2, P * c:P * (c + 1)], ME[:, g % 3, META + P * c:META + P * (c + 1)], P)
                        if b < NT - 1:
                            o = PS[0:META, 4 + no % 2, P * (b + 1):P * (b + 2)]
                        else:
                            if g >= NT:
                                pe.wait_ge(ma_pt, mla_turn_no["item", g - NT] + 1)
                            o = PS[0:META, 7, 0:P]
                        last = turn(o, ME[:, g % 3, 0:META], P)
                    else:
                        pe.wait_ge(ma_on, 2 * g + 2)
                        for c in range(NT):
                            last = turn(PS[:, 4 + no % 2, P * c:P * (c + 1)], MON[:, g % 2, c, :], P)
                    last.then_inc(ma_t, 1)
                if 3 <= s <= HEADS * NT + 2:
                    g = s - 3
                    h, b = g // NT, g % NT
                    pe.wait_ge(ma_pt, mla_turn_no["item", g] + 1)
                    if b == 0 and h:
                        pe.wait_ge(ma_on, h)
                    o = PS[:, 6, 64 * b:64 * (b + 1)]
                    hv = slice(64 * h, 64 * h + 64)
                    for c in range(b + 1):
                        mm(o, MPT[:, g % 2, P * c:P * (c + 1)], MV[:, 1 + c, hv], start=c == 0, stop=False)
                    mm(o, MPT[0:META, g % 2, P * (b + 1):P * (b + 2)], MV[0:META, 0, hv],
                       start=False, stop=True).then_inc(ma_pv, 1)
            pe.wait_ge(ma_pt, len(mla_turns))
            pe.wait_ge(ma_on, HEADS)
            pe.wait_ge(ma_e, HEADS * NT)
            project(j_gqkv, UH, UL, ALL_COLS)
            slot = at_gss[1] % SLOTS
            slot_free(pe, slot, at_gss[1] // SLOTS)
            pe.wait_ge(s_sel, 3)
            for n in range(8):
                pe.wait_ge(gsq_done, n + 1)
                for t in range(0 if n >= 4 else 1, NT + 1):
                    w, cols = tile(t)
                    last = mm(PS[0:w, 2 * slot, 16 * t + 2 * n:16 * t + 2 * n + 2], SG[:, n % 2, cols], SEL[:, 0:2])
                last.then_inc(ss_mm, 1)
            project(j_z, UH, UL, SEQ_COLS)
            for s, n in enumerate(uses_before(j_z.end[1])):
                pe.wait_ge(ps_free[s], n)
            pe.wait_ge(s_al, 32)
            mm(PS[:, 1, 0:16], ONES[0:1, :], ALROW[0:1, :])
            for t in range(NT + 1):
                w, cols = tile(t)
                last = nc.tensor.transpose(PS[0:w, 0, 16 * t:16 * t + 16], MISC[64:80, cols], IDENT[64:80, 64:80])
            last.then_inc(g_pe, 1)
            pe.wait_ge(g_dve, N_PRE_DVE)
            pe.wait_ge(s_tri, 16)
            mm(PS[:, 2, 0:32], TRI[:, 0, :], GG[:, 1:NT + 1, :])
            mm(PS[:, 2, 32:64], TRI[:, 1, :], GG[:, 1:NT + 1, :])
            for c in range(2):
                r = slice(64 * c, 64 * c + 64)
                for par in range(2):
                    mm(PS[64 * par:64 * par + 64, 2 + c, 64 + 16 * c:80 + 16 * c], ONES[r, 0:64],
                       GG[r, 1:NT + 1, :].rearrange("p t (h a) -> p t h a", a=2)[:, :, :, par])
            mm(PS[0:META, 2, 96:104], TRI[0:META, 0, 0:META], GG[0:META, 0, :])
            mm(PS[0:META, 2, 104:112], TRI[0:META, 1, 0:META], GG[0:META, 0, :]).then_inc(g_pe, 1)
            pe.wait_ge(gexp_done, 1)

            def turn_in(t):
                w, cols = tile(t)
                if t:
                    pe.wait_ge(g_dve, DVE_AT[t - 1, ("s", 0 if t == 1 else 1)])
                if t > 1:
                    pe.wait_ge(g_dve, DVE_AT[t - 1, "out_join"])
                for part in range(0 if t else 1, 3):
                    for c in range(4):
                        last = turn(PS[0:w, part, P * c:P * (c + 1)], CVS[:, 4 * part + c, cols], P)
                last.then_inc(g_pe, one("pe", t, "turn_in"))

            turn_in(0)
            for t in range(NT + 1):
                w, cols = tile(t)
                pe.wait_ge(g_pool, POOL_AT[t, "ug"])
                pe.wait_ge(g_act, ACT_AT[t, "rows"])
                for b in range(2):
                    last = mm(PS[0:w, b, 0:4 * w], TRI[0:w, 1, 0:w], UG[0:w, 4 * b:4 * b + 4, 0:w])
                last.then_inc(g_pe, one("pe", t, "decay"))
                for name, ready, pair in (("turn_k", "nk", ((3, NK), (5, KB))), ("turn_q", "qg", ((4, NQ), (6, QG)))):
                    if t or name == "turn_k":
                        pe.wait_ge(g_dve, DVE_AT[t, ready])
                        for bank, src in pair:
                            for c in range(4):
                                last = turn(PS[:, bank, w * c:w * (c + 1)], src[0:w, P * c:P * (c + 1)], w)
                        last.then_inc(g_pe, one("pe", t, name))
                pe.wait_ge(g_act, ACT_AT[t, "turned_k"])
                if t > 1:
                    pe.wait_ge(g_dve, DVE_AT[t - 1, "out_gate"])

                def scores(banks, x):
                    for h in range(HEADS):
                        r = slice(64 * (h % 2), 64 * (h % 2) + 64)
                        last = mm(PS[0:w, banks[h % 2], w * (h // 2):w * (h // 2 + 1)], KT[r, h // 2, 0:w], x[r, h // 2, 0:w])
                    return last
                scores((2, 7), KBT).then_inc(g_pe, one("pe", t, "kk"))
                if t:
                    pe.wait_ge(g_dve, DVE_AT[t, "turned_q"])
                    scores((3, 4), QT).then_inc(g_pe, one("pe", t, "kq"))
                pe.wait_ge(g_act, ACT_AT[t, "decay"])
                pe.wait_ge(g_dve, DVE_AT[t, "e1b"])
                for h in range(HEADS):
                    last = turn(PS[0:w, h // 4, w * (h % 4):w * (h % 4 + 1)], TIT[0:w, h, 0:w], w)
                last.then_inc(g_pe, one("pe", t, "d1"))
                for n, s in enumerate(levels(t)):
                    for g in range(2):
                        if n:
                            pe.wait_ge(g_dve, DVE_AT[t, ("d", levels(t)[n - 1], g)])
                        else:
                            pe.wait_ge(g_act, ACT_AT[t, "d1"])
                            pe.wait_ge(g_dve, DVE_AT[t, "at" if t else "e1b"])
                        for h in range(4 * g, 4 * g + 4):
                            last = mm(PS[0:w, g, w * (h % 4):w * (h % 4 + 1)], LT[0:w, h, 0:w], TI[0:w, h, 0:w])
                        last.then_inc(g_pe, one("pe", t, ("x", s, g)))
                    for g in range(2):
                        pe.wait_ge(g_dve, DVE_AT[t, ("x", s, g)])
                        if n:
                            pe.wait_ge(g_dve, DVE_AT[t, ("e", levels(t)[n - 1], g)])
                        for h in range(4 * g, 4 * g + 4):
                            o = slice(w // 2 * (h % 4), w // 2 * (h % 4 + 1))
                            if s != levels(t)[-1]:
                                mm(PS[0:w, (2, 7)[g], o], TIT[0:w, h, 0:w], joined(XX[0:w, h, 0:w], s, 0))
                            last = mm(PS[0:w, 3 + g, o], XX[0:w, h, 0:w], joined(TIT[0:w, h, 0:w], s, 1))
                        last.then_inc(g_pe, one("pe", t, ("y", s, g)))
                pe.wait_ge(g_dve, DVE_AT[t, ("e", levels(t)[-1], 1)])
                for h in range(HEADS):
                    hv = slice(64 * h, 64 * h + 64)
                    last = mm(PS[0:w, 5, hv], TIT[0:w, h, 0:w], ROWQ[0:w, 2, hv])
                    if t:
                        last = mm(PS[64 * (h % 2):64 * (h % 2) + 64, 6, P * (h // 2):P * (h // 2 + 1)], KBG[:, hv], TIT[:, h, :])
                last.then_inc(g_pe, one("pe", t, "uw"))
                for c in range(2 if t else 1):
                    r = slice(64 * c, 64 * c + 64) if t else slice(0, META)
                    old = (2 * (t - 1) + c) % 2
                    pe.wait_ge(g_act, ACT_AT[t, "uw"])
                    if t:
                        pe.wait_ge(g_dve, DVE_AT[t if c else t - 1, ("s", 0 if c or t == 1 else 1)])
                        for h in range(HEADS):
                            d = slice(64 * (h % 2), 64 * (h % 2) + 64)
                            last = mm(PS[r, 3 * (h % 2), GDN_D * (h // 2):GDN_D * (h // 2 + 1)], WTT[d, h // 2, r], ST[d, old, h // 2, :])
                        last.then_inc(g_pe, one("pe", t, ("ws", c)))
                        pe.wait_ge(g_dve, DVE_AT[t, ("vn", c)])
                    x = VN if t else UU
                    for h in range(HEADS):
                        hv = slice(64 * h, 64 * h + 64)
                        last = mm(PS[64 * (h % 2):64 * (h % 2) + 64, 1, GDN_D * (h // 2):GDN_D * (h // 2 + 1)],
                                  KD[r, hv], x[r, hv])
                    last.then_inc(g_pe, one("pe", t, ("state", c)))
                    if t:
                        pe.wait_ge(g_pool, POOL_AT[t, "at"])
                        for h in range(HEADS):
                            d = slice(64 * (h % 2), 64 * (h % 2) + 64)
                            hv = slice(64 * h, 64 * h + 64)
                            mm(PS[r, 4 + h % 2, GDN_D * (h // 2):GDN_D * (h // 2 + 1)], QGT[d, h // 2, r], ST[d, old, h // 2, :])
                            last = mm(PS[r, 2, hv], AT[r, h, r], VN[r, hv])
                        last.then_inc(g_pe, one("pe", t, ("out", c)))
                if t < NT:
                    turn_in(t + 1)
                if t:
                    pe.wait_ge(g_dve, DVE_AT[t, "out_norm"])
                    for c in range(4):
                        last = turn(PS[:, 7, P * c:P * (c + 1)], GON[:, P * c:P * (c + 1)], P)
                    last.then_inc(g_pe, one("pe", t, "turn_out"))
            pe.wait_ge(g_dve, DVE_AT[NT, "out_gate"])
            for n in range(4):
                for q in range(3):
                    u = j_merge.unit0 + 3 * n + q
                    b = u % SPLITS
                    pe.wait_ge(lo_done, u + 1)
                    if q == 2 and n == 0:
                        pe.wait_ge(ol_done, 4)
                        pe.wait_ge(gl_done, 4)
                    if q < 2:
                        todo = [(range(KC), m, UH, UL, SEQ_COLS) for m in range(2)]
                    else:
                        todo = [(range(4 * br, 4 * br + 4), m, (OMH, GOH)[br], (OML, GOL)[br], PLAIN)
                                for m in range(2) for br in range(2)]
                    for i, (ks, m, xh, xl, cols) in enumerate(todo):
                        c = j_merge.chunk0 + 8 * n + 2 * q + i
                        slot = c % SLOTS
                        slot_free(pe, slot, c // SLOTS)
                        for k in ks:
                            w = slice(k * UCOL + m * P, k * UCOL + (m + 1) * P)
                            x = k - ks[0]
                            last = three(acc(slot, SEQ), WH[:, b, w], WL[:, b, w], xh[:, x, cols], xl[:, x, cols],
                                         k == ks[0], k == ks[-1])
                        last.then_inc(done, 1)
            project(j_wout, MH, ML, PLAIN, k_ready=(ml_done, 0))
            norm_products("ffn2")
            ffn_pe("ffn2", 1)
            norm_products("final")
            pe.wait_ge(f_done, KC)
            for t in range(NT):
                c = at_rows[1] + t
                slot_free(pe, c % SLOTS, c // SLOTS)
                for k in range(KC):
                    last = turn(PS[:, 2 * (c % SLOTS) + k // 4, P * (k % 4):P * (k % 4 + 1)], FN[:, k, P * t:P * (t + 1)], P)
                last.then_inc(done, 1)


INPUTS = [
    "x", "pre_norm", "post_norm", "w_in_a", "w_out_a", "kv_norm", "w_kv", "w_in_b", "lam_q1", "lam_k1", "lam_q2",
    "lam_k2", "sub_norm_b", "w_out_b", "meta_tokens_2", "ffn1_norm_2", "ffn1_w_gate_2", "ffn1_w_up_2",
    "ffn1_w_down_2", "mix_norm_2", "w_in_2", "q_norm_2", "w_uq_2", "kv_norm_2", "w_ukv_2", "w_mla_o_2",
    "conv_w_2", "a_log_2", "dt_bias_2", "gdn_norm_2", "w_gdn_o_2", "w_out_2", "ffn2_norm_2", "ffn2_w_gate_2",
    "ffn2_w_up_2", "ffn2_w_down_2", "final_norm_2",
]

GAIN_ROWS = [("pre_norm", 0), ("post_norm", 0), ("kv_norm", None), ("pre_norm", 1), ("post_norm", 1),
             ("ffn1_norm_2", 0), ("mix_norm_2", 0), ("ffn2_norm_2", 0), ("final_norm_2", None)]

SUB_ROW, GDN_ROW, QN_ROW, KVN_ROW, CONV_ROW = 72, 73, 74, 76, 77
N_ROWS = 125


def other_rows(A):
    return [(SUB_ROW, A["sub_norm_b"]), (GDN_ROW, A["gdn_norm_2"]),
            (QN_ROW, A["q_norm_2"].rearrange("a (c p) -> (a c) p", p=P)), (KVN_ROW, A["kv_norm_2"]),
            (CONV_ROW, A["conv_w_2"][0].rearrange("t (c p) -> (t c) p", p=P))]


def kernel(**inputs):
    from concourse import bacc
    from concourse.bass_utils import run_bass_kernel_spmd

    nc = bacc.Bacc("TRN2", target_bir_lowering=False, num_devices=1)
    arrays, A = {}, {}
    for name in INPUTS:
        a = np.ascontiguousarray(inputs[name])
        arrays[f"in_{name}"] = a
        A[name] = nc.dram_tensor(f"in_{name}", a.shape, mybir.dt.from_np(a.dtype), kind="ExternalInput").ap()
    out = nc.dram_tensor("out", (1, SEQ, D), F32, kind="ExternalOutput").ap()
    build(nc, A, out)
    r = run_bass_kernel_spmd(nc, [arrays], core_ids=[0])
    return r.results[0]["out"]
```
